# Optimizing a Trainium2 kernel written in Bass

```python
import math
import jax, jax.numpy as jnp
from jax import lax
import numpy as np

D_MODEL = 1024
BATCH = 1
SEQ = 256
DEPTH = 1

D_MIX = D_MODEL
SB_HEADS = 8
SB_HEAD_DIM = 64
SB_WIDTH = SB_HEADS * SB_HEAD_DIM
RW_HEADS = 8
RW_HEAD_DIM = 64
RW_WIDTH = RW_HEADS * RW_HEAD_DIM
LORA_W = 64
LORA_A = 64
LORA_G = 128
RW_IN = 3 * RW_WIDTH + LORA_W + LORA_A + LORA_G
SB_IN = 3 * SB_WIDTH
N_IN = SB_IN + RW_IN
Q_BLOCK = 128
N_GROUPS = 4
EXPERTS_PER_GROUP = 8
N_EXPERTS = N_GROUPS * EXPERTS_PER_GROUP
TOP_K_IN_GROUP = 2
D_EXPERT = 256
RMS_EPS = 1e-6
GN_EPS = 64e-5


def rmsnorm(x, g):
    xf = x.astype(jnp.float32)
    y = xf * lax.rsqrt(jnp.mean(xf * xf, axis=-1, keepdims=True) + RMS_EPS)
    return (y * g.astype(jnp.float32)).astype(x.dtype)

def token_shift(u):
    return jnp.pad(u, ((0, 0), (1, 0), (0, 0)))[:, :-1]

def stick_breaking_attention(q, k, v):
    B, H, S, dh = q.shape
    scale = 1.0 / math.sqrt(dh)
    outs = []
    for blk in range(S // Q_BLOCK):
        t0 = blk * Q_BLOCK
        kv_len = t0 + Q_BLOCK
        qb = q[:, :, t0:kv_len].astype(jnp.float32)
        kb = k[:, :, :kv_len].astype(jnp.float32)
        vb = v[:, :, :kv_len].astype(jnp.float32)
        z = jnp.einsum('bhqd,bhkd->bhqk', qb, kb) * scale
        t_pos = t0 + jnp.arange(Q_BLOCK)[:, None]
        s_pos = jnp.arange(kv_len)[None, :]
        strict = s_pos < t_pos
        log_rest = jnp.where(strict, jax.nn.log_sigmoid(-z), 0.0)
        suffix = lax.cumsum(log_rest, axis=3, reverse=True) - log_rest
        weights = jnp.where(strict, jnp.exp(jax.nn.log_sigmoid(z) + suffix), 0.0)
        outs.append(jnp.einsum('bhqk,bhkd->bhqd', weights, vb))
    return jnp.concatenate(outs, axis=2)

def rwkv7_scan(r, w, k, v, kk, a):
    B, S, H, N = r.shape
    xs = tuple(jnp.moveaxis(t, 1, 0) for t in (r, w, k, v, kk, a))

    def step(state, inp):
        r_t, w_t, k_t, v_t, kk_t, a_t = inp
        sa = jnp.einsum('bhij,bhj->bhi', state, -kk_t)
        state = (state * w_t[:, :, None, :]
                 + sa[..., None] * (kk_t * a_t)[:, :, None, :]
                 + v_t[..., None] * k_t[:, :, None, :])
        out = jnp.einsum('bhij,bhj->bhi', state, r_t)
        return state, out

    state0 = jnp.zeros((B, H, N, N), jnp.float32)
    _, outs = lax.scan(step, state0, xs)
    return jnp.moveaxis(outs, 0, 1)

def rwkv7_group(u_rw, shift_mu, w0, w2, a0, a2, g2, k_k, k_a, r_k, ln_w, ln_b):
    B, S, _ = u_rw.shape
    uf = u_rw.astype(jnp.float32)
    um = uf + (token_shift(uf) - uf) * shift_mu.astype(jnp.float32)
    o = 0
    r = um[..., o:o + RW_WIDTH]; o += RW_WIDTH
    k = um[..., o:o + RW_WIDTH]; o += RW_WIDTH
    v = um[..., o:o + RW_WIDTH]; o += RW_WIDTH
    xw = um[..., o:o + LORA_W]; o += LORA_W
    xa = um[..., o:o + LORA_A]; o += LORA_A
    xg = um[..., o:o + LORA_G]
    w_log = -jax.nn.softplus(-(w0 + jnp.tanh(xw) @ w2)) - 0.5
    decay = jnp.exp(-jnp.exp(w_log))
    a = jax.nn.sigmoid(a0 + xa @ a2)
    g = jax.nn.sigmoid(xg) @ g2
    hs = lambda t: t.reshape(B, S, RW_HEADS, RW_HEAD_DIM)
    kk = hs(k * k_k)
    kk = kk * lax.rsqrt(jnp.maximum(jnp.sum(kk * kk, axis=-1, keepdims=True), 1e-24))
    k = k * (1.0 + (a - 1.0) * k_a)
    r_h, k_h, v_h, w_h, a_h = hs(r), hs(k), hs(v), hs(decay), hs(a)
    out = rwkv7_scan(r_h, w_h, k_h, v_h, kk, a_h)
    mean = jnp.mean(out, axis=-1, keepdims=True)
    var = jnp.mean(jnp.square(out - mean), axis=-1, keepdims=True)
    out = ((out - mean) * lax.rsqrt(var + GN_EPS)).reshape(B, S, RW_WIDTH) * ln_w + ln_b
    bonus = jnp.sum(r_h * k_h * r_k, axis=-1, keepdims=True) * v_h
    out = (out + bonus.reshape(B, S, RW_WIDTH)) * g
    return out.astype(u_rw.dtype)

def sb_group(u_sb, sb_out_g):
    B, S, _ = u_sb.shape
    heads = lambda t: t.reshape(B, S, SB_HEADS, SB_HEAD_DIM).transpose(0, 2, 1, 3)
    q = heads(u_sb[..., :SB_WIDTH])
    k = heads(u_sb[..., SB_WIDTH:2 * SB_WIDTH])
    v = heads(u_sb[..., 2 * SB_WIDTH:])
    o = stick_breaking_attention(q, k, v).transpose(0, 2, 1, 3)
    o = o * lax.rsqrt(jnp.mean(o * o, axis=-1, keepdims=True) + RMS_EPS)
    return (o.reshape(B, S, SB_WIDTH) * sb_out_g).astype(u_sb.dtype)

def hier_moe(x2d, w_grp, b_grp, w_exp, b_exp, w_gate, w_up, w_down):
    T = x2d.shape[0]
    xf = x2d.astype(jnp.float32)
    grp_prob = jax.nn.softmax(xf @ w_grp.astype(jnp.float32) + b_grp.astype(jnp.float32), axis=-1)
    g_val, g_idx = lax.top_k(grp_prob, 1)
    exp_logits = (xf @ w_exp.astype(jnp.float32) + b_exp.astype(jnp.float32)).reshape(T, N_GROUPS, EXPERTS_PER_GROUP)
    sel = jnp.take_along_axis(exp_logits, g_idx[:, :, None], axis=1)[:, 0]
    e_val, e_idx = lax.top_k(jax.nn.softmax(sel, axis=-1), TOP_K_IN_GROUP)
    weights = g_val * e_val / jnp.sum(e_val, axis=-1, keepdims=True)
    global_idx = g_idx * EXPERTS_PER_GROUP + e_idx
    combine = jnp.sum(jax.nn.one_hot(global_idx, N_EXPERTS, dtype=jnp.float32) * weights[..., None], axis=1)
    combine = combine.astype(x2d.dtype)
    y = jnp.zeros_like(x2d)
    for e in range(N_EXPERTS):
        h = jax.nn.silu(x2d @ w_gate[e]) * (x2d @ w_up[e])
        y = y + combine[:, e:e + 1] * (h @ w_down[e])
    return y

def first_inputs(seed: int = 0) -> dict:
    key = jax.random.key(seed)
    ks = jax.random.split(key, 28)
    f32 = jnp.float32
    nrm = lambda k, shape, s: jax.random.normal(k, shape, f32) * s
    L = DEPTH
    return {
        "x": jax.random.normal(ks[0], (BATCH, SEQ, D_MODEL), f32),
        "norm_mix_g": 1.0 + nrm(ks[1], (L, D_MODEL), 0.02),
        "w_in": nrm(ks[2], (L, D_MODEL, N_IN), D_MODEL ** -0.5),
        "shift_mu": jax.random.uniform(ks[3], (L, RW_IN), f32, 0.1, 0.9),
        "sb_out_g": 1.0 + nrm(ks[4], (L, SB_WIDTH), 0.02),
        "rw_w0": jax.random.uniform(ks[5], (L, RW_WIDTH), f32, -6.5, -1.5),
        "rw_w2": nrm(ks[6], (L, LORA_W, RW_WIDTH), 0.5 * LORA_W ** -0.5),
        "rw_a0": nrm(ks[7], (L, RW_WIDTH), 0.1),
        "rw_a2": nrm(ks[8], (L, LORA_A, RW_WIDTH), LORA_A ** -0.5),
        "rw_g2": nrm(ks[9], (L, LORA_G, RW_WIDTH), LORA_G ** -0.5),
        "rw_k_k": 0.85 + nrm(ks[10], (L, RW_WIDTH), 0.02),
        "rw_k_a": 1.0 + nrm(ks[11], (L, RW_WIDTH), 0.02),
        "rw_r_k": nrm(ks[12], (L, RW_HEADS, RW_HEAD_DIM), 0.1),
        "rw_ln_w": 1.0 + nrm(ks[13], (L, RW_WIDTH), 0.02),
        "rw_ln_b": nrm(ks[14], (L, RW_WIDTH), 0.02),
        "w_out": nrm(ks[15], (L, D_MIX, D_MODEL), D_MIX ** -0.5),
        "norm_ffn_g": 1.0 + nrm(ks[16], (L, D_MODEL), 0.02),
        "router_grp_w": nrm(ks[17], (L, D_MODEL, N_GROUPS), D_MODEL ** -0.5),
        "router_grp_b": nrm(ks[18], (L, N_GROUPS), 0.01),
        "router_exp_w": nrm(ks[19], (L, D_MODEL, N_EXPERTS), D_MODEL ** -0.5),
        "router_exp_b": nrm(ks[20], (L, N_EXPERTS), 0.01),
        "exp_w_gate": nrm(ks[21], (L, N_EXPERTS, D_MODEL, D_EXPERT), D_MODEL ** -0.5),
        "exp_w_up": nrm(ks[22], (L, N_EXPERTS, D_MODEL, D_EXPERT), D_MODEL ** -0.5),
        "exp_w_down": nrm(ks[23], (L, N_EXPERTS, D_EXPERT, D_MODEL), D_EXPERT ** -0.5),
        "final_norm_g": 1.0 + nrm(ks[24], (D_MODEL,), 0.02),
    }

def first_block(x, norm_mix_g, w_in, shift_mu, sb_out_g, rw_w0, rw_w2, rw_a0, rw_a2, rw_g2,
              rw_k_k, rw_k_a, rw_r_k, rw_ln_w, rw_ln_b, w_out, norm_ffn_g,
              router_grp_w, router_grp_b, router_exp_w, router_exp_b,
              exp_w_gate, exp_w_up, exp_w_down, final_norm_g):
    B, S, D = x.shape
    h = x
    for l in range(DEPTH):
        u = rmsnorm(h, norm_mix_g[l]) @ w_in[l]
        o_sb = sb_group(u[..., :SB_IN], sb_out_g[l])
        o_rw = rwkv7_group(u[..., SB_IN:], shift_mu[l], rw_w0[l], rw_w2[l], rw_a0[l], rw_a2[l],
                           rw_g2[l], rw_k_k[l], rw_k_a[l], rw_r_k[l], rw_ln_w[l], rw_ln_b[l])
        h = h + jnp.concatenate([o_sb, o_rw], axis=-1) @ w_out[l]
        xn = rmsnorm(h, norm_ffn_g[l]).reshape(B * S, D)
        y = hier_moe(xn, router_grp_w[l], router_grp_b[l], router_exp_w[l], router_exp_b[l],
                     exp_w_gate[l], exp_w_up[l], exp_w_down[l])
        h = h + y.reshape(B, S, D)
    return rmsnorm(h, final_norm_g)


DEPTH_2 = 2

D_FF = 2816

SSD_WIDTH = D_MODEL
SSD_HEADDIM = 64
SSD_HEADS = SSD_WIDTH // SSD_HEADDIM
SSD_GROUPS = 2
SSD_HPG = SSD_HEADS // SSD_GROUPS
SSD_STATE = 128
SSD_CONV = 5
SSD_CHUNK = 128
SSD_XBC = SSD_WIDTH + 2 * SSD_GROUPS * SSD_STATE

MLA_HEADS = 8
MLA_Q_LORA = D_MODEL // 4
MLA_KV_LORA = D_MODEL // 8
MLA_NOPE = 64
MLA_ROPE = 32
MLA_QK = MLA_NOPE + MLA_ROPE
MLA_V = 64
MLA_WIDTH = MLA_HEADS * MLA_V
ROPE_BASE = 10000.0
ATTN_BLOCK = 128

CONV_WIDTH = D_MODEL // 2
CONV_GROUPS = 8
CONV_K = 3

D_MIX_2 = SSD_WIDTH + MLA_WIDTH + CONV_WIDTH
IN_SIZES = (SSD_WIDTH, SSD_XBC, 2 * SSD_HEADS, MLA_Q_LORA, MLA_KV_LORA, MLA_ROPE, CONV_WIDTH, CONV_WIDTH, CONV_WIDTH)
D_IN = SSD_WIDTH + SSD_XBC + 2 * SSD_HEADS + MLA_Q_LORA + MLA_KV_LORA + MLA_ROPE + 3 * CONV_WIDTH


def rms_norm(x, g):
    xf = x.astype(jnp.float32)
    y = xf * lax.rsqrt(jnp.mean(xf * xf, axis=-1, keepdims=True) + RMS_EPS)
    return (y * g.astype(jnp.float32)).astype(x.dtype)

def group_rms_norm(x, g, n_groups):
    shp = x.shape
    xg = x.reshape(shp[:-1] + (n_groups, shp[-1] // n_groups))
    return rms_norm(xg, g.reshape(n_groups, -1)).reshape(shp)

def swiglu(x, w_gate, w_up, w_down):
    return (jax.nn.silu(x @ w_gate) * (x @ w_up)) @ w_down

def depthwise_conv(x, w):
    k, c = w.shape
    return lax.conv_general_dilated(x, w[:, None, :].astype(x.dtype), window_strides=(1,),
                                    padding=[(k // 2, k // 2)],
                                    dimension_numbers=('NWC', 'WIO', 'NWC'),
                                    feature_group_count=c)

def rope(x, pos):
    half = x.shape[-1] // 2
    inv = ROPE_BASE ** (-jnp.arange(half, dtype=jnp.float32) / half)
    ang = pos.astype(jnp.float32)[..., None] * inv
    cos = jnp.cos(ang)[:, :, None, :]
    sin = jnp.sin(ang)[:, :, None, :]
    xf = x.astype(jnp.float32)
    x1, x2 = xf[..., :half], xf[..., half:]
    return jnp.concatenate([x1 * cos - x2 * sin, x1 * sin + x2 * cos], axis=-1).astype(x.dtype)

def split_points(sizes):
    pts, acc = [], 0
    for n in sizes[:-1]:
        acc += n
        pts.append(acc)
    return pts

def ssd_chunked(x, dt, a, bm, cm):
    bsz, s = x.shape[0], x.shape[1]
    nc, L = s // SSD_CHUNK, SSD_CHUNK
    xc = x.reshape(bsz, nc, L, SSD_GROUPS, SSD_HPG, SSD_HEADDIM)
    dtc = dt.reshape(bsz, nc, L, SSD_GROUPS, SSD_HPG)
    bc = bm.reshape(bsz, nc, L, SSD_GROUPS, SSD_STATE)
    cc = cm.reshape(bsz, nc, L, SSD_GROUPS, SSD_STATE)
    xd = xc * dtc[..., None]
    a_cs = jnp.cumsum(dtc * a, axis=2)
    seg = a_cs[:, :, :, None] - a_cs[:, :, None, :]
    lower = jnp.tril(jnp.ones((L, L), dtype=bool))[None, None, :, :, None, None]
    decay = jnp.exp(jnp.where(lower, seg, -jnp.inf))
    cb = jnp.einsum('bclgn,bcsgn->bclsg', cc, bc)
    y_diag = jnp.einsum('bclsg,bclsgr,bcsgrp->bclgrp', cb, decay, xd)
    decay_states = jnp.exp(a_cs[:, :, -1:] - a_cs)
    states = jnp.einsum('bclgn,bclgr,bclgrp->bcgrpn', bc, decay_states, xd)
    chunk_decay = jnp.exp(a_cs[:, :, -1])

    def step(carry, inp):
        st, dec = inp
        return carry * dec[..., None, None] + st, carry

    init = jnp.zeros_like(states[:, 0])
    _, prev = lax.scan(step, init, (jnp.moveaxis(states, 1, 0), jnp.moveaxis(chunk_decay, 1, 0)))
    prev = jnp.moveaxis(prev, 0, 1)
    y_off = jnp.einsum('bclgn,bcgrpn,bclgr->bclgrp', cc, prev, jnp.exp(a_cs))
    return (y_diag + y_off).reshape(bsz, s, SSD_GROUPS, SSD_HPG, SSD_HEADDIM)

def ssd_mixer(z, xbc, dt_raw, conv_w, conv_b, dt_bias, a_log, d_skip, norm_g):
    bsz, s = z.shape[0], z.shape[1]
    xbc = jax.nn.silu(depthwise_conv(xbc, conv_w) + conv_b)
    xs = xbc[..., :SSD_WIDTH].reshape(bsz, s, SSD_GROUPS, SSD_HPG, SSD_HEADDIM).astype(jnp.float32)
    bm = xbc[..., SSD_WIDTH:SSD_WIDTH + SSD_GROUPS * SSD_STATE].reshape(bsz, s, SSD_GROUPS, SSD_STATE).astype(jnp.float32)
    cm = xbc[..., SSD_WIDTH + SSD_GROUPS * SSD_STATE:].reshape(bsz, s, SSD_GROUPS, SSD_STATE).astype(jnp.float32)
    dt = jax.nn.softplus(dt_raw.astype(jnp.float32).reshape(bsz, s, 2, SSD_GROUPS, SSD_HPG)
                         + dt_bias.astype(jnp.float32).reshape(2, SSD_GROUPS, SSD_HPG))
    a = -jnp.exp(a_log.astype(jnp.float32)).reshape(2, SSD_GROUPS, SSD_HPG)
    y_fwd = ssd_chunked(xs, dt[:, :, 0], a[0], bm, cm)
    y_bwd = jnp.flip(ssd_chunked(jnp.flip(xs, 1), jnp.flip(dt[:, :, 1], 1), a[1],
                                 jnp.flip(bm, 1), jnp.flip(cm, 1)), 1)
    y = y_fwd + y_bwd + xs * d_skip.astype(jnp.float32).reshape(SSD_GROUPS, SSD_HPG)[..., None]
    y = y.reshape(bsz, s, SSD_WIDTH) * jax.nn.silu(z.astype(jnp.float32))
    return group_rms_norm(y, norm_g, SSD_GROUPS).astype(z.dtype)

def mla_mixer(q_lat, kv_lat, k_pe, positions, q_norm, w_uq, kv_norm, w_ukv,
              q_head_norm, k_head_norm, out_norm):
    bsz, s = q_lat.shape[0], q_lat.shape[1]
    q = (rms_norm(q_lat, q_norm) @ w_uq).reshape(bsz, s, MLA_HEADS, MLA_QK)
    kv = (rms_norm(kv_lat, kv_norm) @ w_ukv).reshape(bsz, s, MLA_HEADS, MLA_NOPE + MLA_V)
    k_nope, v = kv[..., :MLA_NOPE], kv[..., MLA_NOPE:]
    k = jnp.concatenate([k_nope, jnp.broadcast_to(k_pe[:, :, None, :], (bsz, s, MLA_HEADS, MLA_ROPE))], axis=-1)
    q = rms_norm(q, q_head_norm)
    k = rms_norm(k, k_head_norm)
    q = jnp.concatenate([q[..., :MLA_NOPE], rope(q[..., MLA_NOPE:], positions)], axis=-1)
    k = jnp.concatenate([k[..., :MLA_NOPE], rope(k[..., MLA_NOPE:], positions)], axis=-1)
    scale = MLA_QK ** -0.5
    nb = s // ATTN_BLOCK
    q_blocks = q.reshape(bsz, nb, ATTN_BLOCK, MLA_HEADS, MLA_QK).swapaxes(0, 1)

    def attend(qb):
        sc = jnp.einsum('bqhd,bkhd->bhqk', qb, k).astype(jnp.float32) * scale
        p = jax.nn.softmax(sc, axis=-1).astype(v.dtype)
        return jnp.einsum('bhqk,bkhd->bqhd', p, v)

    o = lax.map(attend, q_blocks).swapaxes(0, 1).reshape(bsz, s, MLA_HEADS, MLA_V)
    return rms_norm(o, out_norm.reshape(MLA_HEADS, MLA_V)).reshape(bsz, s, MLA_WIDTH)

def conv_mixer(h_in, b_gate, c_gate, conv_w, out_norm):
    y = b_gate * depthwise_conv(c_gate * h_in, conv_w)
    return group_rms_norm(y, out_norm, CONV_GROUPS)

def second_inputs(seed: int = 0) -> dict:
    key = jax.random.key(seed)
    k = jax.random.split(key, 32)
    f32 = jnp.float32

    def w(i, shape, fan_in):
        return jax.random.normal(k[i], shape, f32) * (fan_in ** -0.5)

    def gain(i, shape):
        return 1.0 + 0.05 * jax.random.normal(k[i], shape, f32)

    u = jax.random.uniform(k[9], (DEPTH_2, 2, SSD_HEADS), f32)
    dt0 = jnp.exp(u * (math.log(0.1) - math.log(1e-3)) + math.log(1e-3))
    ssd_dt_bias = dt0 + jnp.log(-jnp.expm1(-dt0))
    ssd_a_log = jnp.log(jax.random.uniform(k[10], (DEPTH_2, 2, SSD_HEADS), f32, 1.0, 16.0))
    positions = jnp.broadcast_to(jnp.arange(SEQ, dtype=jnp.int32)[None, :], (BATCH, SEQ))
    return {
        'x': jax.random.normal(k[0], (BATCH, SEQ, D_MODEL), f32),
        'positions': positions,
        'ffn1_norm': gain(1, (DEPTH_2, D_MODEL)),
        'ffn1_w_gate': w(2, (DEPTH_2, D_MODEL, D_FF), D_MODEL),
        'ffn1_w_up': w(3, (DEPTH_2, D_MODEL, D_FF), D_MODEL),
        'ffn1_w_down': w(4, (DEPTH_2, D_FF, D_MODEL), D_FF),
        'mix_norm': gain(5, (DEPTH_2, D_MODEL)),
        'w_in': w(6, (DEPTH_2, D_MODEL, D_IN), D_MODEL),
        'ssd_conv_w': w(7, (DEPTH_2, SSD_CONV, SSD_XBC), SSD_CONV),
        'ssd_conv_b': 0.02 * jax.random.normal(k[8], (DEPTH_2, SSD_XBC), f32),
        'ssd_dt_bias': ssd_dt_bias,
        'ssd_a_log': ssd_a_log,
        'ssd_d': 1.0 + 0.1 * jax.random.normal(k[11], (DEPTH_2, SSD_HEADS), f32),
        'ssd_norm': gain(12, (DEPTH_2, SSD_WIDTH)),
        'mla_q_norm': gain(13, (DEPTH_2, MLA_Q_LORA)),
        'mla_w_uq': w(14, (DEPTH_2, MLA_Q_LORA, MLA_HEADS * MLA_QK), MLA_Q_LORA),
        'mla_kv_norm': gain(15, (DEPTH_2, MLA_KV_LORA)),
        'mla_w_ukv': w(16, (DEPTH_2, MLA_KV_LORA, MLA_HEADS * (MLA_NOPE + MLA_V)), MLA_KV_LORA),
        'mla_q_head_norm': gain(17, (DEPTH_2, MLA_QK)),
        'mla_k_head_norm': gain(18, (DEPTH_2, MLA_QK)),
        'mla_out_norm': gain(19, (DEPTH_2, MLA_WIDTH)),
        'conv_w': w(20, (DEPTH_2, CONV_K, CONV_WIDTH), CONV_K),
        'conv_out_norm': gain(21, (DEPTH_2, CONV_WIDTH)),
        'w_out': w(22, (DEPTH_2, D_MIX_2, D_MODEL), D_MIX_2),
        'ffn2_norm': gain(23, (DEPTH_2, D_MODEL)),
        'ffn2_w_gate': w(24, (DEPTH_2, D_MODEL, D_FF), D_MODEL),
        'ffn2_w_up': w(25, (DEPTH_2, D_MODEL, D_FF), D_MODEL),
        'ffn2_w_down': w(26, (DEPTH_2, D_FF, D_MODEL), D_FF),
    }

def second_block(x, positions, ffn1_norm, ffn1_w_gate, ffn1_w_up, ffn1_w_down, mix_norm, w_in,
              ssd_conv_w, ssd_conv_b, ssd_dt_bias, ssd_a_log, ssd_d, ssd_norm,
              mla_q_norm, mla_w_uq, mla_kv_norm, mla_w_ukv, mla_q_head_norm, mla_k_head_norm,
              mla_out_norm, conv_w, conv_out_norm, w_out,
              ffn2_norm, ffn2_w_gate, ffn2_w_up, ffn2_w_down):
    pts = split_points(IN_SIZES)
    for l in range(DEPTH_2):
        x = x + 0.5 * swiglu(rms_norm(x, ffn1_norm[l]), ffn1_w_gate[l], ffn1_w_up[l], ffn1_w_down[l])
        h = rms_norm(x, mix_norm[l])
        u = h @ w_in[l]
        z, xbc, dt_raw, q_lat, kv_lat, k_pe, c_h, c_b, c_c = jnp.split(u, pts, axis=-1)
        y_ssd = ssd_mixer(z, xbc, dt_raw, ssd_conv_w[l], ssd_conv_b[l], ssd_dt_bias[l],
                          ssd_a_log[l], ssd_d[l], ssd_norm[l])
        y_mla = mla_mixer(q_lat, kv_lat, k_pe, positions, mla_q_norm[l], mla_w_uq[l], mla_kv_norm[l],
                          mla_w_ukv[l], mla_q_head_norm[l], mla_k_head_norm[l], mla_out_norm[l])
        y_conv = conv_mixer(c_h, c_b, c_c, conv_w[l], conv_out_norm[l])
        x = x + jnp.concatenate([y_ssd, y_mla, y_conv], axis=-1) @ w_out[l]
        x = x + 0.5 * swiglu(rms_norm(x, ffn2_norm[l]), ffn2_w_gate[l], ffn2_w_up[l], ffn2_w_down[l])
    return x


def setup_inputs(seed=0):
    out = dict(first_inputs(seed))
    for name, value in second_inputs(seed + 1).items():
        if name != "x":
            out[name + "_2"] = value
    return out


def reference(
    x, norm_mix_g, w_in, shift_mu, sb_out_g, rw_w0, rw_w2, rw_a0, rw_a2, rw_g2, rw_k_k, rw_k_a,
    rw_r_k, rw_ln_w, rw_ln_b, w_out, norm_ffn_g, router_grp_w, router_grp_b, router_exp_w,
    router_exp_b, exp_w_gate, exp_w_up, exp_w_down, final_norm_g, positions_2, ffn1_norm_2,
    ffn1_w_gate_2, ffn1_w_up_2, ffn1_w_down_2, mix_norm_2, w_in_2, ssd_conv_w_2, ssd_conv_b_2,
    ssd_dt_bias_2, ssd_a_log_2, ssd_d_2, ssd_norm_2, mla_q_norm_2, mla_w_uq_2, mla_kv_norm_2,
    mla_w_ukv_2, mla_q_head_norm_2, mla_k_head_norm_2, mla_out_norm_2, conv_w_2,
    conv_out_norm_2, w_out_2, ffn2_norm_2, ffn2_w_gate_2, ffn2_w_up_2, ffn2_w_down_2,
):
    x = first_block(
        x, norm_mix_g, w_in, shift_mu, sb_out_g, rw_w0, rw_w2, rw_a0, rw_a2, rw_g2, rw_k_k,
        rw_k_a, rw_r_k, rw_ln_w, rw_ln_b, w_out, norm_ffn_g, router_grp_w, router_grp_b,
        router_exp_w, router_exp_b, exp_w_gate, exp_w_up, exp_w_down, final_norm_g,
    )
    return second_block(
        x, positions_2, ffn1_norm_2, ffn1_w_gate_2, ffn1_w_up_2, ffn1_w_down_2, mix_norm_2,
        w_in_2, ssd_conv_w_2, ssd_conv_b_2, ssd_dt_bias_2, ssd_a_log_2, ssd_d_2, ssd_norm_2,
        mla_q_norm_2, mla_w_uq_2, mla_kv_norm_2, mla_w_ukv_2, mla_q_head_norm_2,
        mla_k_head_norm_2, mla_out_norm_2, conv_w_2, conv_out_norm_2, w_out_2, ffn2_norm_2,
        ffn2_w_gate_2, ffn2_w_up_2, ffn2_w_down_2,
    )


_drawn_inputs = setup_inputs


def setup_inputs(seed=0):
    import zlib

    import numpy as np

    out = dict(_drawn_inputs(seed))
    spreads = {}
    factors = {'rw_k_k': 2.677, 'router_grp_b': 4.628}
    for name, (base, spread) in spreads.items():
        noise = np.random.default_rng([zlib.crc32(name.encode()), seed]).standard_normal(out[name].shape)
        drawn = base * np.exp(spread * noise) if base else spread * noise
        out[name] = __import__('jax').numpy.asarray(drawn.astype(out[name].dtype))
    for name, factor in factors.items():
        out[name] = (out[name] * factor).astype(out[name].dtype)
    return out
```

```python
import math
from contextlib import ExitStack

import numpy as np

import concourse.bass as bass
from concourse import mybir

ALU = mybir.AluOpType
ACT = mybir.ActivationFunctionType
F32 = mybir.dt.float32
I32 = mybir.dt.int32
AX = mybir.AxisListType

NR = 3
SLOT = 6144
ARENA = 26000
BIG = 1.0e30
KAP = math.exp(-0.5)
LEVELS = [1, 2, 4, 8, 16, 32, 64]

CN = {n: i for i, n in enumerate(
    ["ident", "ones", "bones", "ntri", "nones", "mnegs", "triu", "ones2", "tril", "mnegf", "mnegb", "ms"]
    + [f"lv{m}" for m in LEVELS])}


def constants():
    s = np.arange(128)[:, None]
    t = np.arange(128)[None, :]
    f = lambda c: c.astype(np.float32)
    tiles = {
        "ident": f(s == t), "ones": np.ones((128, 128), np.float32), "bones": f(s // 64 == t // 64),
        "ntri": -f(s >= t), "nones": -np.ones((128, 128), np.float32), "mnegs": -BIG * f(s >= t),
        "triu": f(s <= t), "ones2": np.ones((128, 128), np.float32), "tril": f(s >= t),
        "mnegf": -BIG * f(s > t), "mnegb": -BIG * f(s < t), "ms": f(s < t),
    }
    for m in LEVELS:
        tiles[f"lv{m}"] = f((s // (2 * m) == t // (2 * m)) & (s % (2 * m) < m) & (t % (2 * m) >= m))
    inv = (10000.0 ** (-np.arange(16, dtype=np.float64) / 16)).astype(np.float32)
    return np.concatenate([tiles[n].astype(np.float32) for n in CN] + [np.tile(inv[None], (128, 1))], axis=1)


PRM = {}
_n = 0
for _name, _k in ([("norm_mix_g", 8), ("shift_mu", 14), ("sb_out_g", 4), ("w0", 4), ("a0", 4), ("k_k", 4), ("k_a", 4),
                   ("r_k", 4), ("ln_w", 4), ("ln_b", 4), ("norm_ffn_g", 8)]
                  + [(f"{a}{l}", b) for l in range(2) for a, b in (
                      ("ffn1_norm", 8), ("mix_norm", 8), ("conv_w", 60), ("conv_b", 12), ("ssd_norm", 8), ("ssd_d", 8),
                      ("q_norm", 2), ("kv_norm", 1), ("out_norm", 4), ("cw", 12), ("conv_out", 4), ("ffn2_norm", 8))]):
    PRM[_name] = _n
    _n += _k
NPRM = _n
ROW = {"router_b": 0}
for _l in range(2):
    ROW.update({f"dt_bias{_l}": 36 + 256 * _l, f"a_log{_l}": 68 + 256 * _l, f"qk_g{_l}": 100 + 256 * _l})
NROW = 36 + 512


class Sem:

    def __init__(self, sem):
        self.sem, self.n = sem, 0


class Queue(Sem):

    def __init__(self, sem):
        super().__init__(sem)
        self.items, self.seen = [], {}

    def need(self, *toks):
        for t in toks:
            if t is None:
                continue
            if isinstance(t, list):
                self.need(*t)
                continue
            s, v = t
            if self.seen.get(s, 0) < v:
                self.seen[s] = v
                self.items.append((s.sem, v))

    def raw(self, fn, *toks):
        self.need(*toks)
        self.items.append((fn, None, 0))

    def op(self, fn, *toks):
        self.need(*toks)
        self.n += 1
        self.items.append((fn, self.sem, 1))
        return (self, self.n)

    def dma(self, out, in_, sem, *toks):
        self.need(*toks)
        sem.n += 16
        self.items.append((lambda e: e.dma_start(out, in_), sem.sem, 16))
        return (sem, sem.n)

    def emit(self, e):
        for it in self.items:
            if len(it) == 2:
                e.wait_ge(it[0], it[1])
            else:
                ins = it[0](e)
                if it[1] is not None:
                    ins.then_inc(it[1], it[2])

    def tt(self, out, a, b, op, *toks):
        return self.op(lambda e: e.tensor_tensor(out, a, b, op), *toks)

    def ts(self, out, a, s1, s2, op0, op1, *toks):
        if s2 is None:
            return self.op(lambda e: e.tensor_scalar(out, a, s1, None, op0), *toks)
        return self.op(lambda e: e.tensor_scalar(out, a, s1, s2, op0, op1), *toks)

    def stt(self, out, a, s, b, op0, op1, *toks):
        return self.op(lambda e: e.scalar_tensor_tensor(out=out, in0=a, scalar=s, in1=b, op0=op0, op1=op1), *toks)

    def cp(self, out, a, *toks):
        return self.op(lambda e: e.tensor_copy(out, a), *toks)

    def rec(self, out, a, *toks):
        return self.op(lambda e: e.reciprocal(out, a), *toks)

    def red(self, out, a, op, *toks):
        return self.op(lambda e: e.tensor_reduce(out, a, AX.X, op), *toks)

    def set(self, out, v, *toks):
        return self.op(lambda e: e.memset(out, v), *toks)

    def act(self, out, a, func, *toks, bias=None, scale=1.0, accum=None):
        kw = {"scale": scale}
        if bias is not None:
            kw["bias"] = bias
        if accum is not None:
            kw["accum_out"] = accum
        return self.op(lambda e: e.activation(out, a, func, **kw), *toks)


def program(nc, I, out, dbg=None):
    MUL, ADD, SUB, MAX = ALU.mult, ALU.add, ALU.subtract, ALU.max
    with ExitStack() as ctx:
        def sb(name, n, dt=F32):
            return ctx.enter_context(nc.sbuf_tensor(name, [128, n], dt))

        def sem(name):
            return ctx.enter_context(nc.semaphore(name))

        ring = sb("ring", NR * SLOT)
        xtok_ = sb("xtok", 2048)
        xnT_ = sb("xnT", 2048)
        cst = sb("cst", len(CN) * 128 + 16)
        prm = sb("prm", NPRM)
        row = sb("row", NROW)
        small = sb("small", 256)
        comb_ = sb("comb", 64)
        rope_ = sb("rope", 192)
        posi = sb("posi", 2, I32)
        arena = sb("arena", ARENA)
        PS = [ctx.enter_context(nc.psum_tensor(f"ps{i}", [128, 512], F32)) for i in range(8)]
        xtok = xtok_[:, :].rearrange("p (t d) -> p t d", t=2)
        xnT = xnT_[:, :].rearrange("p (c t) -> p c t", c=8)
        mix1 = xnT

        T, V, A, G, L = (Queue(sem(f"s_{n}")) for n in ("pe", "dve", "act", "pool", "sp"))
        d0 = Sem(sem("d_first"))
        dslot = [Sem(sem(f"d_slot{i}")) for i in range(NR)]
        dout = Sem(sem("d_out"))
        free = [[] for _ in range(8)]

        def C(name, n=128):
            return cst[:, CN[name] * 128:CN[name] * 128 + n]

        invf = cst[:, len(CN) * 128:len(CN) * 128 + 16]

        def pr(name, i=0, n=1):
            return prm[:, PRM[name] + i:PRM[name] + i + n]

        def ar(o, n):
            assert o + n <= ARENA, (o, n)
            return arena[:, o:o + n]

        loads = []

        def wload(*parts):
            n = len(loads)
            s = n % NR
            off, views, dmas = 0, [], []
            for src in parts:
                k, a, b = src.shape
                v = ring[0:k, s * SLOT + off:s * SLOT + off + a * b].rearrange("p (a b) -> p a b", a=a)
                views.append(v)
                dmas.append((v, src))
                off += a * b
            assert off <= SLOT
            dslot[s].n += 16 * len(parts)
            loads.append({"dmas": dmas, "sem": dslot[s], "tok": (dslot[s], dslot[s].n), "done": None})
            return loads[-1], views

        def cols(w, a, b):
            return w.rearrange("(c p) n -> p c n", p=128)[:, :, a:b]

        def rows(w, a, b):
            return w.rearrange("(c p) n -> p c n", p=128)[:, a:b, :]

        def mm(out_, lhsT, rhs, start, stop, *toks, sig=False):
            fn = lambda e: e.matmul(out_, lhsT, rhs, start=start, stop=stop, skip_group_check=True)
            if sig:
                return T.op(fn, *toks)
            T.raw(fn, *toks)
            return None

        def tr(out_, in_, *toks, sig=False):
            idn = C("ident")[0:in_.shape[0], 0:in_.shape[0]]
            fn = lambda e: e.transpose(out_, in_, idn)
            if sig:
                return T.op(fn, *toks)
            T.raw(fn, *toks)
            return None

        def barrier():
            every = [(q, q.n) for q in (T, V, A, G) if q.n]
            for q in (T, V, A, G):
                q.need(*every)

        first = [L.dma(xtok, I["x"].rearrange("(t p) d -> p t d", p=128), d0),
                 L.dma(cst[:, :], I["cst"], d0), L.dma(prm[:, :], I["prm"], d0), L.dma(row[:, :], I["rowp"], d0),
                 L.dma(posi[:, :], I["positions"], d0)][-1:]
        for q in (T, V, A, G):
            q.need(*first)

        def rstd(out_, ssq, n, eps, *toks):
            t = V.ts(out_, ssq, 1.0 / n, eps, MUL, ADD, *toks)
            t = A.act(out_, out_, ACT.Sqrt, t)
            return V.rec(out_, out_, t)

        def norm_T(gname, xn_off, *toks):
            xn = ar(xn_off, 2048).rearrange("p (t d) -> p t d", t=2)
            res = []
            for tt in range(2):
                ss = small[:, tt:tt + 1]
                t = A.act(xn[:, tt], xtok[:, tt], ACT.Square, *toks, accum=ss)
                t = rstd(ss, ss, 1024, 1e-6, t)
                t = V.ts(xn[:, tt], xtok[:, tt], ss, None, MUL, None, t)
                for hb in range(2):
                    b = tt * 2 + hb
                    T.need(t, *free[b])
                    for k in range(4):
                        c = hb * 4 + k
                        p = tr(PS[b][:, k * 128:k * 128 + 128], xn[:, tt, c * 128:c * 128 + 128], sig=(k == 3))
                    for k in range(4):
                        c = hb * 4 + k
                        o, i, g = xnT[:, c, tt * 128:tt * 128 + 128], PS[b][:, k * 128:k * 128 + 128], pr(gname, c)
                        if hb:
                            e = V.ts(o, i, g, None, MUL, None, p)
                        else:
                            e = A.act(o, i, ACT.Copy, p, scale=g)
                    free[b] = [e]
                    res.append(e)
            return res

        def proj_T(ld, w, c0, bank, half, last, *toks):
            T.need(ld["tok"], *toks)
            if half == 0:
                T.need(*free[bank])
            for c in range(8):
                p = mm(PS[bank][:, half * 256:half * 256 + 256], w[:, c, c0:c0 + 128], xnT[:, c, :],
                       c == 0, c == 7, sig=(c == 7))
            if last:
                ld["done"] = p
            return p

        def out_proj(mixT, nk, lds, *toks):
            T.need(*toks, *free[4], *free[5], *free[6], *free[7])
            k = 0
            for ld, w in lds:
                T.need(ld["tok"])
                for i in range(w.shape[1]):
                    for tt in range(2):
                        for dh in range(2):
                            p = mm(PS[4 + 2 * tt + dh][:, :], mixT[:, k, tt * 128:tt * 128 + 128],
                                   w[:, i, dh * 512:dh * 512 + 512], k == 0, k == nk - 1,
                                   sig=(tt == 1 and dh == 1))
                    k += 1
                ld["done"] = p
            res = []
            for b in range(4):
                o = xtok[:, b // 2, (b % 2) * 512:(b % 2) * 512 + 512]
                e = V.tt(o, PS[4 + b][:, :], o, ADD, p)
                free[4 + b] = [e]
                res.append(e)
            return res

        w_in = I["w_in"][0]
        ld4, (w4,) = wload(cols(w_in, 3072, 3328))
        wl2, wg2 = ar(18468, 512)[:, None, :], ar(18980, 512)[:, None, :]
        dlo = Sem(sem("d_lora"))
        L.dma(wl2[:, 0], I["w2a2"], dlo)
        lora_t = L.dma(wg2[:, 0], I["rw_g2"][0], dlo)
        ld2, (w2,) = wload(cols(w_in, 1536, 2304))
        ld3, (w3,) = wload(cols(w_in, 2304, 3072))
        ld0, (w0_,) = wload(cols(w_in, 0, 768))
        ld1, (w1_,) = wload(cols(w_in, 768, 1536))
        ldo1 = [wload(rows(I["w_out"][0], 0, 4)), wload(rows(I["w_out"][0], 4, 8))]
        ldo1 = [(a, b[0]) for a, b in ldo1]

        xn_t = norm_T("norm_mix_g", 8212)

        urw = ar(0, 3598).rearrange("p (f t) -> p f t", f=14)
        um = ar(3600, 3584).rearrange("p (f t) -> p f t", f=14)
        Cc = ar(7184, 1028).rearrange("p (f t) -> p f t", f=4)
        EP = ar(8212, 1032).rearrange("p (f c t) -> p f c t", f=4, c=2)
        EN = ar(9244, 1032).rearrange("p (f c t) -> p f c t", f=4, c=2)
        v4 = lambda o: ar(o, 1024).rearrange("p (f t) -> p f t", f=4)
        aT, kkT, rT, zT, bT, kT, gT = (v4(o) for o in (10276, 11300, 12324, 13348, 14372, 15396, 16420))
        Vtok = ar(17444, 1024).rearrange("p (c n) -> p c n", c=2)
        BK = ar(18468, 1024).rearrange("p (c n) -> p c n", c=2)
        AT = ar(19492, 2048).rearrange("p (q t) -> p q t", q=16)
        X = ar(21540, 2048).rearrange("p (q t) -> p q t", q=16)
        XT = ar(23588, 2048).rearrange("p (q t) -> p q t", q=16)
        Y = ar(0, 2048).rearrange("p (q t) -> p q t", q=16)
        M = ar(2048, 1536).rearrange("p (b q t) -> p b q t", b=3, q=4)
        tmp = [v4(0), v4(1024), v4(2048)]
        qk = ar(19492, 2048).rearrange("p (f t) -> p f t", f=8)
        vtok = ar(21540, 1024).rearrange("p (c n) -> p c n", c=2)
        sbe = ar(22564, 768).rearrange("p (b t) -> p b t", b=2)
        sbs = ar(23332, 768).rearrange("p (b t) -> p b t", b=2)
        sbw = ar(24100, 768).rearrange("p (b t) -> p b t", b=2)
        sbo = ar(24868, 1024).rearrange("p (f t) -> p f t", f=4)

        z0 = V.set(urw[:, :, 0:1], 0.0)
        u_t = [None] * 14
        order = [(ld4, w4, [12, 13], 12)] + [(ld2, w2, list(range(0, 6)), 0), (ld3, w3, list(range(6, 12)), 6)]
        nb = 0
        um_t = [None] * 14
        for ld, w, fs, f0 in order:
            for i in range(0, len(fs), 2):
                b = 4 + nb % 4
                nb += 1
                f = fs[i]
                proj_T(ld, w, (f - f0) * 128, b, 0, False, *xn_t)
                p = proj_T(ld, w, (f + 1 - f0) * 128, b, 1, i + 2 >= len(fs))
                e = A.act(urw[:, f:f + 2, 1:257], PS[b][:, :].rearrange("p (f t) -> p f t", f=2), ACT.Copy, p)
                free[b] = [e]
                for ff in (f, f + 1):
                    t = G.tt(um[:, ff], urw[:, ff, 0:256], urw[:, ff, 1:257], SUB, e, z0)
                    um_t[ff] = V.stt(um[:, ff], um[:, ff], pr("shift_mu", ff), urw[:, ff, 1:257], MUL, ADD, t)
        qk_t = [None] * 8
        for ld, w, fs, f0 in ((ld0, w0_, list(range(6)), 0), (ld1, w1_, [6, 7], 6)):
            for i in range(0, len(fs), 2):
                b = 4 + nb % 4
                nb += 1
                f = fs[i]
                proj_T(ld, w, (f - f0) * 128, b, 0, False)
                p = proj_T(ld, w, (f + 1 - f0) * 128, b, 1, f == 4)
                e = A.act(qk[:, f:f + 2, :], PS[b][:, :].rearrange("p (f t) -> p f t", f=2), ACT.Copy, p,
                          scale=0.125 if f < 4 else 1.0)
                free[b] = [e]
                qk_t[f] = qk_t[f + 1] = e
        vt_t = [None, None]
        for tt in range(2):
            b = 4 + nb % 4
            nb += 1
            T.need(*free[b])
            for c in range(8):
                p = mm(PS[b][:, :], xnT[:, c, tt * 128:tt * 128 + 128], w1_[:, c, 256:768], c == 0, c == 7, sig=(c == 7))
            vt_t[tt] = A.act(vtok[:, tt, :], PS[b][:, :], ACT.Copy, p)
            free[b] = [vt_t[tt]]
        ld1["done"] = p
        xn_free = p

        T.need(lora_t)
        th = tmp[0][:, 0]
        t = A.act(th[0:64], um[0:64, 12], ACT.Tanh, *um_t)
        n0 = V.ts(small[:, 8:16], prm[:, PRM["w0"]:PRM["w0"] + 8], -1.0, None, MUL, None)
        sgx = tmp[0][:, 1]
        e1 = A.act(sgx, um[:, 13], ACT.Exp, scale=-1.0)
        e1 = V.ts(sgx, sgx, 1.0, None, ADD, None, e1)
        e1 = V.rec(sgx, sgx, e1)
        lor = []
        for half in range(2):
            b = half
            T.need(t, *free[b])
            for k in range(2):
                f = half * 2 + k
                p = mm(PS[b][:, k * 256:k * 256 + 256], wl2[0:64, 0, f * 128:f * 128 + 128], th[0:64], True, True, sig=(k == 1))
            for k in range(2):
                f = half * 2 + k
                e = A.act(tmp[1][:, f], PS[b][:, k * 256:k * 256 + 256], ACT.Exp, p, n0, scale=-1.0, bias=small[:, 8 + f:9 + f])
            free[b] = [e]
            lor.append(e)
        for half in range(2):
            b = 2 + half
            T.need(*free[b])
            for k in range(2):
                f = half * 2 + k
                p = mm(PS[b][:, k * 256:k * 256 + 256], wl2[64:128, 0, f * 128:f * 128 + 128], um[64:128, 12], True, True, sig=(k == 1))
            for k in range(2):
                f = half * 2 + k
                e = A.act(aT[:, f], PS[b][:, k * 256:k * 256 + 256], ACT.Exp, p, scale=-1.0, bias=small[:, 12 + f:13 + f])
            free[b] = [e]
        at = V.ts(aT, aT, 1.0, None, ADD, None, e)
        at = V.rec(aT, aT, at)
        gt = []
        for half in range(2):
            b = half
            T.need(e1, *free[b])
            for k in range(2):
                f = half * 2 + k
                p = mm(PS[b][:, k * 256:k * 256 + 256], wg2[:, 0, f * 128:f * 128 + 128], sgx, True, True, sig=(k == 1))
            e = A.act(gT[:, 2 * half:2 * half + 2, :], PS[b][:, :].rearrange("p (f t) -> p f t", f=2), ACT.Copy, p)
            free[b] = [e]
            gt.append(e)
        lora_done = p
        lw = V.ts(tmp[1], tmp[1], 1.0, None, ADD, None, *lor)
        lw = V.rec(tmp[1], tmp[1], lw)
        c0 = V.set(Cc[:, :, 0:1], 0.0)
        one = C("ones", 128)
        ct = []
        on256 = V.set(tmp[2][:, 0], 1.0, *um_t)
        for f in range(4):
            ct.append(V.op(lambda e, f=f: e.tensor_tensor_scan(Cc[:, f, 1:257], tmp[2][:, 0], tmp[1][:, f], 0.0, MUL, ADD), lw, on256))
        dt_ = []
        for c in range(2):
            cm = Cc[:, :, 64 + 128 * c:65 + 128 * c].to_broadcast([128, 4, 129])
            dt_.append(V.tt(EP[:, :, c, :], Cc[:, :, 128 * c:128 * c + 129], cm, SUB, *ct, c0, xn_free))
        en = A.act(EN, EP, ACT.Exp, *dt_, scale=KAP)
        ep = A.act(EP, EP, ACT.Exp, en, scale=-KAP)
        sct = V.tt(small[:, 16:20], Cc[:, :, 192:193].rearrange("p f a -> p (f a)"), Cc[:, :, 64:65].rearrange("p f a -> p (f a)"), SUB, *ct)
        sct = A.act(small[:, 16:20], small[:, 16:20], ACT.Exp, sct, scale=-KAP)

        kkr = []
        for f in range(4):
            kkr.append(V.ts(kkT[:, f], um[:, 4 + f], pr("k_k", f), None, MUL, None))
        sq = A.act(tmp[2], kkT, ACT.Square, *kkr, *ct)
        kn = []
        for half in range(2):
            b = 2 + half
            T.need(sq, *free[b])
            p = mm(PS[b][:, :], C("bones"), tmp[2][:, 2 * half:2 * half + 2], True, True, sig=True)
            e = V.ts(tmp[1][:, 2 * half:2 * half + 2], PS[b][:, :].rearrange("p (f t) -> p f t", f=2), 1e-24, None, MAX, None, p, *ct)
            free[b] = [e]
            kn.append(e)
        t = A.act(tmp[1], tmp[1], ACT.Sqrt, *kn)
        t = V.rec(tmp[1], tmp[1], t)
        kkt = V.tt(kkT, kkT, tmp[1], MUL, t, sq)
        km = []
        for f in range(4):
            t = V.ts(tmp[2][:, f], aT[:, f], 1.0, pr("k_a", f), SUB, MUL, at, kn)
            km.append(V.stt(um[:, 4 + f], tmp[2][:, f], 1.0, um[:, 4 + f], ADD, MUL, t, *kkr))
        ch = lambda x: x.rearrange("p f (c t) -> p f c t", c=2)
        zt, rt, bt, kt = [], [], [], []
        ba = G.tt(aT, aT, kkT, MUL, kkt, *km)
        for c in range(2):
            s = slice(128 * c, 128 * c + 128)
            zt.append(V.stt(zT[:, :, s], kkT[:, :, s], -1.0, EP[:, :, c, 0:128], MUL, MUL, kkt, ep))
            rt.append(G.tt(rT[:, :, s], um[:, 0:4, s], EP[:, :, c, 1:129], MUL, ep))
            bt.append(V.tt(bT[:, :, s], aT[:, :, s], EN[:, :, c, 1:129], MUL, ba, en))
            kt.append(G.tt(kT[:, :, s], um[:, 4:8, s], EN[:, :, c, 1:129], MUL, en, *km))
        bo = G.tt(tmp[0], um[:, 0:4], um[:, 4:8], MUL, *km, gt)
        bb = []
        for f in range(4):
            bb.append(V.ts(tmp[0][:, f], tmp[0][:, f], pr("r_k", f), None, MUL, None, bo))
        bon = []
        for half in range(2):
            b = half
            T.need(*bb, *free[b])
            p = mm(PS[b][:, :], C("bones"), tmp[0][:, 2 * half:2 * half + 2], True, True, sig=True)
            e = V.tt(um[:, 4 + 2 * half:6 + 2 * half], PS[b][:, :].rearrange("p (f t) -> p f t", f=2),
                     um[:, 8 + 2 * half:10 + 2 * half], MUL, p, bo, *kt)
            free[b] = [e]
            bon.append(e)
        tk = []
        for c in range(2):
            b = 2 + c
            T.need(*free[b])
            for f in range(4):
                p = tr(PS[b][:, f * 128:f * 128 + 128], um[:, 8 + f, c * 128:c * 128 + 128], sig=(f == 3))
            e = A.act(Vtok[:, c, :], PS[b][:, :], ACT.Copy, p)
            free[b] = [e]
            tk.append(e)
        for c, (src, st) in enumerate(((bT, bt), (kT, kt))):
            b = c
            T.need(*st, *free[b])
            for f in range(4):
                p = tr(PS[b][:, f * 128:f * 128 + 128], src[:, f, 0:128], sig=(f == 3))
            e = A.act(BK[:, c, :], PS[b][:, :], ACT.Copy, p, lora_done)
            free[b] = [e]
            tk.append(e)

        wfree = [[], []]
        so_t = []
        for h in range(8):
            j, po, i = h // 2, 64 * (h % 2), h % 2
            b = 4 + i
            q, k = qk[po:po + 64, j], qk[po:po + 64, 4 + j]
            z = PS[b][:, 0:384]
            T.need(qk_t[j], qk_t[4 + j], *free[b])
            mm(PS[b][:, 0:256], k[:, 0:128], q, True, False)
            mm(PS[b][:, 256:384], k[:, 128:256], q[:, 128:256], False, False)
            mm(PS[b][:, 0:128], C("ident"), C("mnegs"), False, False)
            p = mm(PS[b][:, 256:384], C("ident"), C("mnegs"), False, True, sig=True)
            t = A.act(sbe[:, i], z, ACT.Abs, p, *wfree[i])
            t = A.act(sbe[:, i], sbe[:, i], ACT.Exp, t, scale=-1.0)
            t = A.act(sbe[:, i], sbe[:, i], ACT.Ln, t, bias=1.0)
            t = V.stt(sbs[:, i], z, 0.0, sbe[:, i], MAX, ADD, t)
            T.need(t)
            mm(PS[b][:, 0:256], C("ntri"), sbs[:, i, 0:256], False, False)
            mm(PS[b][:, 128:256], C("nones"), sbs[:, i, 256:384], False, False)
            p = mm(PS[b][:, 256:384], C("ntri"), sbs[:, i, 256:384], False, True, sig=True)
            t = A.act(sbw[:, i], z, ACT.Exp, p)
            free[b] = [t]
            ob = 6 + j % 2
            T.need(t, *vt_t)
            if i == 0:
                T.need(*free[ob])
            hs = slice(h * 64, h * 64 + 64)
            mm(PS[ob][po:po + 64, 0:256], vtok[:, 0, hs], sbw[:, i, 0:256], True, False)
            p = mm(PS[ob][po:po + 64, 128:256], vtok[:, 1, hs], sbw[:, i, 256:384], False, True, sig=True)
            wfree[i] = [p]
            if i == 1:
                t = V.cp(sbo[:, j], PS[ob][:, 0:256], p)
                free[ob] = [t]
                so_t.append(t)
        sq2 = EP4 = ar(22564, 1024).rearrange("p (f t) -> p f t", f=4)
        s2 = A.act(sq2, sbo, ACT.Square, *so_t, *wfree[0], *wfree[1])
        mt = []
        rr = ar(19492, 1024).rearrange("p (f t) -> p f t", f=4)
        rg = []
        for half in range(2):
            b = 4 + half
            T.need(s2, *free[b])
            p = mm(PS[b][:, :], C("bones"), sq2[:, 2 * half:2 * half + 2], True, True, sig=True)
            e = V.ts(rr[:, 2 * half:2 * half + 2], PS[b][:, :].rearrange("p (f t) -> p f t", f=2), 1.0 / 64, 1e-6, MUL, ADD, p)
            free[b] = [e]
            rg.append(e)
        t = A.act(rr, rr, ACT.Sqrt, *rg)
        t = V.rec(rr, rr, t)
        for f in range(4):
            mt.append(V.stt(mix1[:, f], sbo[:, f], pr("sb_out_g", f), rr[:, f], MUL, MUL, t, xn_free))
        sb_done = mt[-1]

        AZ = V.cp
        at_t = []
        for g in range(4):
            c, par = g // 2, g % 2
            b = g
            T.need(*zt, *bt, *free[b])
            for i in range(4):
                po, s = 64 * par, slice(128 * c, 128 * c + 128)
                p = mm(PS[b][:, i * 128:i * 128 + 128], bT[po:po + 64, i, s], zT[po:po + 64, i, s], True, True, sig=(i == 3))
            ms = C("ms")[:, None, :].to_broadcast([128, 4, 128])
            e = V.tt(AT[:, 4 * g:4 * g + 4], PS[b][:, :].rearrange("p (q t) -> p q t", q=4), ms, MUL, p, sb_done)
            free[b] = [e]
            at_t.append(e)
        idb = C("ident")[:, None, :].to_broadcast([128, 4, 128])
        p3 = lambda b: PS[b][:, :].rearrange("p (q t) -> p q t", q=4)
        x_t = [[] for _ in range(4)]
        y_r = [[] for _ in range(4)]
        m_r = [[] for _ in range(3)]
        mi = 0
        for li, m in enumerate(LEVELS):
            lastl = li == len(LEVELS) - 1
            lv = C(f"lv{m}")[:, None, :].to_broadcast([128, 4, 128])
            for g in range(4):
                gs = slice(4 * g, 4 * g + 4)
                Mb = M[:, mi % 3]
                mtok = G.tt(Mb, AT[:, gs], lv, MUL, at_t[g], *m_r[mi % 3], *bon)
                b0, b1, b2 = (g % 2) * 3, (g % 2) * 3 + 1, (g % 2) * 3 + 2
                T.need(mtok, *x_t[g], *free[b0])
                for i in range(4):
                    q = 4 * g + i
                    p = mm(PS[b0][:, i * 128:i * 128 + 128], Mb[:, i], C("ident") if li == 0 else X[:, q], True, True, sig=(i == 3))
                m_r[mi % 3] = [p]
                mi += 1
                if li == 0:
                    e1 = V.tt(X[:, gs], p3(b0), idb, ADD, p, sb_done)
                    e2 = G.tt(XT[:, gs], Mb, idb, ADD, mtok, sb_done)
                    m_r[(mi - 1) % 3].append(e2)
                    free[b0] = [e1]
                    x_t[g] = [e1, e2]
                    continue
                yt = A.act(Y[:, gs], p3(b0), ACT.Copy, p, *y_r[g])
                free[b0] = [yt]
                T.need(yt, *free[b1], *free[b2])
                if not lastl:
                    for i in range(4):
                        q = 4 * g + i
                        p1 = mm(PS[b1][:, i * 128:i * 128 + 128], XT[:, q], Y[:, q], True, True, sig=(i == 3))
                for i in range(4):
                    q = 4 * g + i
                    p2 = mm(PS[b2][:, i * 128:i * 128 + 128], Y[:, q], XT[:, q], True, True, sig=(i == 3))
                y_r[g] = [p2]
                x_t[g] = []
                if not lastl:
                    e1 = V.tt(X[:, gs], p3(b1), X[:, gs], ADD, p1)
                    free[b1] = [e1]
                    x_t[g].append(e1)
                e2 = V.tt(XT[:, gs], p3(b2), XT[:, gs], ADD, p2)
                free[b2] = [e2]
                x_t[g].append(e2)

        GT = ar(8212, 2048).rearrange("p (k q t) -> p k q t", k=4, q=4)
        RHS = ar(10276, 1024).rearrange("p (c q n) -> p c q n", c=2, q=8)
        U = ar(0, 1024).rearrange("p (c q n) -> p c q n", c=2, q=8)
        S0 = ar(1024, 256).rearrange("p (f n) -> p f n", f=4)
        oT = kkT
        o_t = []
        s0_t = []
        msb = C("ms")[:, None, :].to_broadcast([128, 4, 128])
        mib = C("triu")[:, None, :].to_broadcast([128, 4, 128])
        gr = [[], [], []]
        for c in range(2):
            s = slice(128 * c, 128 * c + 128)
            ut = [None, None]
            for hg in range(2):
                g = c * 2 + hg
                hh = [2 * i + hg for i in range(4)]
                po = 64 * hg
                fb = lambda x, h: x[64 * (h % 2):64 * (h % 2) + 64, h // 2, s]
                mats = ((0, kT, zT, msb), (1, kT, rT, mib), (2, bT, rT, mib))
                gt_ = []
                for k, l_, r_, mk in mats:
                    b = k
                    T.need(*kt, *rt, *free[b], *x_t[g])
                    for i, h in enumerate(hh):
                        p = mm(PS[b][:, i * 128:i * 128 + 128], fb(l_, h), fb(r_, h), True, True, sig=(i == 3))
                    e = V.tt(GT[:, k], p3(b), mk, MUL, p, *gr[k], *zt, *bt, *rt, *kt)
                    free[b] = [e]
                    gt_.append(e)
                b = 3
                T.need(gt_[0], *tk, *s0_t, *free[b])
                for i, h in enumerate(hh):
                    o = PS[b][:, i * 64:i * 64 + 64]
                    p = mm(o, GT[:, 0, i], Vtok[:, c, h * 64:h * 64 + 64], i == 0, c == 0 and i == 3, sig=(c == 0 and i == 3))
                    if c == 1:
                        p = mm(o, fb(zT, h), S0[po:po + 64, h // 2], False, i == 3, sig=(i == 3))
                gr[0] = [p]
                rhs_t = A.act(RHS[:, c, 4 * hg:4 * hg + 4], PS[b][:, 0:256].rearrange("p (q n) -> p q n", q=4), ACT.Copy, p, *bt)
                free[b] = [rhs_t]
                b = 4
                T.need(rhs_t, *free[b])
                for i, h in enumerate(hh):
                    p = mm(PS[b][:, i * 64:i * 64 + 64], XT[:, 4 * g + i], RHS[:, c, 4 * hg + i], True, True, sig=(i == 3))
                ut[hg] = A.act(U[:, c, 4 * hg:4 * hg + 4], PS[b][:, 0:256].rearrange("p (q n) -> p q n", q=4), ACT.Copy, p, y_r[0], y_r[1], y_r[2], y_r[3])
                free[b] = [ut[hg]]
                b = 5
                T.need(ut[hg], gt_[1], gt_[2], *free[b])
                for i, h in enumerate(hh):
                    o = PS[b][po:po + 64, i * 128:i * 128 + 128]
                    mm(o, Vtok[:, c, h * 64:h * 64 + 64], GT[:, 1, i], i == 0, False)
                    p = mm(o, U[:, c, 4 * hg + i], GT[:, 2, i], False, False, sig=True)
                    if c == 1:
                        p = mm(o, S0[po:po + 64, h // 2], fb(rT, h), False, i == 3, sig=True)
                gr[1] = gr[2] = [p]
                e = A.act(oT[po:po + 64, :, s], PS[b][po:po + 64, :].rearrange("p (j t) -> p j t", j=4), ACT.Copy, p, *zt, ba)
                free[b] = [e]
                o_t.append(e)
            if c == 0:
                b = 6
                T.need(*ut, *tk, *free[b])
                for h in range(8):
                    po = 64 * (h % 2)
                    o = PS[b][po:po + 64, (h // 2) * 64:(h // 2) * 64 + 64]
                    mm(o, BK[:, 0, h * 64:h * 64 + 64], U[:, 0, 4 * (h % 2) + h // 2], h < 2, False)
                    p = mm(o, BK[:, 1, h * 64:h * 64 + 64], Vtok[:, 0, h * 64:h * 64 + 64], False, h >= 6, sig=(h == 7))
                for f in range(4):
                    e = V.ts(S0[:, f], PS[b][:, f * 64:f * 64 + 64], small[:, 16 + f:17 + f], None, MUL, None, p, sct, *y_r)
                    s0_t.append(e)
                free[b] = [e]

        mu = v4(12324)
        sqd = v4(13348)
        us = []
        for half in range(2):
            b = half
            hs2 = slice(2 * half, 2 * half + 2)
            T.need(*o_t, *free[b])
            p = mm(PS[b][:, :], C("bones"), oT[:, hs2], True, True, sig=True)
            e = V.stt(mu[:, hs2], PS[b][:, :].rearrange("p (f t) -> p f t", f=2), -1.0 / 64, oT[:, hs2], MUL, ADD, p)
            free[b] = [e]
            us.append(e)
        s2 = A.act(sqd, mu, ACT.Square, *us)
        vr = []
        for half in range(2):
            b = 2 + half
            hs2 = slice(2 * half, 2 * half + 2)
            T.need(s2, *free[b])
            p = mm(PS[b][:, :], C("bones"), sqd[:, hs2], True, True, sig=True)
            e = V.ts(bT[:, hs2], PS[b][:, :].rearrange("p (f t) -> p f t", f=2), 1.0 / 64, 64e-5, MUL, ADD, p)
            free[b] = [e]
            vr.append(e)
        t = A.act(bT, bT, ACT.Sqrt, *vr)
        t = V.rec(bT, bT, t)
        fin = []
        for f in range(4):
            t1 = V.stt(mu[:, f], mu[:, f], pr("ln_w", f), bT[:, f], MUL, MUL, t, s2)
            t1 = V.stt(mu[:, f], mu[:, f], pr("ln_b", f), um[:, 4 + f], ADD, ADD, t1, *bon)
            fin.append(V.tt(mix1[:, 4 + f], mu[:, f], gT[:, f], MUL, t1, *gt))
        ot = out_proj(mix1, 8, ldo1, *mt, *fin)
        barrier()

        def dump(ap, n):
            t = [(q, q.n) for q in (T, V, A, G) if q.n]
            tk_ = L.dma(dbg[:, 0:n], ap, dout, *t)
            return tk_

        xn_t = norm_T("norm_ffn_g", 0, *ot)
        ldr, (wr,) = wload(I["router"].rearrange("p (c n) -> p c n", c=8))
        lg = ar(2048, 72).rearrange("p (t n) -> p t n", t=2)
        for tt in range(2):
            T.need(ldr["tok"], *xn_t, *free[4 + tt])
            for c in range(8):
                p = mm(PS[4 + tt][:, 0:36], xnT[:, c, tt * 128:tt * 128 + 128], wr[:, c, :], c == 0, c == 7, sig=(c == 7))
            e = V.tt(lg[:, tt], PS[4 + tt][:, 0:36], row[:, 0:36], ADD, p)
            free[4 + tt] = [e]
        ldr["done"] = p
        comb = comb_[:, :].rearrange("p (t n) -> p t n", t=2)
        sc = ar(2200, 400)
        on8 = ar(2600, 32)
        t_on = V.set(on8, 1.0)
        cmb_t = []
        for tt in range(2):
            o = 200 * tt
            gl, el = lg[:, tt, 0:4], lg[:, tt, 4:36]
            gm, gs_, ngm = sc[:, o:o + 1], sc[:, o + 1:o + 2], sc[:, o + 2:o + 3]
            ge, eq, cs, oh, pen = (sc[:, o + 4 + 4 * i:o + 8 + 4 * i] for i in range(5))
            ml, e1h, c32, m2 = (sc[:, o + 28 + 32 * i:o + 60 + 32 * i] for i in range(4))
            m1, mx2, ex, den, w1, w2s = (sc[:, o + 160 + i:o + 161 + i] for i in range(6))

            def onehot(dst, src, mx, cum, n, tk_):
                t_ = V.ts(dst, src, mx, None, ALU.is_equal, None, tk_)
                t_ = V.op(lambda e: e.tensor_tensor_scan(cum, on8[:, 0:n], dst, 0.0, MUL, ADD), t_, t_on)
                return V.stt(dst, cum, 1.0, dst, ALU.is_equal, MUL, t_)

            t = V.red(gm, gl, MAX, e)
            tg = V.ts(ngm, gm, -1.0, None, MUL, None, t)
            tg = A.act(ge, gl, ACT.Exp, tg, bias=ngm, accum=gs_)
            t = onehot(oh, gl, gm, cs, 4, t)
            t = V.ts(pen, oh, -1.0, BIG, ADD, MUL, t)
            t = V.tt(ml.rearrange("p (g n) -> p g n", g=4), el.rearrange("p (g n) -> p g n", g=4),
                     pen[:, :, None].to_broadcast([128, 4, 8]), ADD, t)
            t = V.red(m1, ml, MAX, t)
            t = onehot(e1h, ml, m1, c32, 32, t)
            t = V.stt(ml, e1h, -4.0 * BIG, ml, MUL, ADD, t)
            t = V.red(mx2, ml, MAX, t)
            t2 = onehot(m2, ml, mx2, c32, 32, t)
            t = V.tt(ex, mx2, m1, SUB, t)
            t = A.act(ex, ex, ACT.Exp, t)
            t = V.stt(den, ex, 1.0, gs_, ADD, MUL, t, tg)
            t = V.rec(w1, den, t)
            t = V.tt(w2s, ex, w1, MUL, t)
            t3 = V.ts(m2, m2, w2s, None, MUL, None, t, t2)
            cmb_t.append(V.stt(comb[:, tt], e1h, w1, m2, MUL, ADD, t3))

        hE = ar(3072, 1024).rearrange("p (b f t) -> p b f t", b=2, f=2)
        sg = ar(4096, 512).rearrange("p (b t) -> p b t", b=2)
        sg_r = [None, None]
        hE_r = [None, None]

        def gate_up(ld, wg, wu, c0, i, dst, dst_r):
            bg, bu = i % 2, 2 + i % 2
            pg = proj_T(ld, wg, c0, bg, 0, False, *xn_t)
            pu = proj_T(ld, wu, c0, bu, 0, False)
            a = A.act(sg[:, i % 2], PS[bg][:, 0:256], ACT.Silu, pg, sg_r[i % 2])
            free[bg] = [a]
            v = V.tt(dst, PS[bu][:, 0:256], sg[:, i % 2], MUL, pu, a, dst_r)
            free[bu] = [v]
            sg_r[i % 2] = v
            return v

        def moe_load(ei):
            return wload(cols(I["exp_w_gate"][0, ei], 0, 256), cols(I["exp_w_up"][0, ei], 0, 256),
                         rows(I["exp_w_down"][0, ei], 0, 2))

        for ei in range(32):
            ld, (wg, wu, wd) = moe_load(ei)
            hv = [gate_up(ld, wg, wu, 128 * f, f, hE[:, ei % 2, f], hE_r[ei % 2]) for f in range(2)]
            for tt in range(2):
                for dh in range(2):
                    b = 4 + 2 * tt + dh
                    T.need(*hv, *free[b])
                    for f in range(2):
                        p = mm(PS[b][:, :], hE[:, ei % 2, f, tt * 128:tt * 128 + 128], wd[:, f, dh * 512:dh * 512 + 512],
                               f == 0, f == 1, sig=(f == 1))
                    o = xtok[:, tt, dh * 512:dh * 512 + 512]
                    e = V.stt(o, PS[b][:, :], comb[:, tt, ei:ei + 1], o, MUL, ADD, p, *cmb_t,
                              (V, V.n) if ei == 0 else moe_prev[tt * 2 + dh])
                    free[b] = [e]
                    if ei == 0 and b == 4:
                        moe_prev = [None] * 4
                    moe_prev[tt * 2 + dh] = e
            hE_r[ei % 2] = p
            ld["done"] = p
        barrier()
        gB = ar(8192, 1024)
        dg = Sem(sem("d_gb"))
        gb_t = L_gb = G.dma(gB, I["final_norm_g"].rearrange("(a n) -> a n", a=1).to_broadcast([128, 1024]), dg)
        jk = ar(6000, 1024)
        for tt in range(2):
            ss = small[:, 32 + tt:33 + tt]
            t = A.act(jk, xtok[:, tt], ACT.Square, *([t] if tt else []), accum=ss)
            tq = rstd(ss, ss, 1024, 1e-6, t)
            xt = V.stt(xtok[:, tt], xtok[:, tt], ss, gB, MUL, MUL, tq, gb_t)
        barrier()

        ang, rk, rq = (rope_[:, 64 * i:64 * i + 64].rearrange("p (f t n) -> p f t n", f=2, t=2) for i in range(3))
        posf = small[:, 36:38]
        t = V.cp(posf, posi[:, :])
        for tt in range(2):
            for f in range(2):
                last = V.ts(ang[:, f, tt], invf, posf[:, tt:tt + 1], None, MUL, None, t)
        fl = lambda x: x.rearrange("p f t n -> p (f t n)")
        MAGIC = 12582912.0
        P1, P2, P3 = 6.28125, 1.9350051879882812e-3, 3.01991598195675e-7
        t = last
        tk_ = []
        for f in range(2):
            t0 = V.ts(rk[:, f], ang[:, f], 1.0 / (2 * math.pi), 0.25 if f == 0 else 0.0, MUL, ADD, t)
            t0 = V.ts(rk[:, f], rk[:, f], MAGIC, MAGIC, ADD, SUB, t0)
            tk_.append(t0)
        t = V.stt(fl(rq), fl(rk), -P1, fl(ang), MUL, ADD, *tk_)
        t = V.stt(fl(rq), fl(rk), -P2, fl(rq), MUL, ADD, t)
        t = V.stt(fl(rq), fl(rk), -P3, fl(rq), MUL, ADD, t)
        t = V.ts(rq[:, 0], rq[:, 0], math.pi / 2, None, ADD, None, t)
        t = V.ts(fl(rq), fl(rq), 3.1415925, -3.1415925, ALU.min, MAX, t)
        rope_t = A.act(fl(ang), fl(rq), ACT.Sin, t)
        cosT, sinT = ang[:, 0], ang[:, 1]

        def ffn(wg_, wu_, wd_, gname, *toks):
            nonlocal xn_t, sg
            hT = ar(0, 5632).rearrange("p (f t) -> p f t", f=22)
            sg = ar(5632, 512).rearrange("p (b t) -> p b t", b=2)
            sg_r[0] = sg_r[1] = None
            xn_t = norm_T(gname, 8192, *toks)
            hv = []
            for f in range(22):
                if f % 3 == 0:
                    n = min(22, f + 3)
                    ld, (wg, wu) = wload(cols(wg_, f * 128, n * 128), cols(wu_, f * 128, n * 128))
                hv.append(gate_up(ld, wg, wu, 128 * (f % 3), f, hT[:, f], None))
                if f % 3 == 2 or f == 21:
                    ld["done"] = (T, T.n)
            T.need(*free[4], *free[5], *free[6], *free[7])
            for k0 in range(0, 22, 6):
                k1 = min(22, k0 + 6)
                ld, (wd,) = wload(rows(wd_, k0, k1))
                T.need(ld["tok"])
                for k in range(k0, k1):
                    T.need(hv[k])
                    for tt in range(2):
                        for dh in range(2):
                            p = mm(PS[4 + 2 * tt + dh][:, :], hT[:, k, tt * 128:tt * 128 + 128],
                                   wd[:, k - k0, dh * 512:dh * 512 + 512], k == 0, k == 21, sig=(tt == 1 and dh == 1))
                ld["done"] = p
            for b in range(4):
                o = xtok[:, b // 2, (b % 2) * 512:(b % 2) * 512 + 512]
                e = V.stt(o, PS[4 + b][:, :], 0.5, o, MUL, ADD, p)
                free[4 + b] = [e]
            barrier()

        def mixer(l):
            nonlocal xn_t
            N = lambda s: f"{s}{l}"
            w = I["w_in_2"][l]
            xn_t = norm_T(N("mix_norm"), 16000)
            zs = ar(0, 2048).rearrange("p (f t) -> p f t", f=8)
            yT = ar(2048, 4096).rearrange("p (f t) -> p f t", f=16)
            qkl = ar(6144, 768).rearrange("p (f t) -> p f t", f=3)
            cc = ar(6912, 1032).rearrange("p (f t) -> p f t", f=4)
            cbg = ar(7944, 1024).rearrange("p (f t) -> p f t", f=4)
            chh = ar(8968, 1024).rearrange("p (f t) -> p f t", f=4)
            dts = ar(9992, 512)
            B0 = 10504
            xb = ar(B0, 3120).rearrange("p (f t) -> p f t", f=12)
            xbc = ar(B0 + 3120, 3072).rearrange("p (f t) -> p f t", f=12)
            xs = ar(B0 + 6192, 2048).rearrange("p (c n) -> p c n", c=2)
            cb = ar(B0 + 8240, 1024).rearrange("p (g s t) -> p g s t", g=2, s=2)
            seg = ar(B0 + 9264, 1536).rearrange("p (b t) -> p b t", b=4)
            Md = ar(B0 + 10800, 1536).rearrange("p (b t) -> p b t", b=4)
            dtr = dts[:, 0:192].rearrange("p (t n) -> p t n", t=2)
            kpe = dts[:, 192:256].rearrange("p (t n) -> p t n", t=2)
            dt = dts[:, 256:320].rearrange("p (t n) -> p t n", t=2)
            dta = dts[:, 320:384].rearrange("p (t n) -> p t n", t=2)
            ncs = dts[:, 384:448].rearrange("p (t n) -> p t n", t=2)
            Ar = dts[:, 448:480]
            tsp = dts[:, 0:64].rearrange("p (t n) -> p t n", t=2)

            pad = [V.set(xb[:, :, 0:2], 0.0), V.set(xb[:, :, 258:260], 0.0), V.set(cc[:, :, 0:1], 0.0), V.set(cc[:, :, 257:258], 0.0)]
            st = {"b": 0}

            def nxt():
                st["b"] += 1
                return 4 + st["b"] % 4

            def pair(ld, wv, c0, c1, last):
                b = nxt()
                proj_T(ld, wv, c0, b, 0, False, *xn_t)
                p = proj_T(ld, wv, c1, b, 1, last)
                return b, p, PS[b][:, :].rearrange("p (f t) -> p f t", f=2)

            conv_t = []
            for blk in range(2):
                ld, (wv,) = wload(cols(w, 1024 + 768 * blk, 1792 + 768 * blk))
                for i in range(3):
                    b, p, v = pair(ld, wv, 256 * i, 256 * i + 128, i == 2)
                    f = 6 * blk + 2 * i
                    e = A.act(xb[:, f:f + 2, 2:258], v, ACT.Copy, p)
                    free[b] = [e]
                    for ff in (f, f + 1):
                        t = V.ts(xbc[:, ff], xb[:, ff, 0:256], pr(N("conv_w"), ff), None, MUL, None, e, *pad)
                        for k in range(1, 5):
                            t = V.stt(xbc[:, ff], xb[:, ff, k:k + 256], pr(N("conv_w"), 12 * k + ff), xbc[:, ff], MUL, ADD, t)
                        conv_t.append(t)
            ld, (wv,) = wload(cols(w, 2560, 3264))
            dt_t, pe_t = [], []
            for tt in range(2):
                b = nxt()
                T.need(ld["tok"], *xn_t, *free[b])
                for c in range(8):
                    mm(PS[b][:, 0:32], xnT[:, c, tt * 128:tt * 128 + 128], wv[:, c, 0:32], c == 0, False)
                for c in range(8):
                    p = mm(PS[b][:, 32:64], xnT[:, c, tt * 128:tt * 128 + 128], wv[:, c, 416:448], False, c == 7, sig=(c == 7))
                r = ROW[N("dt_bias")]
                dt_t.append(V.tt(dt[:, tt], PS[b][:, 0:32], row[:, r:r + 32], ADD, p))
                e = V.cp(kpe[:, tt], PS[b][:, 32:64], p)
                pe_t.append(e)
                free[b] = [e]
            b, p, v = pair(ld, wv, 32, 160, False)
            e = A.act(qkl[:, 0:2], v, ACT.Copy, p)
            free[b] = [e]
            ql_t = [e]
            b = nxt()
            p = proj_T(ld, wv, 288, b, 0, False)
            e = A.act(qkl[:, 2], PS[b][:, 0:256], ACT.Copy, p)
            free[b] = [e]
            ql_t.append(e)
            b, p, v = pair(ld, wv, 448, 576, True)
            ch_t = [A.act(chh[:, 0:2], v, ACT.Copy, p)]
            free[b] = [ch_t[0]]
            ld, (wv,) = wload(cols(w, 3264, 4032))
            b, p, v = pair(ld, wv, 0, 128, False)
            ch_t.append(A.act(chh[:, 2:4], v, ACT.Copy, p))
            free[b] = [ch_t[1]]
            cb_t = []
            for i in range(2):
                b, p, v = pair(ld, wv, 256 + 256 * i, 384 + 256 * i, i == 1)
                e = A.act(cbg[:, 2 * i:2 * i + 2], v, ACT.Copy, p)
                free[b] = [e]
                cb_t.append(e)
            ld, (wv,) = wload(cols(w, 4032, 4544))
            cc_t = []
            for i in range(2):
                b, p, v = pair(ld, wv, 256 * i, 256 * i + 128, i == 1)
                e = V.tt(cc[:, 2 * i:2 * i + 2, 1:257], v, chh[:, 2 * i:2 * i + 2], MUL, p, ch_t[i])
                free[b] = [e]
                cc_t.append(e)
            zs_t = []
            for blk, (a, n) in enumerate(((0, 4), (512, 4))):
                ld, (wv,) = wload(cols(w, a, a + 512))
                for i in range(2):
                    b, p, v = pair(ld, wv, 256 * i, 256 * i + 128, i == 1)
                    e = A.act(zs[:, 4 * blk + 2 * i:4 * blk + 2 * i + 2], v, ACT.Silu, p)
                    free[b] = [e]
                    zs_t.append(e)
            ldm, (wuq, wukv) = wload(rows(I["mla_w_uq_2"][l], 0, 2), rows(I["mla_w_ukv_2"][l], 0, 1))

            cv = []
            for f in range(4):
                t = V.ts(chh[:, f], cc[:, f, 0:256], pr(N("cw"), f), None, MUL, None, cc_t, pad)
                for k in (1, 2):
                    t = V.stt(chh[:, f], cc[:, f, k:k + 256], pr(N("cw"), 4 * k + f), chh[:, f], MUL, ADD, t)
                cv.append(t)
            t = V.tt(chh, chh, cbg, MUL, *cv, *cb_t)
            t = cq = A.act(cbg, chh, ACT.Square, t)
            rc = yT[:, 12:16]
            rg = []
            for half in range(2):
                b = half
                hs2 = slice(2 * half, 2 * half + 2)
                T.need(t, *free[b])
                p = mm(PS[b][:, :], C("bones"), cbg[:, hs2], True, True, sig=True)
                e = V.ts(rc[:, hs2], PS[b][:, :].rearrange("p (f t) -> p f t", f=2), 1.0 / 64, 1e-6, MUL, ADD, p)
                free[b] = [e]
                rg.append(e)
            t = A.act(rc, rc, ACT.Sqrt, *rg)
            t = V.rec(rc, rc, t)
            yc = [V.stt(rc[:, f], chh[:, f], pr(N("conv_out"), f), rc[:, f], MUL, MUL, t) for f in range(4)]

            xb_t = []
            for f in range(12):
                xb_t.append(A.act(xbc[:, f], xbc[:, f], ACT.Silu, conv_t[f], bias=pr(N("conv_b"), f)))
            r = ROW[N("a_log")]
            t = A.act(Ar, row[:, r:r + 32], ACT.Exp)
            ta = V.ts(Ar, Ar, -1.0, None, MUL, None, t)
            t = A.act(tsp, dt, ACT.Abs, *dt_t)
            t = A.act(tsp, tsp, ACT.Exp, t, scale=-1.0)
            t = A.act(tsp, tsp, ACT.Ln, t, bias=1.0)
            td = V.stt(dt, dt, 0.0, tsp, MAX, ADD, t)
            t = V.tt(dta, dt, Ar[:, None, :].to_broadcast([128, 2, 32]), MUL, td, ta)
            b = 2
            T.need(t, *free[b])
            o = lambda tt, d: PS[b][:, 32 * tt + 16 * d:32 * tt + 16 * d + 16]
            f_, k_ = slice(0, 16), slice(16, 32)
            mm(o(0, 0), C("triu"), dta[:, 0, f_], True, False)
            mm(o(1, 0), C("triu"), dta[:, 1, f_], False, False)
            mm(o(1, 0), C("ones"), dta[:, 0, f_], False, False)
            mm(o(0, 1), C("tril"), dta[:, 0, k_], False, False)
            mm(o(0, 1), C("ones"), dta[:, 1, k_], False, False)
            p = mm(o(1, 1), C("tril"), dta[:, 1, k_], False, True, sig=True)
            cs_t = V.ts(ncs, PS[b][:, 0:64].rearrange("p (t n) -> p t n", t=2), 1.0, None, MUL, None, p)
            free[b] = [cs_t]
            xs_t = []
            for tt in range(2):
                for hb in range(2):
                    b = nxt()
                    T.need(*xb_t[0:8], *free[b])
                    for k in range(4):
                        p = tr(PS[b][:, k * 128:k * 128 + 128], xbc[:, hb * 4 + k, tt * 128:tt * 128 + 128], sig=(k == 3))
                    e = A.act(xs[:, tt, hb * 512:hb * 512 + 512], PS[b][:, :], ACT.Copy, p)
                    free[b] = [e]
                    xs_t.append(e)
            cbt = []
            for g in range(2):
                b = nxt()
                T.need(xb_t[8 + g], xb_t[10 + g], *free[b])
                mm(PS[b][:, 0:256], xbc[:, 8 + g, 0:128], xbc[:, 10 + g], True, False)
                p = mm(PS[b][:, 256:512], xbc[:, 8 + g, 128:256], xbc[:, 10 + g], False, True, sig=True)
                e = A.act(cb[:, g], PS[b][:, :].rearrange("p (s t) -> p s t", s=2), ACT.Copy, p)
                free[b] = [e]
                cbt.append(e)
            seg_r, Md_r = [None] * 4, [None] * 4
            ys = []
            it = 0
            for h in range(16):
                g, po = h // 8, 64 * (h % 2)
                mt_ = []
                for d in range(2):
                    hd = 16 * d + h
                    b = it % 4
                    i = it % 4
                    it += 1
                    T.need(*free[b])
                    bc = lambda tt: dta[:, tt, hd:hd + 1].to_broadcast([128, 128])
                    if d == 0:
                        mm(PS[b][:, 0:256], bc(0), cst[:, CN["triu"] * 128:CN["triu"] * 128 + 256], True, False)
                        p = mm(PS[b][:, 128:256], bc(1), C("triu"), False, True, sig=True)
                    else:
                        mm(PS[b][:, 0:256], bc(1), cst[:, CN["ones2"] * 128:CN["ones2"] * 128 + 256], True, False)
                        p = mm(PS[b][:, 0:128], bc(0), C("tril"), False, True, sig=True)
                    sfull, shalf = (0, 1) if d == 0 else (1, 0)
                    mk = C("mnegf") if d == 0 else C("mnegb")
                    dg_ = slice(0, 128) if d == 0 else slice(128, 256)
                    of_ = slice(128, 256) if d == 0 else slice(0, 128)
                    V.stt(seg[:, i, dg_], PS[b][:, dg_], ncs[:, sfull, hd:hd + 1], mk, SUB, ADD, p, cs_t, seg_r[i])
                    V.ts(seg[:, i, of_], PS[b][:, of_], ncs[:, sfull, hd:hd + 1], None, SUB, None)
                    e = V.stt(seg[:, i, 256:384], PS[b][:, of_], ncs[:, shalf, hd:hd + 1], mk, SUB, ADD)
                    free[b] = [e]
                    a = A.act(seg[:, i], seg[:, i], ACT.Exp, e)
                    V.stt(Md[:, i, 0:256], seg[:, i, 0:256], dt[:, sfull, hd:hd + 1], cb[:, g, sfull], MUL, MUL, a, td, cbt[g], Md_r[i])
                    e = V.stt(Md[:, i, 256:384], seg[:, i, 256:384], dt[:, shalf, hd:hd + 1], cb[:, g, shalf, of_], MUL, MUL)
                    seg_r[i] = e
                    mt_.append((i, e))
                ob = 4 + (h // 2) % 4
                T.need(*[e for _, e in mt_], *xs_t)
                if po == 0:
                    T.need(*free[ob])
                O = lambda a, n: PS[ob][po:po + 64, a:a + n]
                hx = slice(h * 64, h * 64 + 64)
                i0, i1 = mt_[0][0], mt_[1][0]
                mm(O(0, 256), xs[:, 0, hx], Md[:, i0, 0:256], True, False)
                mm(O(128, 128), xs[:, 1, hx], Md[:, i0, 256:384], False, False)
                mm(O(0, 256), xs[:, 1, hx], Md[:, i1, 0:256], False, False)
                p = mm(O(0, 128), xs[:, 0, hx], Md[:, i1, 256:384], False, True, sig=True)
                Md_r[i0] = Md_r[i1] = p
                if po:
                    f = h // 2
                    t = V.stt(yT[:, f], xbc[:, f], pr(N("ssd_d"), f), PS[ob][:, 0:256], MUL, ADD, p)
                    free[ob] = [t]
                    ys.append(V.tt(yT[:, f], yT[:, f], zs[:, f], MUL, t, *zs_t))
            sqs = ar(B0, 2048).rearrange("p (f t) -> p f t", f=8)
            t = A.act(sqs, yT[:, 0:8], ACT.Square, *ys)
            rs = ar(B0 + 2048, 512).rearrange("p (g t) -> p g t", g=2)
            T.need(t, *free[0])
            for g in range(2):
                for k in range(4):
                    p = mm(PS[0][:, 256 * g:256 * g + 256], C("ones"), sqs[:, 4 * g + k], k == 0 and g == 0, k == 3 and g == 1, sig=(k == 3))
            e = V.ts(rs, PS[0][:, :].rearrange("p (g t) -> p g t", g=2), 1.0 / 512, 1e-6, MUL, ADD, p, conv_t)
            free[0] = [e]
            t = A.act(rs, rs, ACT.Sqrt, e)
            t = V.rec(rs, rs, t)
            y_t = [V.stt(yT[:, f], yT[:, f], pr(N("ssd_norm"), f), rs[:, f // 4], MUL, MUL, t) for f in range(8)]
            barrier()

            qks = ar(B0, 3072).rearrange("p (t h n) -> p t h n", t=2, h=16)
            kv = ar(B0 + 3072, 2048).rearrange("p (t h n) -> p t h n", t=2, h=8)
            qkT = ar(B0 + 5120, 4096).rearrange("p (h t) -> p h t", h=16)
            Pm = ar(B0 + 9216, 1024).rearrange("p (b k) -> p b k", b=4)
            PT = ar(B0 + 10240, 1024).rearrange("p (b k t) -> p b k t", b=2, k=4)
            om = ar(B0 + 11264, 1024).rearrange("p (t h n) -> p t h n", t=2, h=8)
            tq = ar(B0 + 12288, 1536).rearrange("p (h n) -> p h n", h=16)
            t3 = ar(B0 + 13824, 1536)
            ms_ = small[:, 40:240]
            ql = ar(B0 + 9216, 768).rearrange("p (f t) -> p f t", f=3)
            t = A.act(ql, qkl, ACT.Square, *ql_t)
            gq = [V.ts(qkl[:, f], qkl[:, f], pr(N("q_norm"), f) if f < 2 else pr(N("kv_norm")), None, MUL, None, t) for f in range(3)]
            T.need(t, *free[0])
            for tt in range(2):
                s = slice(128 * tt, 128 * tt + 128)
                mm(PS[0][:, 2 * tt:2 * tt + 1], ql[:, 0, s], C("ones", 1), tt == 0, False)
                mm(PS[0][:, 2 * tt:2 * tt + 1], ql[:, 1, s], C("ones", 1), False, False)
                p = mm(PS[0][:, 2 * tt + 1:2 * tt + 2], ql[:, 2, s], C("ones", 1), False, tt == 1, sig=True)
            lr = ms_[:, 0:4].rearrange("p (t n) -> p t n", t=2)
            pv = PS[0][:, 0:4].rearrange("p (t n) -> p t n", t=2)
            a = V.ts(lr[:, :, 0], pv[:, :, 0], 1.0 / 256, 1e-6, MUL, ADD, p)
            a2 = V.ts(lr[:, :, 1], pv[:, :, 1], 1.0 / 128, 1e-6, MUL, ADD)
            free[0] = [a2]
            t = A.act(ms_[:, 0:4], ms_[:, 0:4], ACT.Sqrt, a, a2)
            lr_t = V.rec(ms_[:, 0:4], ms_[:, 0:4], t)
            T.need(ldm["tok"], *gq)
            qk_t = [[], []]
            for tt in range(2):
                s = slice(128 * tt, 128 * tt + 128)
                for part, (a, n, h0, nh) in enumerate(((0, 480, 0, 5), (480, 288, 5, 3))):
                    b = 1 + part
                    T.need(*free[b])
                    mm(PS[b][:, 0:n], qkl[:, 0, s], wuq[:, 0, a:a + n], True, False)
                    p = mm(PS[b][:, 0:n], qkl[:, 1, s], wuq[:, 1, a:a + n], False, True, sig=True)
                    e = A.act(qks[:, tt, h0:h0 + nh], PS[b][:, 0:n].rearrange("p (h n) -> p h n", n=96), ACT.Copy, p, lr_t, scale=lr[:, tt, 0:1])
                    free[b] = [e]
                    qk_t[tt].append(e)
                for part in range(2):
                    b = 3 + part
                    T.need(*free[b])
                    p = mm(PS[b][:, :], qkl[:, 2, s], wukv[:, 0, part * 512:part * 512 + 512], True, True, sig=True)
                    e = A.act(kv[:, tt, 4 * part:4 * part + 4], PS[b][:, :].rearrange("p (h n) -> p h n", h=4), ACT.Copy, p, lr_t, scale=lr[:, tt, 1:2])
                    free[b] = [e]
                    qk_t[tt].append(e)
            ldm["done"] = p
            kt_ = []
            for tt in range(2):
                t1 = V.cp(qks[:, tt, 8:16, 0:64], kv[:, tt, :, 0:64], *qk_t[tt])
                t2 = V.cp(qks[:, tt, 8:16, 64:96], kpe[:, tt, None, :].to_broadcast([128, 8, 32]), pe_t[tt])
                t = V.tt(tq, qks[:, tt], qks[:, tt], MUL, t1, t2)
                nr = ms_[:, 8 + 16 * tt:24 + 16 * tt]
                t = V.red(nr, tq, ADD, t)
                t = rstd(nr, nr, 96, 1e-6, t)
                t = V.tt(qks[:, tt], qks[:, tt], nr[:, :, None].to_broadcast([128, 16, 96]), MUL, t)
                r = ROW[N("qk_g")]
                for half in range(2):
                    gb = row[:, r + 96 * half:r + 96 * half + 96][:, None, :].to_broadcast([128, 8, 96])
                    t = V.tt(qks[:, tt, 8 * half:8 * half + 8], qks[:, tt, 8 * half:8 * half + 8], gb, MUL, t)
                x1, x2 = qks[:, tt, :, 64:80], qks[:, tt, :, 80:96]
                cB = cosT[:, tt, None, :].to_broadcast([128, 16, 16])
                sB = sinT[:, tt, None, :].to_broadcast([128, 16, 16])
                m = [t3[:, 256 * i:256 * i + 256].rearrange("p (h n) -> p h n", h=16) for i in range(4)]
                a0 = V.tt(m[0], x1, cB, MUL, t, rope_t)
                a1 = V.tt(m[1], x2, sB, MUL)
                a2 = V.tt(m[2], x1, sB, MUL)
                a3 = V.tt(m[3], x2, cB, MUL)
                a1 = V.tt(x1, m[0], m[1], SUB, a3)
                a3 = V.tt(x2, m[2], m[3], ADD)
                for q4 in range(4):
                    b = 4 + q4
                    T.need(a3, *free[b])
                    for k in range(4):
                        p = tr(PS[b][0:96, k * 128:k * 128 + 128], qks[:, tt, 4 * q4 + k], sig=(k == 3))
                    e = A.act(qkT[0:96, 4 * q4:4 * q4 + 4, 128 * tt:128 * tt + 128], PS[b][0:96, :].rearrange("p (h t) -> p h t", h=4), ACT.Copy, p)
                    free[b] = [e]
                    kt_.append(e)
            mx, sm = ms_[:, 40:56], ms_[:, 56:72]
            P_r, PT_r = [None] * 4, [None] * 2
            scl = 96.0 ** -0.5
            pv_t = []
            for h in range(8):
                b = h % 2
                T.need(*kt_, *free[b])
                for tt in range(2):
                    p = mm(PS[b][:, 256 * tt:256 * tt + 256], qkT[0:96, h, 128 * tt:128 * tt + 128], qkT[0:96, 8 + h], tt == 0, tt == 1, sig=(tt == 1))
                t = V.op(lambda e, b=b, h=h: e.tensor_reduce(mx[:, 2 * h:2 * h + 2], PS[b][:, :].rearrange("p (t k) -> p t k", t=2), AX.X, MAX), p)
                t = V.ts(mx[:, 2 * h:2 * h + 2], mx[:, 2 * h:2 * h + 2], -scl, None, MUL, None, t)
                for tt in range(2):
                    i = (2 * h + tt) % 4
                    a = A.act(Pm[:, i], PS[b][:, 256 * tt:256 * tt + 256], ACT.Exp, t, P_r[i],
                              bias=mx[:, 2 * h + tt:2 * h + tt + 1], scale=scl, accum=sm[:, 2 * h + tt:2 * h + tt + 1])
                free[b] = [a]
                b = 2 + h % 2
                T.need(a, *free[b])
                for tt in range(2):
                    for ks in range(2):
                        p = tr(PS[b][:, (2 * tt + ks) * 128:(2 * tt + ks) * 128 + 128], Pm[:, (2 * h + tt) % 4, ks * 128:ks * 128 + 128], sig=True)
                P_r[(2 * h) % 4] = P_r[(2 * h + 1) % 4] = p
                e = V.cp(PT[:, h % 2], PS[b][:, :].rearrange("p (k t) -> p k t", k=4), p, PT_r[h % 2])
                free[b] = [e]
                for tt in range(2):
                    T.need(e)
                    if h == 0:
                        T.need(*free[4 + tt])
                    for ks in range(2):
                        p = mm(PS[4 + tt][:, h * 64:h * 64 + 64], PT[:, h % 2, 2 * tt + ks], kv[:, ks, h, 64:128], h == 0 and ks == 0, h == 7 and ks == 1, sig=True)
                PT_r[h % 2] = p
            t = V.rec(sm, sm, a)
            smv = sm.rearrange("p (h t) -> p h t", t=2)
            mla_t = []
            for tt in range(2):
                o = V.tt(om[:, tt], PS[4 + tt][:, :].rearrange("p (h n) -> p h n", h=8), smv[:, :, tt:tt + 1].to_broadcast([128, 8, 64]), MUL, p, t)
                free[4 + tt] = [o]
                q8 = tq[:, 0:8, 0:64]
                a = V.tt(q8, om[:, tt], om[:, tt], MUL, o)
                nr = ms_[:, 80 + 8 * tt:88 + 8 * tt]
                a = V.red(nr, q8, ADD, a)
                a = rstd(nr, nr, 64, 1e-6, a)
                a = V.tt(om[:, tt], om[:, tt], nr[:, :, None].to_broadcast([128, 8, 64]), MUL, a)
                b = 6 + tt
                T.need(a, *free[b])
                fo = om[:, tt].rearrange("p h n -> p (h n)")
                for k in range(4):
                    p2 = tr(PS[b][:, k * 128:k * 128 + 128], fo[:, k * 128:k * 128 + 128], sig=(k == 3))
                for k in range(4):
                    e = A.act(yT[:, 8 + k, 128 * tt:128 * tt + 128], PS[b][:, k * 128:k * 128 + 128], ACT.Copy, p2, scale=pr(N("out_norm"), k))
                free[b] = [e]
                mla_t.append(e)
            lds = [wload(rows(I["w_out_2"][l], a, min(16, a + 6))) for a in (0, 6, 12)]
            out_proj(yT, 16, [(a, b[0]) for a, b in lds], *mla_t, *y_t, *yc)
            barrier()

        nl = 2 if dbg is None or not isinstance(dbg, tuple) else 0
        for l in range(nl):
            ffn(I["ffn1_w_gate_2"][l], I["ffn1_w_up_2"][l], I["ffn1_w_down_2"][l], f"ffn1_norm{l}")
            mixer(l)
            ffn(I["ffn2_w_gate_2"][l], I["ffn2_w_up_2"][l], I["ffn2_w_down_2"][l], f"ffn2_norm{l}")

        for n, ld in enumerate(loads):
            if n >= NR:
                L.need(loads[n - NR]["done"])
            for dst, src in ld["dmas"]:
                L.items.append((lambda e, dst=dst, src=src: e.dma_start(dst, src), ld["sem"].sem, 16))
        done = L.dma(out.rearrange("(t p) d -> p t d", p=128), xtok, dout, (V, V.n))
        L.need(done)

        block = ctx.enter_context(nc.Block())

        @block.sync
        def _(e):
            L.emit(e)

        @block.tensor
        def _(e):
            T.emit(e)

        @block.vector
        def _(e):
            V.emit(e)

        @block.scalar
        def _(e):
            A.emit(e)

        @block.gpsimd
        def _(e):
            G.emit(e)


_BIG = ["w_in", "rw_g2", "w_out", "exp_w_gate", "exp_w_up", "exp_w_down", "final_norm_g"]
_BIG2 = ["ffn1_w_gate_2", "ffn1_w_up_2", "ffn1_w_down_2", "w_in_2", "mla_w_uq_2", "mla_w_ukv_2", "w_out_2",
         "ffn2_w_gate_2", "ffn2_w_up_2", "ffn2_w_down_2"]


def layout(inputs):
    a = {n: np.ascontiguousarray(inputs[n]) for n in _BIG + _BIG2}
    f = {n: np.asarray(v) for n, v in inputs.items()}
    a["x"] = np.ascontiguousarray(f["x"][0])
    a["positions"] = np.ascontiguousarray(f["positions_2"].reshape(2, 128).T)
    a["w2a2"] = np.concatenate([f["rw_w2"][0], f["rw_a2"][0]], axis=0)
    a["router"] = np.ascontiguousarray(
        np.concatenate([f["router_grp_w"][0], f["router_exp_w"][0]], axis=1).reshape(8, 128, 36).transpose(1, 0, 2).reshape(128, 288))
    c = lambda v: np.asarray(v).reshape(-1, 128).T
    parts = [c(f[n][0]) for n in ("norm_mix_g", "shift_mu", "sb_out_g", "rw_w0", "rw_a0", "rw_k_k", "rw_k_a", "rw_r_k",
                                  "rw_ln_w", "rw_ln_b", "norm_ffn_g")]
    for l in range(2):
        parts += [c(f["ffn1_norm_2"][l]), c(f["mix_norm_2"][l]), c(f["ssd_conv_w_2"][l]), c(f["ssd_conv_b_2"][l]),
                  c(f["ssd_norm_2"][l]), c(np.repeat(f["ssd_d_2"][l], 64)), c(f["mla_q_norm_2"][l]), c(f["mla_kv_norm_2"][l]),
                  c(f["mla_out_norm_2"][l]), c(f["conv_w_2"][l]), c(f["conv_out_norm_2"][l]), c(f["ffn2_norm_2"][l])]
    a["prm"] = np.ascontiguousarray(np.concatenate(parts, axis=1))
    rows_ = [f["router_grp_b"][0], f["router_exp_b"][0]]
    for l in range(2):
        rows_ += [f["ssd_dt_bias_2"][l].reshape(-1), f["ssd_a_log_2"][l].reshape(-1), f["mla_q_head_norm_2"][l], f["mla_k_head_norm_2"][l]]
    a["rowp"] = np.ascontiguousarray(np.broadcast_to(np.concatenate(rows_)[None], (128, NROW)))
    a["cst"] = constants()
    return a


def kernel(**inputs):
    import concourse.bacc as bacc
    from concourse.bass_utils import run_bass_kernel_spmd

    nc = bacc.Bacc("TRN2", target_bir_lowering=False, num_devices=1)
    arrays = {f"in_{n}": v for n, v in layout(inputs).items()}
    aps = {n[3:]: nc.dram_tensor(n, v.shape, mybir.dt.from_np(v.dtype), kind="ExternalInput").ap() for n, v in arrays.items()}
    out = nc.dram_tensor("out_0", (256, 1024), F32, kind="ExternalOutput").ap()
    program(nc, aps, out)
    r = run_bass_kernel_spmd(nc, [arrays], core_ids=[0])
    return r.results[0]["out_0"].reshape(1, 256, 1024)
```

```python
import math
from contextlib import ExitStack

import numpy as np

import concourse.bass as bass
from concourse import mybir

ALU = mybir.AluOpType
ACT = mybir.ActivationFunctionType
F32 = mybir.dt.float32
F32R = mybir.dt.float32r
I32 = mybir.dt.int32
AX = mybir.AxisListType

NR = 4
NS = 2
SLOT = 2048
DVE_PART = 1280
ARENA = 26000
BIG = 1.0e30
KAP = math.exp(-0.5)
LEVELS = [1, 2, 4, 8, 16, 32, 64]

CN = {n: i for i, n in enumerate(
    ["ident", "ones", "bones", "ntri", "nones", "mnegs", "triu", "ones2", "tril", "mnegf", "mnegb", "ms"]
    + [f"lv{m}" for m in LEVELS])}


def constants():
    s = np.arange(128)[:, None]
    t = np.arange(128)[None, :]
    f = lambda c: c.astype(np.float32)
    tiles = {
        "ident": f(s == t), "ones": np.ones((128, 128), np.float32), "bones": f(s // 64 == t // 64),
        "ntri": -f(s >= t), "nones": -np.ones((128, 128), np.float32), "mnegs": -BIG * f(s >= t),
        "triu": f(s <= t), "ones2": np.ones((128, 128), np.float32), "tril": f(s >= t),
        "mnegf": -BIG * f(s > t), "mnegb": -BIG * f(s < t), "ms": f(s < t),
    }
    for m in LEVELS:
        tiles[f"lv{m}"] = f((s // (2 * m) == t // (2 * m)) & (s % (2 * m) < m) & (t % (2 * m) >= m))
    inv = (10000.0 ** (-np.arange(16, dtype=np.float64) / 16)).astype(np.float32)
    return np.concatenate([tiles[n].astype(np.float32) for n in CN] + [np.tile(inv[None], (128, 1))], axis=1)


PRM = {}
_n = 0
for _name, _k in ([("norm_mix_g", 8), ("shift_mu", 14), ("sb_out_g", 4), ("w0", 4), ("a0", 4), ("k_k", 4), ("k_a", 4),
                   ("r_k", 4), ("ln_w", 4), ("ln_b", 4), ("norm_ffn_g", 8)]
                  + [(f"{a}{l}", b) for l in range(2) for a, b in (
                      ("ffn1_norm", 8), ("mix_norm", 8), ("conv_w", 60), ("conv_b", 12), ("ssd_norm", 8), ("ssd_d", 8),
                      ("q_norm", 2), ("kv_norm", 1), ("out_norm", 4), ("cw", 12), ("conv_out", 4), ("ffn2_norm", 8))]):
    PRM[_name] = _n
    _n += _k
NPRM = _n
ROW = {"router_b": 0}
for _l in range(2):
    ROW.update({f"dt_bias{_l}": 36 + 256 * _l, f"a_log{_l}": 68 + 256 * _l, f"qk_g{_l}": 100 + 256 * _l})
NROW = 36 + 512


class Sem:

    def __init__(self, sem):
        self.sem, self.n = sem, 0


class Queue(Sem):

    def __init__(self, sem):
        super().__init__(sem)
        self.items, self.seen = [], {}

    def need(self, *toks):
        for t in toks:
            if t is None:
                continue
            if isinstance(t, list):
                self.need(*t)
                continue
            s, v = t
            if self.seen.get(s, 0) < v:
                self.seen[s] = v
                self.items.append((s.sem, v))

    def raw(self, fn, *toks):
        self.need(*toks)
        self.items.append((fn, None, 0))

    def op(self, fn, *toks):
        self.need(*toks)
        self.n += 1
        self.items.append((fn, self.sem, 1))
        return (self, self.n)

    def dma(self, out, in_, sem, *toks):
        self.need(*toks)
        sem.n += 16
        self.items.append((lambda e: e.dma_start(out, in_), sem.sem, 16))
        return (sem, sem.n)

    def emit(self, e):
        for it in self.items:
            if len(it) == 2:
                e.wait_ge(it[0], it[1])
            else:
                ins = it[0](e)
                if it[1] is not None:
                    ins.then_inc(it[1], it[2])

    def tt(self, out, a, b, op, *toks):
        return self.op(lambda e: e.tensor_tensor(out, a, b, op), *toks)

    def ts(self, out, a, s1, s2, op0, op1, *toks):
        if s2 is None:
            return self.op(lambda e: e.tensor_scalar(out, a, s1, None, op0), *toks)
        return self.op(lambda e: e.tensor_scalar(out, a, s1, s2, op0, op1), *toks)

    def stt(self, out, a, s, b, op0, op1, *toks):
        return self.op(lambda e: e.scalar_tensor_tensor(out=out, in0=a, scalar=s, in1=b, op0=op0, op1=op1), *toks)

    def cp(self, out, a, *toks):
        return self.op(lambda e: e.tensor_copy(out, a), *toks)

    def rec(self, out, a, *toks):
        return self.op(lambda e: e.reciprocal(out, a), *toks)

    def red(self, out, a, op, *toks):
        return self.op(lambda e: e.tensor_reduce(out, a, AX.X, op), *toks)

    def set(self, out, v, *toks):
        return self.op(lambda e: e.memset(out, v), *toks)

    def act(self, out, a, func, *toks, bias=None, scale=1.0, accum=None):
        kw = {"scale": scale}
        if bias is not None:
            kw["bias"] = bias
        if accum is not None:
            kw["accum_out"] = accum
        return self.op(lambda e: e.activation(out, a, func, **kw), *toks)


def program(nc, I, out):
    MUL, ADD, SUB, MAX = ALU.mult, ALU.add, ALU.subtract, ALU.max
    with ExitStack() as ctx:
        def sb(name, n, dt=F32):
            return ctx.enter_context(nc.sbuf_tensor(name, [128, n], dt))

        def sem(name):
            return ctx.enter_context(nc.semaphore(name))

        ring = sb("ring", NR * SLOT)
        xtok_ = sb("xtok", 2048)
        rhi = sb("rhi", NS * SLOT, F32R)
        rlo = sb("rlo", NS * SLOT, F32R)
        xnh_ = sb("xnh", 2048, F32R)
        xnl_ = sb("xnl", 2048, F32R)
        cst = sb("cst", len(CN) * 128 + 16)
        prm = sb("prm", NPRM)
        row = sb("row", NROW)
        small = sb("small", 256)
        comb_ = sb("comb", 64)
        rope_ = sb("rope", 192)
        posi = sb("posi", 2, I32)
        with nc.sbuf_tensor("arena", [128, ARENA], F32) as arena:
            pass
        hhi_ = sb("hhi", 5632, F32R)
        hlo_ = sb("hlo", 5632, F32R)
        sg_ = sb("sg", 1024)
        hf_ = sb("hf", 1024)
        xnt_ = sb("xnt", 2048)
        ftmp = sb("ftmp", 2048)
        PS = [ctx.enter_context(nc.psum_tensor(f"ps{i}", [128, 512], F32)) for i in range(8)]
        xtok = xtok_[:, :].rearrange("p (t d) -> p t d", t=2)
        xnh, xnl = (x[:, :].rearrange("p (c t) -> p c t", c=8) for x in (xnh_, xnl_))
        f32 = lambda v: v.bitcast(F32)

        T, V, A, G, L = (Queue(sem(f"s_{n}")) for n in ("pe", "dve", "act", "pool", "sp"))
        d0 = Sem(sem("d_first"))
        dslot = [Sem(sem(f"d_slot{i}")) for i in range(NR)]
        dout = Sem(sem("d_out"))
        free = [[] for _ in range(8)]

        def C(name, n=128):
            return cst[:, CN[name] * 128:CN[name] * 128 + n]

        invf = cst[:, len(CN) * 128:len(CN) * 128 + 16]

        def pr(name, i=0, n=1):
            return prm[:, PRM[name] + i:PRM[name] + i + n]

        def ar(o, n):
            assert o + n <= ARENA, (o, n)
            return arena[:, o:o + n]

        def cols(w, a, b):
            return w.rearrange("(c p) n -> p c n", p=128)[:, :, a:b]

        def rows(w, a, b):
            return w.rearrange("(c p) n -> p c n", p=128)[:, a:b, :]

        loads = []

        def plan(*parts, split=True):
            n = len(loads)
            s = n % NR
            off, shapes, dmas = 0, [], []
            for src in parts:
                k, a, b = src.shape
                dmas.append((ring[0:k, s * SLOT + off:s * SLOT + off + a * b].rearrange("p (a b) -> p a b", a=a), src))
                shapes.append((off, a, b))
                off += a * b
            assert off <= SLOT
            dslot[s].n += 16 * len(parts)
            loads.append({"dmas": dmas, "sem": dslot[s], "tok": (dslot[s], dslot[s].n), "raw_done": None,
                          "split": split, "shapes": shapes, "n": off, "at": n, "done": None, "ready": None})

        w_in = I["w_in"][0]
        for a in [3072] + list(range(1536, 3072, 256)) + list(range(0, 1536, 256)):
            plan(cols(w_in, a, a + 256))
        for a in range(0, 8, 2):
            plan(rows(I["w_out"][0], a, a + 2))
        plan(I["router"].rearrange("p (c n) -> p c n", c=8))
        for e in range(33):
            if e < 32:
                plan(cols(I["exp_w_gate"][0, e], 0, 256))
                plan(cols(I["exp_w_up"][0, e], 0, 256))
            if e:
                plan(rows(I["exp_w_down"][0, e - 1], 0, 2))

        def plan_ffn(wg_, wu_, wd_):
            for a in range(0, 2816, 256):
                plan(cols(wg_, a, a + 256))
                plan(cols(wu_, a, a + 256))
            for a in range(0, 22, 2):
                plan(rows(wd_, a, a + 2))

        for l in range(2):
            plan_ffn(I["ffn1_w_gate_2"][l], I["ffn1_w_up_2"][l], I["ffn1_w_down_2"][l])
            w = I["w_in_2"][l]
            for a in range(1024, 2560, 256):
                plan(cols(w, a, a + 256))
            plan(cols(w, 2592, 2848))
            plan(cols(w, 2848, 2976), cols(w, 2560, 2592), cols(w, 2976, 3008))
            for a in list(range(3008, 4544, 256)) + list(range(0, 1024, 256)):
                plan(cols(w, a, a + 256))
            plan(rows(I["mla_w_uq_2"][l], 0, 2), split=False)
            plan(rows(I["mla_w_ukv_2"][l], 0, 1), split=False)
            for a in range(0, 16, 2):
                plan(rows(I["w_out_2"][l], a, a + 2), split=False)
            plan_ffn(I["ffn2_w_gate_2"][l], I["ffn2_w_up_2"][l], I["ffn2_w_down_2"][l])

        split_loads = [x for x in loads if x["split"]]

        def prepare(n):
            if n >= len(loads) or not loads[n]["split"] or loads[n]["ready"]:
                return
            k = split_loads.index(loads[n])
            ld = split_loads[k]
            n, o, s = ld["n"], k % NS * SLOT, ld["at"] % NR * SLOT
            before = split_loads[k - NS]["done"] if k >= NS else None
            toks, mid = [], min(n, DVE_PART)
            for a, b in ((0, mid), (mid, n)):
                if a == b:
                    continue
                hi, lo, raw = rhi[:, o + a:o + b], rlo[:, o + a:o + b], ring[:, s + a:s + b]
                t = A.act(hi, raw, ACT.Copy, ld["tok"], before)
                q = G if a else V
                toks += [t, q.tt(lo, raw, f32(hi), ALU.subtract, t, ld["tok"], before)]
            ld["ready"] = ld["raw_done"] = toks
            ld["hi"] = [rhi[:, o + a:o + a + x * y].rearrange("p (a b) -> p a b", a=x) for a, x, y in ld["shapes"]]
            ld["lo"] = [rlo[:, o + a:o + a + x * y].rearrange("p (a b) -> p a b", a=x) for a, x, y in ld["shapes"]]

        turn = {"n": 0}

        def take():
            n = turn["n"]
            turn["n"] += 1
            prepare(n)
            prepare(n + 1)
            T.need(loads[n]["ready"] if loads[n]["split"] else loads[n]["tok"])
            return loads[n]

        def done(ld, p):
            ld["done"] = p
            if not ld["split"]:
                ld["raw_done"] = p

        def mm(out_, lhsT, rhs, start, stop, *toks, sig=False):
            fn = lambda e: e.matmul(out_, lhsT, rhs, start=start, stop=stop, skip_group_check=True)
            if sig:
                return T.op(fn, *toks)
            T.raw(fn, *toks)
            return None

        def tr(out_, in_, *toks, sig=False):
            idn = C("ident")[0:in_.shape[0], 0:in_.shape[0]]
            fn = lambda e: e.transpose(out_, in_, idn)
            if sig:
                return T.op(fn, *toks)
            T.raw(fn, *toks)
            return None

        def barrier():
            every = [(q, q.n) for q in (T, V, A, G) if q.n]
            for q in (T, V, A, G):
                q.need(*every)

        first = [L.dma(xtok, I["x"].rearrange("(t p) d -> p t d", p=128), d0),
                 L.dma(cst[:, :], I["cst"], d0), L.dma(prm[:, :], I["prm"], d0), L.dma(row[:, :], I["rowp"], d0),
                 L.dma(posi[:, :], I["positions"], d0)][-1:]
        for q in (T, V, A, G):
            q.need(*first)

        def rstd(out_, ssq, n, eps, *toks):
            t = V.ts(out_, ssq, 1.0 / n, eps, MUL, ADD, *toks)
            t = A.act(out_, out_, ACT.Sqrt, t)
            return V.rec(out_, out_, t)

        def norm_T(gname, xn_, *toks):
            xn = xn_.rearrange("p (t d) -> p t d", t=2)
            res = []
            for tt in range(2):
                ss = small[:, tt:tt + 1]
                t = A.act(xn[:, tt], xtok[:, tt], ACT.Square, *toks, accum=ss)
                t = rstd(ss, ss, 1024, 1e-6, t)
                t = V.ts(xn[:, tt], xtok[:, tt], ss, None, MUL, None, t)
                for hb in range(2):
                    b = tt * 2 + hb
                    T.need(t, *free[b])
                    for k in range(4):
                        c = hb * 4 + k
                        p = tr(PS[b][:, k * 128:k * 128 + 128], xn[:, tt, c * 128:c * 128 + 128], sig=(k == 3))
                    for k in range(4):
                        c = hb * 4 + k
                        o, i, g = xnh[:, c, tt * 128:tt * 128 + 128], PS[b][:, k * 128:k * 128 + 128], pr(gname, c)
                        eh = A.act(o, i, ACT.Copy, p, scale=g)
                    for k in range(4):
                        c = hb * 4 + k
                        s = slice(tt * 128, tt * 128 + 128)
                        e = V.stt(xnl[:, c, s], PS[b][:, k * 128:k * 128 + 128], pr(gname, c), f32(xnh[:, c, s]), MUL, SUB, eh)
                    free[b] = [e]
                    res += [eh, e]
            return res

        def mm3(out_, lh, ll, rh, rl, start, stop, sig=False):
            mm(out_, lh, rh, start, False)
            mm(out_, lh, rl, False, False)
            return mm(out_, ll, rh, False, stop, sig=sig)

        def proj_T(ld, c0, bank, half, last, *toks, part=0):
            T.need(*toks)
            if half == 0:
                T.need(*free[bank])
            wh, wl = ld["hi"][part], ld["lo"][part]
            for c in range(8):
                p = mm3(PS[bank][:, half * 256:half * 256 + 256], wh[:, c, c0:c0 + 128], wl[:, c, c0:c0 + 128],
                        xnh[:, c, :], xnl[:, c, :], c == 0, c == 7, sig=(c == 7))
            if last:
                done(ld, p)
            return p

        def proj_tok(o, ld, part, tt, a, n, first, stop):
            s = slice(128 * tt, 128 * tt + 128)
            for c in range(8):
                p = mm3(o, xnh[:, c, s], xnl[:, c, s], ld["hi"][part][:, c, a:a + n], ld["lo"][part][:, c, a:a + n],
                        first and c == 0, stop and c == 7, sig=(c == 7))
            return p

        def down(ld, k0, nk, hh, hl, k_of=lambda k: k, needs=None):
            for i in range(2):
                k = k0 + i
                if needs:
                    T.need(*needs[k])
                for tt in range(2):
                    s = slice(128 * tt, 128 * tt + 128)
                    for dh in range(2):
                        d = slice(512 * dh, 512 * dh + 512)
                        p = mm3(PS[4 + 2 * tt + dh][:, :], hh[:, k_of(k), s], hl[:, k_of(k), s], ld["hi"][0][:, i, d], ld["lo"][0][:, i, d],
                                k == 0, k == nk - 1, sig=True)
            done(ld, p)
            return p

        def parts_of(hi, lo, v, *toks):
            t = A.act(hi, v, ACT.Copy, *toks)
            return [t, V.tt(lo, v, f32(hi), SUB, t)]

        def add_x(p, scale=1.0):
            res = []
            for b in range(4):
                o = xtok[:, b // 2, (b % 2) * 512:(b % 2) * 512 + 512]
                e = V.stt(o, PS[4 + b][:, :], scale, o, MUL, ADD, p)
                free[4 + b] = [e]
                res.append(e)
            return res

        wl2, wg2 = ar(18468, 512)[:, None, :], ar(18980, 512)[:, None, :]
        dlo = Sem(sem("d_lora"))
        L.dma(wl2[:, 0], I["w2a2"], dlo)
        lora_t = L.dma(wg2[:, 0], I["rw_g2"][0], dlo)
        xn_t = norm_T("norm_mix_g", ar(8212, 2048))

        urw = ar(0, 3598).rearrange("p (f t) -> p f t", f=14)
        um = ar(3600, 3584).rearrange("p (f t) -> p f t", f=14)
        Cc = ar(7184, 1028).rearrange("p (f t) -> p f t", f=4)
        EP = ar(8212, 1032).rearrange("p (f c t) -> p f c t", f=4, c=2)
        EN = ar(9244, 1032).rearrange("p (f c t) -> p f c t", f=4, c=2)
        v4 = lambda o: ar(o, 1024).rearrange("p (f t) -> p f t", f=4)
        aT, kkT, rT, zT, bT, kT, gT = (v4(o) for o in (10276, 11300, 12324, 13348, 14372, 15396, 16420))
        Vtok = ar(17444, 1024).rearrange("p (c n) -> p c n", c=2)
        BK = ar(18468, 1024).rearrange("p (c n) -> p c n", c=2)
        AT = ar(19492, 2048).rearrange("p (q t) -> p q t", q=16)
        X = ar(21540, 2048).rearrange("p (q t) -> p q t", q=16)
        XT = ar(23588, 2048).rearrange("p (q t) -> p q t", q=16)
        Y = ar(0, 2048).rearrange("p (q t) -> p q t", q=16)
        M = ar(2048, 1536).rearrange("p (b q t) -> p b q t", b=3, q=4)
        tmp = [v4(0), v4(1024), v4(2048)]
        qk = ar(19492, 2048).rearrange("p (f t) -> p f t", f=8)
        vtok = ar(21540, 1024).rearrange("p (c n) -> p c n", c=2)
        sbe = ar(22564, 1152).rearrange("p (b t) -> p b t", b=3)
        sbs = ar(23716, 1152).rearrange("p (b t) -> p b t", b=3)
        sbo = ar(24868, 1024).rearrange("p (f t) -> p f t", f=4)

        z0 = V.set(urw[:, :, 0:1], 0.0)
        um_t = [None] * 14
        nb = 0
        for f in [12, 0, 2, 4, 6, 8, 10]:
            ld = take()
            b = 4 + nb % 4
            nb += 1
            proj_T(ld, 0, b, 0, False, *xn_t)
            p = proj_T(ld, 128, b, 1, True)
            e = A.act(urw[:, f:f + 2, 1:257], PS[b][:, :].rearrange("p (f t) -> p f t", f=2), ACT.Copy, p)
            free[b] = [e]
            for ff in (f, f + 1):
                t = G.tt(um[:, ff], urw[:, ff, 0:256], urw[:, ff, 1:257], SUB, e, z0)
                um_t[ff] = V.stt(um[:, ff], um[:, ff], pr("shift_mu", ff), urw[:, ff, 1:257], MUL, ADD, t)
        qk_t = [None] * 8
        for f in range(0, 8, 2):
            ld = take()
            b = 4 + nb % 4
            nb += 1
            proj_T(ld, 0, b, 0, False)
            p = proj_T(ld, 128, b, 1, True)
            e = A.act(qk[:, f:f + 2, :], PS[b][:, :].rearrange("p (f t) -> p f t", f=2), ACT.Copy, p,
                      scale=0.125 if f < 4 else 1.0)
            free[b] = [e]
            qk_t[f] = qk_t[f + 1] = e
        vt_t = []
        for half in range(2):
            ld = take()
            b = 4 + nb % 4
            nb += 1
            T.need(*free[b])
            for tt in range(2):
                p = proj_tok(PS[b][:, 256 * tt:256 * tt + 256], ld, 0, tt, 0, 256, tt == 0, tt == 1)
            e = A.act(vtok[:, :, 256 * half:256 * half + 256], PS[b][:, :].rearrange("p (t n) -> p t n", t=2), ACT.Copy, p)
            vt_t.append(e)
            free[b] = [e]
            done(ld, p)
        xn_free = p

        T.need(lora_t)
        th = tmp[0][:, 0]
        t = A.act(th[0:64], um[0:64, 12], ACT.Tanh, *um_t)
        n0 = V.ts(small[:, 8:16], prm[:, PRM["w0"]:PRM["w0"] + 8], -1.0, None, MUL, None)
        sgx = tmp[0][:, 1]
        e1 = A.act(sgx, um[:, 13], ACT.Exp, scale=-1.0)
        e1 = V.ts(sgx, sgx, 1.0, None, ADD, None, e1)
        e1 = V.rec(sgx, sgx, e1)
        lor = []
        for half in range(2):
            b = half
            T.need(t, *free[b])
            for k in range(2):
                f = half * 2 + k
                p = mm(PS[b][:, k * 256:k * 256 + 256], wl2[0:64, 0, f * 128:f * 128 + 128], th[0:64], True, True, sig=(k == 1))
            for k in range(2):
                f = half * 2 + k
                e = A.act(tmp[1][:, f], PS[b][:, k * 256:k * 256 + 256], ACT.Exp, p, n0, scale=-1.0, bias=small[:, 8 + f:9 + f])
            free[b] = [e]
            lor.append(e)
        for half in range(2):
            b = 2 + half
            T.need(*free[b])
            for k in range(2):
                f = half * 2 + k
                p = mm(PS[b][:, k * 256:k * 256 + 256], wl2[64:128, 0, f * 128:f * 128 + 128], um[64:128, 12], True, True, sig=(k == 1))
            for k in range(2):
                f = half * 2 + k
                e = A.act(aT[:, f], PS[b][:, k * 256:k * 256 + 256], ACT.Exp, p, scale=-1.0, bias=small[:, 12 + f:13 + f])
            free[b] = [e]
        at = V.ts(aT, aT, 1.0, None, ADD, None, e)
        at = V.rec(aT, aT, at)
        gt = []
        for half in range(2):
            b = half
            T.need(e1, *free[b])
            for k in range(2):
                f = half * 2 + k
                p = mm(PS[b][:, k * 256:k * 256 + 256], wg2[:, 0, f * 128:f * 128 + 128], sgx, True, True, sig=(k == 1))
            e = A.act(gT[:, 2 * half:2 * half + 2, :], PS[b][:, :].rearrange("p (f t) -> p f t", f=2), ACT.Copy, p)
            free[b] = [e]
            gt.append(e)
        lora_done = p
        lw = V.ts(tmp[1], tmp[1], 1.0, None, ADD, None, *lor)
        lw = V.rec(tmp[1], tmp[1], lw)
        c0 = V.set(Cc[:, :, 0:1], 0.0)
        one = C("ones", 128)
        ct = []
        on256 = V.set(tmp[2][:, 0], 1.0, *um_t)
        for f in range(4):
            ct.append(V.op(lambda e, f=f: e.tensor_tensor_scan(Cc[:, f, 1:257], tmp[2][:, 0], tmp[1][:, f], 0.0, MUL, ADD), lw, on256))
        dt_ = []
        for c in range(2):
            cm = Cc[:, :, 64 + 128 * c:65 + 128 * c].to_broadcast([128, 4, 129])
            dt_.append(V.tt(EP[:, :, c, :], Cc[:, :, 128 * c:128 * c + 129], cm, SUB, *ct, c0, xn_free))
        en = A.act(EN, EP, ACT.Exp, *dt_, scale=KAP)
        ep = A.act(EP, EP, ACT.Exp, en, scale=-KAP)
        sct = V.tt(small[:, 16:20], Cc[:, :, 192:193].rearrange("p f a -> p (f a)"), Cc[:, :, 64:65].rearrange("p f a -> p (f a)"), SUB, *ct)
        sct = A.act(small[:, 16:20], small[:, 16:20], ACT.Exp, sct, scale=-KAP)

        kkr = []
        for f in range(4):
            kkr.append(V.ts(kkT[:, f], um[:, 4 + f], pr("k_k", f), None, MUL, None))
        sq = A.act(tmp[2], kkT, ACT.Square, *kkr, *ct)
        kn = []
        for half in range(2):
            b = 2 + half
            T.need(sq, *free[b])
            p = mm(PS[b][:, :], C("bones"), tmp[2][:, 2 * half:2 * half + 2], True, True, sig=True)
            e = V.ts(tmp[1][:, 2 * half:2 * half + 2], PS[b][:, :].rearrange("p (f t) -> p f t", f=2), 1e-24, None, MAX, None, p, *ct)
            free[b] = [e]
            kn.append(e)
        t = A.act(tmp[1], tmp[1], ACT.Sqrt, *kn)
        t = V.rec(tmp[1], tmp[1], t)
        kkt = V.tt(kkT, kkT, tmp[1], MUL, t, sq)
        km = []
        for f in range(4):
            t = V.ts(tmp[2][:, f], aT[:, f], 1.0, pr("k_a", f), SUB, MUL, at, kn)
            km.append(V.stt(um[:, 4 + f], tmp[2][:, f], 1.0, um[:, 4 + f], ADD, MUL, t, *kkr))
        ch = lambda x: x.rearrange("p f (c t) -> p f c t", c=2)
        zt, rt, bt, kt = [], [], [], []
        ba = G.tt(aT, aT, kkT, MUL, kkt, *km)
        for c in range(2):
            s = slice(128 * c, 128 * c + 128)
            zt.append(V.stt(zT[:, :, s], kkT[:, :, s], -1.0, EP[:, :, c, 0:128], MUL, MUL, kkt, ep))
            rt.append(G.tt(rT[:, :, s], um[:, 0:4, s], EP[:, :, c, 1:129], MUL, ep))
            bt.append(V.tt(bT[:, :, s], aT[:, :, s], EN[:, :, c, 1:129], MUL, ba, en))
            kt.append(G.tt(kT[:, :, s], um[:, 4:8, s], EN[:, :, c, 1:129], MUL, en, *km))
        bo = G.tt(tmp[0], um[:, 0:4], um[:, 4:8], MUL, *km, gt)
        bb = []
        for f in range(4):
            bb.append(V.ts(tmp[0][:, f], tmp[0][:, f], pr("r_k", f), None, MUL, None, bo))
        bon = []
        for half in range(2):
            b = half
            T.need(*bb, *free[b])
            p = mm(PS[b][:, :], C("bones"), tmp[0][:, 2 * half:2 * half + 2], True, True, sig=True)
            e = V.tt(um[:, 4 + 2 * half:6 + 2 * half], PS[b][:, :].rearrange("p (f t) -> p f t", f=2),
                     um[:, 8 + 2 * half:10 + 2 * half], MUL, p, bo, *kt)
            free[b] = [e]
            bon.append(e)
        tk = []
        for c in range(2):
            b = 2 + c
            T.need(*free[b])
            for f in range(4):
                p = tr(PS[b][:, f * 128:f * 128 + 128], um[:, 8 + f, c * 128:c * 128 + 128], sig=(f == 3))
            e = A.act(Vtok[:, c, :], PS[b][:, :], ACT.Copy, p)
            free[b] = [e]
            tk.append(e)
        for c, (src, st) in enumerate(((bT, bt), (kT, kt))):
            b = c
            T.need(*st, *free[b])
            for f in range(4):
                p = tr(PS[b][:, f * 128:f * 128 + 128], src[:, f, 0:128], sig=(f == 3))
            e = A.act(BK[:, c, :], PS[b][:, :], ACT.Copy, p, lora_done)
            free[b] = [e]
            tk.append(e)

        so_t, sp_t, w_t, pv_t = [], {}, {}, {}
        zb = [4, 5, 0]

        def sb_scores(h):
            j, po, i = h // 2, 64 * (h % 2), h % 3
            b = zb[i]
            q, k, z = qk[po:po + 64, j], qk[po:po + 64, 4 + j], PS[b][:, 0:384]
            T.need(qk_t[j], qk_t[4 + j], *free[b])
            mm(PS[b][:, 0:256], k[:, 0:128], q, True, False)
            mm(PS[b][:, 256:384], k[:, 128:256], q[:, 128:256], False, False)
            mm(PS[b][:, 0:128], C("ident"), C("mnegs"), False, False)
            p = mm(PS[b][:, 256:384], C("ident"), C("mnegs"), False, True, sig=True)
            t = A.act(sbe[:, i], z, ACT.Abs, p, pv_t.get(h - 3))
            t = A.act(sbe[:, i], sbe[:, i], ACT.Exp, t, scale=-1.0)
            t = A.act(sbe[:, i], sbe[:, i], ACT.Ln, t, bias=1.0)
            sp_t[h] = V.stt(sbs[:, i], z, 0.0, sbe[:, i], MAX, ADD, t)

        def sb_weights(h):
            i = h % 3
            b = zb[i]
            T.need(sp_t[h])
            mm(PS[b][:, 0:256], C("ntri"), sbs[:, i, 0:256], False, False)
            mm(PS[b][:, 128:256], C("nones"), sbs[:, i, 256:384], False, False)
            p = mm(PS[b][:, 256:384], C("ntri"), sbs[:, i, 256:384], False, True, sig=True)
            w_t[h] = A.act(sbe[:, i], PS[b][:, 0:384], ACT.Exp, p, sp_t[h])
            free[b] = [w_t[h]]

        def sb_values(h):
            j, po, i = h // 2, 64 * (h % 2), h % 3
            ob = 6 + j % 2
            T.need(w_t[h], *vt_t)
            if po == 0:
                T.need(*free[ob])
            hs = slice(h * 64, h * 64 + 64)
            mm(PS[ob][po:po + 64, 0:256], vtok[:, 0, hs], sbe[:, i, 0:256], True, False)
            pv_t[h] = mm(PS[ob][po:po + 64, 128:256], vtok[:, 1, hs], sbe[:, i, 256:384], False, True, sig=True)
            if po:
                t = A.act(sbo[:, j], PS[ob][:, 0:256], ACT.Copy, pv_t[h])
                free[ob] = [t]
                so_t.append(t)

        for h in range(10):
            if h < 8:
                sb_scores(h)
            if 1 <= h < 9:
                sb_weights(h - 1)
            if h >= 2:
                sb_values(h - 2)
        sq2 = ar(22564, 1024).rearrange("p (f t) -> p f t", f=4)
        s2 = A.act(sq2, sbo, ACT.Square, *so_t, *pv_t.values())
        mt = []
        rr = ar(19492, 1024).rearrange("p (f t) -> p f t", f=4)
        rg = []
        for half in range(2):
            b = 4 + half
            T.need(s2, *free[b])
            p = mm(PS[b][:, :], C("bones"), sq2[:, 2 * half:2 * half + 2], True, True, sig=True)
            e = V.ts(rr[:, 2 * half:2 * half + 2], PS[b][:, :].rearrange("p (f t) -> p f t", f=2), 1.0 / 64, 1e-6, MUL, ADD, p)
            free[b] = [e]
            rg.append(e)
        t = A.act(rr, rr, ACT.Sqrt, *rg)
        t = V.rec(rr, rr, t)
        for f in range(4):
            mt.append(V.stt(sbo[:, f], sbo[:, f], pr("sb_out_g", f), rr[:, f], MUL, MUL, t, s2))
        mt = parts_of(xnh[:, 0:4], xnl[:, 0:4], sbo, *mt, xn_free)
        sb_done = mt

        at_t = []
        for g in range(4):
            c, par = g // 2, g % 2
            b = g
            T.need(*zt, *bt, *free[b])
            for i in range(4):
                po, s = 64 * par, slice(128 * c, 128 * c + 128)
                p = mm(PS[b][:, i * 128:i * 128 + 128], bT[po:po + 64, i, s], zT[po:po + 64, i, s], True, True, sig=(i == 3))
            ms = C("ms")[:, None, :].to_broadcast([128, 4, 128])
            e = V.tt(AT[:, 4 * g:4 * g + 4], PS[b][:, :].rearrange("p (q t) -> p q t", q=4), ms, MUL, p, *sb_done)
            free[b] = [e]
            at_t.append(e)
        idb = C("ident")[:, None, :].to_broadcast([128, 4, 128])
        p3 = lambda b: PS[b][:, :].rearrange("p (q t) -> p q t", q=4)
        x_t = [[] for _ in range(4)]
        y_r = [[] for _ in range(4)]
        m_r = [[] for _ in range(3)]
        units = [(li, g) for li in range(len(LEVELS)) for g in range(4)]
        m_t, yt = {}, {}

        def mask_level(u):
            li, g = units[u]
            lv = C(f"lv{LEVELS[li]}")[:, None, :].to_broadcast([128, 4, 128])
            m_t[u] = G.tt(M[:, u % 3], AT[:, 4 * g:4 * g + 4], lv, MUL, at_t[g], *m_r[u % 3], *bon)

        def level_y(u):
            li, g = units[u]
            gs, b0, Mb = slice(4 * g, 4 * g + 4), (g % 2) * 3, M[:, u % 3]
            T.need(m_t[u], *x_t[g], *free[b0])
            for i in range(4):
                p = mm(PS[b0][:, i * 128:i * 128 + 128], Mb[:, i], C("ident") if li == 0 else X[:, 4 * g + i], True, True, sig=(i == 3))
            m_r[u % 3] = [p]
            if li == 0:
                e1 = V.tt(X[:, gs], p3(b0), idb, ADD, p, *sb_done)
                e2 = V.tt(XT[:, gs], Mb, idb, ADD, m_t[u], *sb_done)
                m_r[u % 3].append(e2)
                free[b0] = [e1]
                x_t[g] = [e1, e2]
                return
            yt[u] = A.act(Y[:, gs], p3(b0), ACT.Copy, p, *y_r[g])
            free[b0] = [yt[u]]

        def level_x(u):
            li, g = units[u]
            lastl = li == len(LEVELS) - 1
            gs, b1, b2 = slice(4 * g, 4 * g + 4), (g % 2) * 3 + 1, (g % 2) * 3 + 2
            T.need(yt[u], *free[b1], *free[b2])
            if not lastl:
                for i in range(4):
                    q = 4 * g + i
                    p1 = mm(PS[b1][:, i * 128:i * 128 + 128], XT[:, q], Y[:, q], True, True, sig=(i == 3))
            for i in range(4):
                q = 4 * g + i
                p2 = mm(PS[b2][:, i * 128:i * 128 + 128], Y[:, q], XT[:, q], True, True, sig=(i == 3))
            y_r[g] = [p2]
            x_t[g] = []
            if not lastl:
                e1 = V.tt(X[:, gs], p3(b1), X[:, gs], ADD, p1)
                free[b1] = [e1]
                x_t[g].append(e1)
            e2 = V.tt(XT[:, gs], p3(b2), XT[:, gs], ADD, p2)
            free[b2] = [e2]
            x_t[g].append(e2)

        mask_level(0)
        for u in range(len(units) + 1):
            if u + 1 < len(units):
                mask_level(u + 1)
            if u < len(units):
                level_y(u)
            if u and units[u - 1][0]:
                level_x(u - 1)

        GT = ar(8212, 2048).rearrange("p (k q t) -> p k q t", k=4, q=4)
        RHS = ar(10276, 1024).rearrange("p (c q n) -> p c q n", c=2, q=8)
        U = ar(0, 1024).rearrange("p (c q n) -> p c q n", c=2, q=8)
        S0 = ar(1024, 256).rearrange("p (f n) -> p f n", f=4)
        oT = kkT
        o_t = []
        s0_t = []
        msb = C("ms")[:, None, :].to_broadcast([128, 4, 128])
        mib = C("triu")[:, None, :].to_broadcast([128, 4, 128])
        gr = [[], [], []]
        for c in range(2):
            s = slice(128 * c, 128 * c + 128)
            ut = [None, None]
            for hg in range(2):
                g = c * 2 + hg
                hh = [2 * i + hg for i in range(4)]
                po = 64 * hg
                fb = lambda x, h: x[64 * (h % 2):64 * (h % 2) + 64, h // 2, s]
                mats = ((0, kT, zT, msb), (1, kT, rT, mib), (2, bT, rT, mib))
                gt_ = []
                for k, l_, r_, mk in mats:
                    b = k
                    T.need(*kt, *rt, *free[b], *x_t[g])
                    for i, h in enumerate(hh):
                        p = mm(PS[b][:, i * 128:i * 128 + 128], fb(l_, h), fb(r_, h), True, True, sig=(i == 3))
                    e = V.tt(GT[:, k], p3(b), mk, MUL, p, *gr[k], *zt, *bt, *rt, *kt)
                    free[b] = [e]
                    gt_.append(e)
                b = 3
                T.need(gt_[0], *tk, *s0_t, *free[b])
                for i, h in enumerate(hh):
                    o = PS[b][:, i * 64:i * 64 + 64]
                    p = mm(o, GT[:, 0, i], Vtok[:, c, h * 64:h * 64 + 64], i == 0, c == 0 and i == 3, sig=(c == 0 and i == 3))
                    if c == 1:
                        p = mm(o, fb(zT, h), S0[po:po + 64, h // 2], False, i == 3, sig=(i == 3))
                gr[0] = [p]
                rhs_t = A.act(RHS[:, c, 4 * hg:4 * hg + 4], PS[b][:, 0:256].rearrange("p (q n) -> p q n", q=4), ACT.Copy, p, *bt)
                free[b] = [rhs_t]
                b = 4
                T.need(rhs_t, *free[b])
                for i, h in enumerate(hh):
                    p = mm(PS[b][:, i * 64:i * 64 + 64], XT[:, 4 * g + i], RHS[:, c, 4 * hg + i], True, True, sig=(i == 3))
                ut[hg] = A.act(U[:, c, 4 * hg:4 * hg + 4], PS[b][:, 0:256].rearrange("p (q n) -> p q n", q=4), ACT.Copy, p, y_r[0], y_r[1], y_r[2], y_r[3])
                free[b] = [ut[hg]]
                b = 5
                T.need(ut[hg], gt_[1], gt_[2], *free[b])
                for i, h in enumerate(hh):
                    o = PS[b][po:po + 64, i * 128:i * 128 + 128]
                    mm(o, Vtok[:, c, h * 64:h * 64 + 64], GT[:, 1, i], i == 0, False)
                    p = mm(o, U[:, c, 4 * hg + i], GT[:, 2, i], False, False, sig=True)
                    if c == 1:
                        p = mm(o, S0[po:po + 64, h // 2], fb(rT, h), False, i == 3, sig=True)
                gr[1] = gr[2] = [p]
                e = A.act(oT[po:po + 64, :, s], PS[b][po:po + 64, :].rearrange("p (j t) -> p j t", j=4), ACT.Copy, p, *zt, ba)
                free[b] = [e]
                o_t.append(e)
            if c == 0:
                b = 6
                T.need(*ut, *tk, *free[b])
                for h in range(8):
                    po = 64 * (h % 2)
                    o = PS[b][po:po + 64, (h // 2) * 64:(h // 2) * 64 + 64]
                    mm(o, BK[:, 0, h * 64:h * 64 + 64], U[:, 0, 4 * (h % 2) + h // 2], h < 2, False)
                    p = mm(o, BK[:, 1, h * 64:h * 64 + 64], Vtok[:, 0, h * 64:h * 64 + 64], False, h >= 6, sig=(h == 7))
                for f in range(4):
                    e = V.ts(S0[:, f], PS[b][:, f * 64:f * 64 + 64], small[:, 16 + f:17 + f], None, MUL, None, p, sct, *y_r)
                    s0_t.append(e)
                free[b] = [e]

        mu = v4(12324)
        sqd = v4(13348)
        us = []
        for half in range(2):
            b = half
            hs2 = slice(2 * half, 2 * half + 2)
            T.need(*o_t, *free[b])
            p = mm(PS[b][:, :], C("bones"), oT[:, hs2], True, True, sig=True)
            e = V.stt(mu[:, hs2], PS[b][:, :].rearrange("p (f t) -> p f t", f=2), -1.0 / 64, oT[:, hs2], MUL, ADD, p)
            free[b] = [e]
            us.append(e)
        s2 = A.act(sqd, mu, ACT.Square, *us)
        vr = []
        for half in range(2):
            b = 2 + half
            hs2 = slice(2 * half, 2 * half + 2)
            T.need(s2, *free[b])
            p = mm(PS[b][:, :], C("bones"), sqd[:, hs2], True, True, sig=True)
            e = V.ts(bT[:, hs2], PS[b][:, :].rearrange("p (f t) -> p f t", f=2), 1.0 / 64, 64e-5, MUL, ADD, p)
            free[b] = [e]
            vr.append(e)
        t = A.act(bT, bT, ACT.Sqrt, *vr)
        t = V.rec(bT, bT, t)
        fin = []
        for f in range(4):
            t1 = V.stt(mu[:, f], mu[:, f], pr("ln_w", f), bT[:, f], MUL, MUL, t, s2)
            t1 = V.stt(mu[:, f], mu[:, f], pr("ln_b", f), um[:, 4 + f], ADD, ADD, t1, *bon)
            fin.append(V.tt(mu[:, f], mu[:, f], gT[:, f], MUL, t1, *gt))
        fin = parts_of(xnh[:, 4:8], xnl[:, 4:8], mu, *fin, xn_free)
        T.need(*mt, *free[4], *free[5], *free[6], *free[7])
        for k in range(0, 8, 2):
            if k == 4:
                T.need(*fin)
            p = down(take(), k, 8, xnh, xnl)
        ot = add_x(p)
        barrier()

        xn_t = norm_T("norm_ffn_g", xnt_[:, :], *ot)
        lg = ftmp[:, 0:72].rearrange("p (t n) -> p t n", t=2)
        ld = take()
        lg_t = []
        for tt in range(2):
            T.need(*xn_t, *free[4 + tt])
            p = proj_tok(PS[4 + tt][:, 0:36], ld, 0, tt, 0, 36, True, True)
            lg_t.append(V.tt(lg[:, tt], PS[4 + tt][:, 0:36], row[:, 0:36], ADD, p))
            free[4 + tt] = [lg_t[tt]]
        done(ld, p)
        comb = comb_[:, :].rearrange("p (t n) -> p t n", t=2)
        sc = ftmp[:, 128:528]
        on8 = ftmp[:, 96:128]
        t_on = V.set(on8, 1.0)
        cmb_t = []
        for tt in range(2):
            o, e = 200 * tt, lg_t[tt]
            gl, el = lg[:, tt, 0:4], lg[:, tt, 4:36]
            gm, gs_, ngm = sc[:, o:o + 1], sc[:, o + 1:o + 2], sc[:, o + 2:o + 3]
            ge, eq, cs, oh, pen = (sc[:, o + 4 + 4 * i:o + 8 + 4 * i] for i in range(5))
            ml, e1h, c32, m2 = (sc[:, o + 28 + 32 * i:o + 60 + 32 * i] for i in range(4))
            m1, mx2, ex, den, w1, w2s = (sc[:, o + 160 + i:o + 161 + i] for i in range(6))

            def onehot(dst, src, mx, cum, n, tk_):
                t_ = V.ts(dst, src, mx, None, ALU.is_equal, None, tk_)
                t_ = V.op(lambda e: e.tensor_tensor_scan(cum, on8[:, 0:n], dst, 0.0, MUL, ADD), t_, t_on)
                return V.stt(dst, cum, 1.0, dst, ALU.is_equal, MUL, t_)

            t = V.red(gm, gl, MAX, e)
            tg = V.ts(ngm, gm, -1.0, None, MUL, None, t)
            tg = A.act(ge, gl, ACT.Exp, tg, bias=ngm, accum=gs_)
            t = onehot(oh, gl, gm, cs, 4, t)
            t = V.ts(pen, oh, -1.0, BIG, ADD, MUL, t)
            t = V.tt(ml.rearrange("p (g n) -> p g n", g=4), el.rearrange("p (g n) -> p g n", g=4),
                     pen[:, :, None].to_broadcast([128, 4, 8]), ADD, t)
            t = V.red(m1, ml, MAX, t)
            t = onehot(e1h, ml, m1, c32, 32, t)
            t = V.stt(ml, e1h, -4.0 * BIG, ml, MUL, ADD, t)
            t = V.red(mx2, ml, MAX, t)
            t2 = onehot(m2, ml, mx2, c32, 32, t)
            t = V.tt(ex, mx2, m1, SUB, t)
            t = A.act(ex, ex, ACT.Exp, t)
            t = V.stt(den, ex, 1.0, gs_, ADD, MUL, t, tg)
            t = V.rec(w1, den, t)
            t = V.tt(w2s, ex, w1, MUL, t)
            t3 = V.ts(m2, m2, w2s, None, MUL, None, t, t2)
            cmb_t.append(V.stt(comb[:, tt], e1h, w1, m2, MUL, ADD, t3))

        hhi, hlo = (x[:, :].rearrange("p (f t) -> p f t", f=22) for x in (hhi_, hlo_))
        sg, hf = (x[:, :].rearrange("p (b f t) -> p b f t", b=2, f=2) for x in (sg_, hf_))
        hf_r = [None, None]

        def gate_up(i, f, *reads):
            bg, bu, i = i % 2, 2 + i % 2, i % 2
            v2 = lambda b: PS[b][:, :].rearrange("p (f t) -> p f t", f=2)
            ld = take()
            proj_T(ld, 0, bg, 0, False, *xn_t)
            pg = proj_T(ld, 128, bg, 1, True)
            ld = take()
            proj_T(ld, 0, bu, 0, False)
            pu = proj_T(ld, 128, bu, 1, True)
            a = A.act(sg[:, i], v2(bg), ACT.Silu, pg, hf_r[i])
            free[bg] = [a]
            v = V.tt(hf[:, i], v2(bu), sg[:, i], MUL, pu, a, hf_r[i])
            free[bu] = [v]
            t = A.act(hhi[:, f:f + 2], hf[:, i], ACT.Copy, v, *reads)
            hf_r[i] = G.tt(hlo[:, f:f + 2], hf[:, i], f32(hhi[:, f:f + 2]), SUB, t, v, *reads)
            return [t, hf_r[i]]

        moe_prev = [[c] for c in cmb_t for _ in range(2)]
        hv, hE_r = {}, [None, None]
        for ei in range(33):
            if ei < 32:
                hv[ei] = gate_up(ei, 2 * (ei % 2), hE_r[ei % 2])
            if ei == 0:
                continue
            c = ei - 1
            ld = take()
            T.need(*hv[c], *free[4], *free[5], *free[6], *free[7])
            p = down(ld, 0, 2, hhi, hlo, k_of=lambda k: 2 * (c % 2) + k)
            hE_r[c % 2] = p
            for b in range(4):
                o = xtok[:, b // 2, (b % 2) * 512:(b % 2) * 512 + 512]
                e = V.stt(o, PS[4 + b][:, :], comb[:, b // 2, c:c + 1], o, MUL, ADD, p, *moe_prev[b])
                free[4 + b] = [e]
                moe_prev[b] = [e]
        barrier()
        gB = ftmp[:, 1024:2048]
        dg = Sem(sem("d_gb"))
        gb_t = G.dma(gB, I["final_norm_g"].rearrange("(a n) -> a n", a=1).to_broadcast([128, 1024]), dg)
        jk = xnt_[:, 0:1024]
        for tt in range(2):
            ss = small[:, 32 + tt:33 + tt]
            t = A.act(jk, xtok[:, tt], ACT.Square, *([t] if tt else []), accum=ss)
            tq = rstd(ss, ss, 1024, 1e-6, t)
            xt = V.stt(xtok[:, tt], xtok[:, tt], ss, gB, MUL, MUL, tq, gb_t)
        barrier()

        ang, rk, rq = (rope_[:, 64 * i:64 * i + 64].rearrange("p (f t n) -> p f t n", f=2, t=2) for i in range(3))
        posf = small[:, 36:38]
        t = V.cp(posf, posi[:, :])
        for tt in range(2):
            for f in range(2):
                last = V.ts(ang[:, f, tt], invf, posf[:, tt:tt + 1], None, MUL, None, t)
        fl = lambda x: x.rearrange("p f t n -> p (f t n)")
        MAGIC = 12582912.0
        P1, P2, P3 = 6.28125, 1.9350051879882812e-3, 3.01991598195675e-7
        t = last
        tk_ = []
        for f in range(2):
            t0 = V.ts(rk[:, f], ang[:, f], 1.0 / (2 * math.pi), 0.25 if f == 0 else 0.0, MUL, ADD, t)
            t0 = V.ts(rk[:, f], rk[:, f], MAGIC, MAGIC, ADD, SUB, t0)
            tk_.append(t0)
        t = V.stt(fl(rq), fl(rk), -P1, fl(ang), MUL, ADD, *tk_)
        t = V.stt(fl(rq), fl(rk), -P2, fl(rq), MUL, ADD, t)
        t = V.stt(fl(rq), fl(rk), -P3, fl(rq), MUL, ADD, t)
        t = V.ts(rq[:, 0], rq[:, 0], math.pi / 2, None, ADD, None, t)
        t = V.ts(fl(rq), fl(rq), 3.1415925, -3.1415925, ALU.min, MAX, t)
        rope_t = A.act(fl(ang), fl(rq), ACT.Sin, t)
        cosT, sinT = ang[:, 0], ang[:, 1]

        def ffn(gname, *toks):
            nonlocal xn_t
            hf_r[0] = hf_r[1] = None
            xn_t = norm_T(gname, xnt_[:, :], *toks)
            needs = {}
            for i in range(11):
                needs[2 * i] = needs[2 * i + 1] = gate_up(i, 2 * i)
            T.need(*free[4], *free[5], *free[6], *free[7])
            for i in range(11):
                p = down(take(), 2 * i, 22, hhi, hlo, needs=needs)
            add_x(p, 0.5)
            barrier()

        def mixer(l):
            nonlocal xn_t
            N = lambda s: f"{s}{l}"
            xn_t = norm_T(N("mix_norm"), ar(16000, 2048))
            zs = ar(0, 2048).rearrange("p (f t) -> p f t", f=8)
            yT = ar(2048, 4096).rearrange("p (f t) -> p f t", f=16)
            qkl = ar(6144, 768).rearrange("p (f t) -> p f t", f=3)
            cc = ar(6912, 1032).rearrange("p (f t) -> p f t", f=4)
            cbg = ar(7944, 1024).rearrange("p (f t) -> p f t", f=4)
            chh = ar(8968, 1024).rearrange("p (f t) -> p f t", f=4)
            dts = ar(9992, 512)
            B0 = 10504
            xb = ar(B0, 3120).rearrange("p (f t) -> p f t", f=12)
            xbc = ar(B0 + 3120, 3072).rearrange("p (f t) -> p f t", f=12)
            xs = ar(B0 + 6192, 2048).rearrange("p (c n) -> p c n", c=2)
            cb = ar(B0 + 8240, 1024).rearrange("p (g s t) -> p g s t", g=2, s=2)
            seg = ar(B0 + 9264, 1536).rearrange("p (b t) -> p b t", b=4)
            Md = ar(B0 + 10800, 1536).rearrange("p (b t) -> p b t", b=4)
            dtr = dts[:, 0:192].rearrange("p (t n) -> p t n", t=2)
            kpe = dts[:, 192:256].rearrange("p (t n) -> p t n", t=2)
            dt = dts[:, 256:320].rearrange("p (t n) -> p t n", t=2)
            dta = dts[:, 320:384].rearrange("p (t n) -> p t n", t=2)
            ncs = dts[:, 384:448].rearrange("p (t n) -> p t n", t=2)
            Ar = dts[:, 448:480]
            tsp = dts[:, 0:64].rearrange("p (t n) -> p t n", t=2)

            pad = [V.set(xb[:, :, 0:2], 0.0), V.set(xb[:, :, 258:260], 0.0), V.set(cc[:, :, 0:1], 0.0), V.set(cc[:, :, 257:258], 0.0)]
            st = {"b": 0}

            def nxt():
                st["b"] += 1
                return 4 + st["b"] % 4

            def pair():
                b = nxt()
                ld = take()
                proj_T(ld, 0, b, 0, False, *xn_t)
                p = proj_T(ld, 128, b, 1, True)
                return b, p, PS[b][:, :].rearrange("p (f t) -> p f t", f=2)

            conv_t = []

            def conv(f, e):
                for ff in (f, f + 1):
                    t = V.ts(xbc[:, ff], xb[:, ff, 0:256], pr(N("conv_w"), ff), None, MUL, None, e, *pad)
                    for k in range(1, 5):
                        t = V.stt(xbc[:, ff], xb[:, ff, k:k + 256], pr(N("conv_w"), 12 * k + ff), xbc[:, ff], MUL, ADD, t)
                    conv_t.append(t)

            late = []
            for f in range(0, 12, 2):
                b, p, v = pair()
                e = A.act(xb[:, f:f + 2, 2:258], v, ACT.Copy, p)
                free[b] = [e]
                if late:
                    conv(*late.pop())
                late.append((f, e))
            b, p, v = pair()
            conv(*late.pop())
            e = A.act(qkl[:, 0:2], v, ACT.Copy, p)
            free[b] = [e]
            ql_t = [e]
            ld = take()
            b = nxt()
            p = proj_T(ld, 0, b, 0, False)
            e = A.act(qkl[:, 2], PS[b][:, 0:256], ACT.Copy, p)
            free[b] = [e]
            ql_t.append(e)
            dt_t, pe_t = [], []
            for tt in range(2):
                b = nxt()
                T.need(*free[b])
                proj_tok(PS[b][:, 0:32], ld, 1, tt, 0, 32, True, False)
                p = proj_tok(PS[b][:, 32:64], ld, 2, tt, 0, 32, False, True)
                r = ROW[N("dt_bias")]
                dt_t.append(V.tt(dt[:, tt], PS[b][:, 0:32], row[:, r:r + 32], ADD, p))
                e = V.cp(kpe[:, tt], PS[b][:, 32:64], p)
                pe_t.append(e)
                free[b] = [e]
            done(ld, p)
            ch_t, cb_t, cc_t, zs_t = [], [], [], []
            for i in range(2):
                b, p, v = pair()
                ch_t.append(A.act(chh[:, 2 * i:2 * i + 2], v, ACT.Copy, p))
                free[b] = [ch_t[i]]
            for i in range(2):
                b, p, v = pair()
                cb_t.append(A.act(cbg[:, 2 * i:2 * i + 2], v, ACT.Copy, p))
                free[b] = [cb_t[i]]
            for i in range(2):
                b, p, v = pair()
                cc_t.append(V.tt(cc[:, 2 * i:2 * i + 2, 1:257], v, chh[:, 2 * i:2 * i + 2], MUL, p, ch_t[i]))
                free[b] = [cc_t[i]]
            for i in range(4):
                b, p, v = pair()
                zs_t.append(A.act(zs[:, 2 * i:2 * i + 2], v, ACT.Silu, p))
                free[b] = [zs_t[i]]

            cv = []
            for f in range(4):
                t = V.ts(chh[:, f], cc[:, f, 0:256], pr(N("cw"), f), None, MUL, None, cc_t, pad)
                for k in (1, 2):
                    t = V.stt(chh[:, f], cc[:, f, k:k + 256], pr(N("cw"), 4 * k + f), chh[:, f], MUL, ADD, t)
                cv.append(t)
            t = V.tt(chh, chh, cbg, MUL, *cv, *cb_t)
            t = cq = A.act(cbg, chh, ACT.Square, t)
            rc = yT[:, 12:16]
            rg = []
            for half in range(2):
                b = half
                hs2 = slice(2 * half, 2 * half + 2)
                T.need(t, *free[b])
                p = mm(PS[b][:, :], C("bones"), cbg[:, hs2], True, True, sig=True)
                e = V.ts(rc[:, hs2], PS[b][:, :].rearrange("p (f t) -> p f t", f=2), 1.0 / 64, 1e-6, MUL, ADD, p)
                free[b] = [e]
                rg.append(e)
            t = A.act(rc, rc, ACT.Sqrt, *rg)
            t = V.rec(rc, rc, t)
            yc = [V.stt(rc[:, f], chh[:, f], pr(N("conv_out"), f), rc[:, f], MUL, MUL, t) for f in range(4)]

            xb_t = []
            for f in range(12):
                xb_t.append(A.act(xbc[:, f], xbc[:, f], ACT.Silu, conv_t[f], bias=pr(N("conv_b"), f)))
            r = ROW[N("a_log")]
            t = A.act(Ar, row[:, r:r + 32], ACT.Exp)
            ta = V.ts(Ar, Ar, -1.0, None, MUL, None, t)
            t = A.act(tsp, dt, ACT.Abs, *dt_t)
            t = A.act(tsp, tsp, ACT.Exp, t, scale=-1.0)
            t = A.act(tsp, tsp, ACT.Ln, t, bias=1.0)
            td = V.stt(dt, dt, 0.0, tsp, MAX, ADD, t)
            t = V.tt(dta, dt, Ar[:, None, :].to_broadcast([128, 2, 32]), MUL, td, ta)
            b = 2
            T.need(t, *free[b])
            o = lambda tt, d: PS[b][:, 32 * tt + 16 * d:32 * tt + 16 * d + 16]
            f_, k_ = slice(0, 16), slice(16, 32)
            mm(o(0, 0), C("triu"), dta[:, 0, f_], True, False)
            mm(o(1, 0), C("triu"), dta[:, 1, f_], False, False)
            mm(o(1, 0), C("ones"), dta[:, 0, f_], False, False)
            mm(o(0, 1), C("tril"), dta[:, 0, k_], False, False)
            mm(o(0, 1), C("ones"), dta[:, 1, k_], False, False)
            p = mm(o(1, 1), C("tril"), dta[:, 1, k_], False, True, sig=True)
            cs_t = V.ts(ncs, PS[b][:, 0:64].rearrange("p (t n) -> p t n", t=2), 1.0, None, MUL, None, p)
            free[b] = [cs_t]
            xs_t = []
            for tt in range(2):
                for hb in range(2):
                    b = nxt()
                    T.need(*xb_t[0:8], *free[b])
                    for k in range(4):
                        p = tr(PS[b][:, k * 128:k * 128 + 128], xbc[:, hb * 4 + k, tt * 128:tt * 128 + 128], sig=(k == 3))
                    e = A.act(xs[:, tt, hb * 512:hb * 512 + 512], PS[b][:, :], ACT.Copy, p)
                    free[b] = [e]
                    xs_t.append(e)
            cbt = []
            for g in range(2):
                b = nxt()
                T.need(xb_t[8 + g], xb_t[10 + g], *free[b])
                mm(PS[b][:, 0:256], xbc[:, 8 + g, 0:128], xbc[:, 10 + g], True, False)
                p = mm(PS[b][:, 256:512], xbc[:, 8 + g, 128:256], xbc[:, 10 + g], False, True, sig=True)
                e = A.act(cb[:, g], PS[b][:, :].rearrange("p (s t) -> p s t", s=2), ACT.Copy, p)
                free[b] = [e]
                cbt.append(e)
            seg_r, Md_r = {}, {}
            exp_t, m_t, y_t, ys = {}, {}, {}, []
            ends = lambda d: (0, 1) if d == 0 else (1, 0)
            near = lambda d: slice(128 * d, 128 * d + 128)
            far = lambda d: slice(128 - 128 * d, 256 - 128 * d)

            def ssd_decay(k):
                h, d, b, i = k // 2, k % 2, k % 4, k % 4
                hd = 16 * d + h
                T.need(*free[b])
                bc = lambda tt: dta[:, tt, hd:hd + 1].to_broadcast([128, 128])
                wide, tri = ("triu", "triu") if d == 0 else ("ones2", "tril")
                mm(PS[b][:, 0:256], bc(d), C(wide, 256), True, False)
                p = mm(PS[b][:, far(d)], bc(1 - d), C(tri), False, True, sig=True)
                (sfull, shalf), mk = ends(d), C("mnegf") if d == 0 else C("mnegb")
                V.stt(seg[:, i, near(d)], PS[b][:, near(d)], ncs[:, sfull, hd:hd + 1], mk, SUB, ADD, p, cs_t, seg_r.get(k - 4))
                V.ts(seg[:, i, far(d)], PS[b][:, far(d)], ncs[:, sfull, hd:hd + 1], None, SUB, None)
                e = V.stt(seg[:, i, 256:384], PS[b][:, far(d)], ncs[:, shalf, hd:hd + 1], mk, SUB, ADD)
                free[b] = [e]
                exp_t[k] = A.act(seg[:, i], seg[:, i], ACT.Exp, e)

            def ssd_weights(k):
                h, d, i = k // 2, k % 2, k % 4
                hd, g, (sfull, shalf) = 16 * d + h, h // 8, ends(d)
                V.stt(Md[:, i, 0:256], seg[:, i, 0:256], dt[:, sfull, hd:hd + 1], cb[:, g, sfull], MUL, MUL, exp_t[k], td, cbt[g], Md_r.get(k - 4))
                e = V.stt(Md[:, i, 256:384], seg[:, i, 256:384], dt[:, shalf, hd:hd + 1], cb[:, g, shalf, far(d)], MUL, MUL)
                seg_r[k] = m_t[k] = e

            def ssd_values(h):
                po, ob = 64 * (h % 2), 4 + (h // 2) % 4
                T.need(m_t[2 * h], m_t[2 * h + 1], *xs_t)
                if po == 0:
                    T.need(*free[ob])
                O = lambda a, n: PS[ob][po:po + 64, a:a + n]
                hx = slice(h * 64, h * 64 + 64)
                i0, i1 = 2 * h % 4, (2 * h + 1) % 4
                mm(O(0, 256), xs[:, 0, hx], Md[:, i0, 0:256], True, False)
                mm(O(128, 128), xs[:, 1, hx], Md[:, i0, 256:384], False, False)
                mm(O(0, 256), xs[:, 1, hx], Md[:, i1, 0:256], False, False)
                y_t[h] = mm(O(0, 128), xs[:, 0, hx], Md[:, i1, 256:384], False, True, sig=True)
                Md_r[2 * h] = Md_r[2 * h + 1] = y_t[h]

            def ssd_out(f):
                ob = 4 + f % 4
                t = V.stt(yT[:, f], xbc[:, f], pr(N("ssd_d"), f), PS[ob][:, 0:256], MUL, ADD, y_t[2 * f + 1])
                free[ob] = [t]
                ys.append(G.tt(yT[:, f], yT[:, f], zs[:, f], MUL, t, *zs_t))

            for k in range(40):
                if k < 32:
                    ssd_decay(k)
                if 2 <= k < 34:
                    ssd_weights(k - 2)
                if k >= 4 and k % 2 == 0 and k < 36:
                    ssd_values((k - 4) // 2)
                if k >= 8 and k % 4 == 0:
                    ssd_out((k - 8) // 4)
            sqs = ar(B0, 2048).rearrange("p (f t) -> p f t", f=8)
            t = A.act(sqs, yT[:, 0:8], ACT.Square, *ys)
            rs = ar(B0 + 2048, 512).rearrange("p (g t) -> p g t", g=2)
            T.need(t, *free[0])
            for g in range(2):
                for k in range(4):
                    p = mm(PS[0][:, 256 * g:256 * g + 256], C("ones"), sqs[:, 4 * g + k], k == 0 and g == 0, k == 3 and g == 1, sig=(k == 3))
            e = V.ts(rs, PS[0][:, :].rearrange("p (g t) -> p g t", g=2), 1.0 / 512, 1e-6, MUL, ADD, p, conv_t)
            free[0] = [e]
            t = A.act(rs, rs, ACT.Sqrt, e)
            t = V.rec(rs, rs, t)
            y_t = [V.stt(yT[:, f], yT[:, f], pr(N("ssd_norm"), f), rs[:, f // 4], MUL, MUL, t) for f in range(8)]
            barrier()

            qks = ar(B0, 3072).rearrange("p (t h n) -> p t h n", t=2, h=16)
            kv = ar(B0 + 3072, 2048).rearrange("p (t h n) -> p t h n", t=2, h=8)
            qkT = ar(B0 + 5120, 4096).rearrange("p (h t) -> p h t", h=16)
            Pm = ar(B0 + 9216, 1024).rearrange("p (b k) -> p b k", b=4)
            PT = ar(B0 + 10240, 1024).rearrange("p (b k t) -> p b k t", b=2, k=4)
            om = ar(B0 + 11264, 1024).rearrange("p (t h n) -> p t h n", t=2, h=8)
            tq = ar(B0 + 12288, 1536).rearrange("p (h n) -> p h n", h=16)
            t3 = ar(B0 + 13824, 1536)
            ms_ = small[:, 40:240]
            ql = ar(B0 + 9216, 768).rearrange("p (f t) -> p f t", f=3)
            t = A.act(ql, qkl, ACT.Square, *ql_t)
            gq = [V.ts(qkl[:, f], qkl[:, f], pr(N("q_norm"), f) if f < 2 else pr(N("kv_norm")), None, MUL, None, t) for f in range(3)]
            T.need(t, *free[0])
            for tt in range(2):
                s = slice(128 * tt, 128 * tt + 128)
                mm(PS[0][:, 2 * tt:2 * tt + 1], ql[:, 0, s], C("ones", 1), tt == 0, False)
                mm(PS[0][:, 2 * tt:2 * tt + 1], ql[:, 1, s], C("ones", 1), False, False)
                p = mm(PS[0][:, 2 * tt + 1:2 * tt + 2], ql[:, 2, s], C("ones", 1), False, tt == 1, sig=True)
            lr = ms_[:, 0:4].rearrange("p (t n) -> p t n", t=2)
            pv = PS[0][:, 0:4].rearrange("p (t n) -> p t n", t=2)
            a = V.ts(lr[:, :, 0], pv[:, :, 0], 1.0 / 256, 1e-6, MUL, ADD, p)
            a2 = V.ts(lr[:, :, 1], pv[:, :, 1], 1.0 / 128, 1e-6, MUL, ADD)
            free[0] = [a2]
            t = A.act(ms_[:, 0:4], ms_[:, 0:4], ACT.Sqrt, a, a2)
            lr_t = V.rec(ms_[:, 0:4], ms_[:, 0:4], t)
            T.need(*gq)
            raw = lambda ld: ld["dmas"][0][0]
            ldq, ldk = take(), take()
            wuq, wukv = raw(ldq), raw(ldk)
            qk_t = [[], []]
            for tt in range(2):
                s = slice(128 * tt, 128 * tt + 128)
                for part, (a, n, h0, nh) in enumerate(((0, 480, 0, 5), (480, 288, 5, 3))):
                    b = 1 + part
                    T.need(*free[b])
                    mm(PS[b][:, 0:n], qkl[:, 0, s], wuq[:, 0, a:a + n], True, False)
                    p = mm(PS[b][:, 0:n], qkl[:, 1, s], wuq[:, 1, a:a + n], False, True, sig=True)
                    e = A.act(qks[:, tt, h0:h0 + nh], PS[b][:, 0:n].rearrange("p (h n) -> p h n", n=96), ACT.Copy, p, lr_t, scale=lr[:, tt, 0:1])
                    free[b] = [e]
                    qk_t[tt].append(e)
                for part in range(2):
                    b = 3 + part
                    T.need(*free[b])
                    p = mm(PS[b][:, :], qkl[:, 2, s], wukv[:, 0, part * 512:part * 512 + 512], True, True, sig=True)
                    v = PS[b][:, :].rearrange("p (h n) -> p h n", h=4)
                    e = A.act(qks[:, tt, 8 + 4 * part:12 + 4 * part, 0:64], v[:, :, 0:64], ACT.Copy, p, lr_t, scale=lr[:, tt, 1:2])
                    qk_t[tt].append(e)
                    e = A.act(kv[:, tt, 4 * part:4 * part + 4, 64:128], v[:, :, 64:128], ACT.Copy, scale=lr[:, tt, 1:2])
                    free[b] = [e]
                    qk_t[tt].append(e)
            done(ldq, p)
            done(ldk, p)
            kt_ = []
            t3h = t3.rearrange("p (h n) -> p h n", h=16)
            t4 = ar(B0 + 10240, 1024)
            for tt in range(2):
                t2 = G.cp(qks[:, tt, 8:16, 64:96], kpe[:, tt, None, :].to_broadcast([128, 8, 32]), pe_t[tt])
                sq_ = (tq, t3h)[tt]
                t = A.act(sq_, qks[:, tt], ACT.Square, *qk_t[tt], t2)
                nr = ms_[:, 8 + 16 * tt:24 + 16 * tt]
                t = V.red(nr, sq_, ADD, t)
                t = rstd(nr, nr, 96, 1e-6, t)
                t = V.tt(qks[:, tt], qks[:, tt], nr[:, :, None].to_broadcast([128, 16, 96]), MUL, t)
                r = ROW[N("qk_g")]
                for half in range(2):
                    gb = row[:, r + 96 * half:r + 96 * half + 96][:, None, :].to_broadcast([128, 8, 96])
                    t = V.tt(qks[:, tt, 8 * half:8 * half + 8], qks[:, tt, 8 * half:8 * half + 8], gb, MUL, t)
                x1, x2 = qks[:, tt, :, 64:80], qks[:, tt, :, 80:96]
                cB = cosT[:, tt, None, :].to_broadcast([128, 16, 16])
                sB = sinT[:, tt, None, :].to_broadcast([128, 16, 16])
                m = [t4[:, 256 * i:256 * i + 256].rearrange("p (h n) -> p h n", h=16) for i in range(4)]
                a0 = V.tt(m[0], x1, cB, MUL, t, rope_t)
                a1 = V.tt(m[1], x2, sB, MUL)
                a2 = V.tt(m[2], x1, sB, MUL)
                a3 = V.tt(m[3], x2, cB, MUL)
                a1 = V.tt(x1, m[0], m[1], SUB, a3)
                a3 = V.tt(x2, m[2], m[3], ADD)
                for q4 in range(4):
                    b = 4 + q4
                    T.need(a3, *free[b])
                    for k in range(4):
                        p = tr(PS[b][0:96, k * 128:k * 128 + 128], qks[:, tt, 4 * q4 + k], sig=(k == 3))
                    e = A.act(qkT[0:96, 4 * q4:4 * q4 + 4, 128 * tt:128 * tt + 128], PS[b][0:96, :].rearrange("p (h t) -> p h t", h=4), ACT.Copy, p)
                    free[b] = [e]
                    kt_.append(e)
            mx, sm = ms_[:, 40:56], ms_[:, 56:72]
            scl = 96.0 ** -0.5
            mx_t, pt_t, pv_t = {}, {}, {}

            def scores(h):
                b = h % 2
                T.need(*kt_, *free[b])
                for tt in range(2):
                    p = mm(PS[b][:, 256 * tt:256 * tt + 256], qkT[0:96, h, 128 * tt:128 * tt + 128], qkT[0:96, 8 + h], tt == 0, tt == 1, sig=(tt == 1))
                t = V.red(mx[:, 2 * h:2 * h + 2], PS[b][:, :].rearrange("p (t k) -> p t k", t=2), MAX, p)
                t = V.ts(mx[:, 2 * h:2 * h + 2], mx[:, 2 * h:2 * h + 2], -scl, None, MUL, None, t)
                for tt in range(2):
                    i = (2 * h + tt) % 4
                    a = A.act(Pm[:, i], PS[b][:, 256 * tt:256 * tt + 256], ACT.Exp, t, P_r[i],
                              bias=mx[:, 2 * h + tt:2 * h + tt + 1], scale=scl, accum=sm[:, 2 * h + tt:2 * h + tt + 1])
                free[b] = [a]
                mx_t[h] = a

            def turned(h):
                b = 2 + h % 2
                T.need(mx_t[h], *free[b])
                for tt in range(2):
                    for ks in range(2):
                        p = tr(PS[b][:, (2 * tt + ks) * 128:(2 * tt + ks) * 128 + 128], Pm[:, (2 * h + tt) % 4, ks * 128:ks * 128 + 128], sig=True)
                P_r[(2 * h) % 4] = P_r[(2 * h + 1) % 4] = p
                pt_t[h] = V.cp(PT[:, h % 2], PS[b][:, :].rearrange("p (k t) -> p k t", k=4), p, PT_r[h % 2])
                free[b] = [pt_t[h]]

            def values(h):
                T.need(pt_t[h])
                for tt in range(2):
                    if h == 0:
                        T.need(*free[4 + tt])
                    for ks in range(2):
                        p = mm(PS[4 + tt][:, h * 64:h * 64 + 64], PT[:, h % 2, 2 * tt + ks], kv[:, ks, h, 64:128], h == 0 and ks == 0, h == 7 and ks == 1, sig=True)
                PT_r[h % 2] = p
                return p

            P_r, PT_r = [None] * 4, [None] * 2
            for h in range(10):
                if h < 8:
                    scores(h)
                if 1 <= h < 9:
                    turned(h - 1)
                if h >= 2:
                    p = values(h - 2)
            a = mx_t[7]
            t = V.rec(sm, sm, a)
            smv = sm.rearrange("p (h t) -> p h t", t=2)
            mla_t = []
            for tt in range(2):
                o = V.tt(om[:, tt], PS[4 + tt][:, :].rearrange("p (h n) -> p h n", h=8), smv[:, :, tt:tt + 1].to_broadcast([128, 8, 64]), MUL, p, t)
                free[4 + tt] = [o]
                q8 = tq[:, 0:8, 0:64]
                a = V.tt(q8, om[:, tt], om[:, tt], MUL, o)
                nr = ms_[:, 80 + 8 * tt:88 + 8 * tt]
                a = V.red(nr, q8, ADD, a)
                a = rstd(nr, nr, 64, 1e-6, a)
                a = V.tt(om[:, tt], om[:, tt], nr[:, :, None].to_broadcast([128, 8, 64]), MUL, a)
                b = 6 + tt
                T.need(a, *free[b])
                fo = om[:, tt].rearrange("p h n -> p (h n)")
                for k in range(4):
                    p2 = tr(PS[b][:, k * 128:k * 128 + 128], fo[:, k * 128:k * 128 + 128], sig=(k == 3))
                for k in range(4):
                    e = A.act(yT[:, 8 + k, 128 * tt:128 * tt + 128], PS[b][:, k * 128:k * 128 + 128], ACT.Copy, p2, scale=pr(N("out_norm"), k))
                free[b] = [e]
                mla_t.append(e)
            T.need(*mla_t, *y_t, *yc, *free[4], *free[5], *free[6], *free[7])
            for k in range(16):
                if k % 2 == 0:
                    ld = take()
                for tt in range(2):
                    for dh in range(2):
                        p = mm(PS[4 + 2 * tt + dh][:, :], yT[:, k, tt * 128:tt * 128 + 128],
                               raw(ld)[:, k % 2, dh * 512:dh * 512 + 512], k == 0, k == 15, sig=True)
                if k % 2:
                    done(ld, p)
            add_x(p)
            barrier()

        for l in range(2):
            ffn(f"ffn1_norm{l}")
            mixer(l)
            ffn(f"ffn2_norm{l}")
        assert turn["n"] == len(loads)

        for n, ld in enumerate(loads):
            if n >= NR:
                L.need(loads[n - NR]["raw_done"])
            for dst, src in ld["dmas"]:
                L.items.append((lambda e, dst=dst, src=src: e.dma_start(dst, src), ld["sem"].sem, 16))
        done = L.dma(out.rearrange("(t p) d -> p t d", p=128), xtok, dout, (V, V.n))
        L.need(done)

        block = ctx.enter_context(nc.Block())

        @block.sync
        def _(e):
            L.emit(e)

        @block.tensor
        def _(e):
            T.emit(e)

        @block.vector
        def _(e):
            V.emit(e)

        @block.scalar
        def _(e):
            A.emit(e)

        @block.gpsimd
        def _(e):
            G.emit(e)


_BIG = ["w_in", "rw_g2", "w_out", "exp_w_gate", "exp_w_up", "exp_w_down", "final_norm_g"]
_BIG2 = ["ffn1_w_gate_2", "ffn1_w_up_2", "ffn1_w_down_2", "w_in_2", "mla_w_uq_2", "mla_w_ukv_2", "w_out_2",
         "ffn2_w_gate_2", "ffn2_w_up_2", "ffn2_w_down_2"]


def layout(inputs):
    a = {n: np.ascontiguousarray(inputs[n]) for n in _BIG + _BIG2}
    f = {n: np.asarray(v) for n, v in inputs.items()}
    a["x"] = np.ascontiguousarray(f["x"][0])
    a["positions"] = np.ascontiguousarray(f["positions_2"].reshape(2, 128).T)
    a["w2a2"] = np.concatenate([f["rw_w2"][0], f["rw_a2"][0]], axis=0)
    a["router"] = np.ascontiguousarray(
        np.concatenate([f["router_grp_w"][0], f["router_exp_w"][0]], axis=1).reshape(8, 128, 36).transpose(1, 0, 2).reshape(128, 288))
    c = lambda v: np.asarray(v).reshape(-1, 128).T
    parts = [c(f[n][0]) for n in ("norm_mix_g", "shift_mu", "sb_out_g", "rw_w0", "rw_a0", "rw_k_k", "rw_k_a", "rw_r_k",
                                  "rw_ln_w", "rw_ln_b", "norm_ffn_g")]
    for l in range(2):
        parts += [c(f["ffn1_norm_2"][l]), c(f["mix_norm_2"][l]), c(f["ssd_conv_w_2"][l]), c(f["ssd_conv_b_2"][l]),
                  c(f["ssd_norm_2"][l]), c(np.repeat(f["ssd_d_2"][l], 64)), c(f["mla_q_norm_2"][l]), c(f["mla_kv_norm_2"][l]),
                  c(f["mla_out_norm_2"][l]), c(f["conv_w_2"][l]), c(f["conv_out_norm_2"][l]), c(f["ffn2_norm_2"][l])]
    a["prm"] = np.ascontiguousarray(np.concatenate(parts, axis=1))
    rows_ = [f["router_grp_b"][0], f["router_exp_b"][0]]
    for l in range(2):
        rows_ += [f["ssd_dt_bias_2"][l].reshape(-1), f["ssd_a_log_2"][l].reshape(-1), f["mla_q_head_norm_2"][l], f["mla_k_head_norm_2"][l]]
    a["rowp"] = np.ascontiguousarray(np.broadcast_to(np.concatenate(rows_)[None], (128, NROW)))
    a["cst"] = constants()
    return a


def kernel(**inputs):
    import concourse.bacc as bacc
    from concourse.bass_utils import run_bass_kernel_spmd

    nc = bacc.Bacc("TRN2", target_bir_lowering=False, num_devices=1)
    arrays = {f"in_{n}": v for n, v in layout(inputs).items()}
    aps = {n[3:]: nc.dram_tensor(n, v.shape, mybir.dt.from_np(v.dtype), kind="ExternalInput").ap() for n, v in arrays.items()}
    out = nc.dram_tensor("out_0", (256, 1024), F32, kind="ExternalOutput").ap()
    program(nc, aps, out)
    r = run_bass_kernel_spmd(nc, [arrays], core_ids=[0])
    return r.results[0]["out_0"].reshape(1, 256, 1024)
```

```python
import math
from contextlib import ExitStack

import numpy as np

import concourse.bass as bass
from concourse import mybir

ALU = mybir.AluOpType
ACT = mybir.ActivationFunctionType
F32 = mybir.dt.float32
F32R = mybir.dt.float32r
I32 = mybir.dt.int32
AX = mybir.AxisListType

NR = 5
NS = 3
SLOT = 2048
DVE_PART = 1280
ARENA = 26000
BIG = 1.0e30
KAP = math.exp(-0.5)
LEVELS = [1, 2, 4, 8, 16, 32, 64]
W_OUT_ORDER = [12, 13, 14, 15] + list(range(12))

CN = {n: i for i, n in enumerate(
    ["ident", "ones", "bones", "ntri", "nones", "mnegs", "triu", "ones2", "tril", "mnegf", "mnegb", "ms"]
    + [f"lv{m}" for m in LEVELS])}


def constants():
    s = np.arange(128)[:, None]
    t = np.arange(128)[None, :]
    f = lambda c: c.astype(np.float32)
    tiles = {
        "ident": f(s == t), "ones": np.ones((128, 128), np.float32), "bones": f(s // 64 == t // 64),
        "ntri": -f(s >= t), "nones": -np.ones((128, 128), np.float32), "mnegs": -BIG * f(s >= t),
        "triu": f(s <= t), "ones2": np.ones((128, 128), np.float32), "tril": f(s >= t),
        "mnegf": -BIG * f(s > t), "mnegb": -BIG * f(s < t), "ms": f(s < t),
    }
    for m in LEVELS:
        tiles[f"lv{m}"] = f((s // (2 * m) == t // (2 * m)) & (s % (2 * m) < m) & (t % (2 * m) >= m))
    inv = (10000.0 ** (-np.arange(16, dtype=np.float64) / 16)).astype(np.float32)
    return np.concatenate([tiles[n].astype(np.float32) for n in CN] + [np.tile(inv[None], (128, 1))], axis=1)


PRM = {}
_n = 0
for _name, _k in ([("norm_mix_g", 8), ("shift_mu", 14), ("sb_out_g", 4), ("w0", 4), ("a0", 4), ("k_k", 4), ("k_a", 4),
                   ("r_k", 4), ("ln_w", 4), ("ln_b", 4), ("norm_ffn_g", 8)]
                  + [(f"{a}{l}", b) for l in range(2) for a, b in (
                      ("ffn1_norm", 8), ("mix_norm", 8), ("conv_w", 60), ("conv_b", 12), ("ssd_norm", 8), ("ssd_d", 8),
                      ("q_norm", 2), ("kv_norm", 1), ("out_norm", 4), ("cw", 12), ("conv_out", 4), ("ffn2_norm", 8))]):
    PRM[_name] = _n
    _n += _k
NPRM = _n
ROW = {"router_b": 0}
for _l in range(2):
    ROW.update({f"dt_bias{_l}": 36 + 256 * _l, f"a_log{_l}": 68 + 256 * _l, f"qk_g{_l}": 100 + 256 * _l})
NROW = 36 + 512


class Sem:

    def __init__(self, sem):
        self.sem, self.n = sem, 0


class Queue(Sem):

    def __init__(self, sem):
        super().__init__(sem)
        self.items, self.seen = [], {}

    def need(self, *toks):
        for t in toks:
            if t is None:
                continue
            if isinstance(t, list):
                self.need(*t)
                continue
            s, v = t
            if self.seen.get(s, 0) < v:
                self.seen[s] = v
                self.items.append((s.sem, v))

    def raw(self, fn, *toks):
        self.need(*toks)
        self.items.append((fn, None, 0))

    def op(self, fn, *toks):
        self.need(*toks)
        self.n += 1
        self.items.append((fn, self.sem, 1))
        return (self, self.n)

    def dma(self, out, in_, sem, *toks):
        self.need(*toks)
        sem.n += 16
        self.items.append((lambda e: e.dma_start(out, in_), sem.sem, 16))
        return (sem, sem.n)

    def emit(self, e):
        for it in self.items:
            if len(it) == 2:
                e.wait_ge(it[0], it[1])
            else:
                ins = it[0](e)
                if it[1] is not None:
                    ins.then_inc(it[1], it[2])

    def tt(self, out, a, b, op, *toks):
        return self.op(lambda e: e.tensor_tensor(out, a, b, op), *toks)

    def ts(self, out, a, s1, s2, op0, op1, *toks):
        if s2 is None:
            return self.op(lambda e: e.tensor_scalar(out, a, s1, None, op0), *toks)
        return self.op(lambda e: e.tensor_scalar(out, a, s1, s2, op0, op1), *toks)

    def stt(self, out, a, s, b, op0, op1, *toks):
        return self.op(lambda e: e.scalar_tensor_tensor(out=out, in0=a, scalar=s, in1=b, op0=op0, op1=op1), *toks)

    def cp(self, out, a, *toks):
        return self.op(lambda e: e.tensor_copy(out, a), *toks)

    def rec(self, out, a, *toks):
        return self.op(lambda e: e.reciprocal(out, a), *toks)

    def red(self, out, a, op, *toks):
        return self.op(lambda e: e.tensor_reduce(out, a, AX.X, op), *toks)

    def set(self, out, v, *toks):
        return self.op(lambda e: e.memset(out, v), *toks)

    def act(self, out, a, func, *toks, bias=None, scale=1.0, accum=None):
        kw = {"scale": scale}
        if bias is not None:
            kw["bias"] = bias
        if accum is not None:
            kw["accum_out"] = accum
        return self.op(lambda e: e.activation(out, a, func, **kw), *toks)


def program(nc, I, out):
    MUL, ADD, SUB, MAX = ALU.mult, ALU.add, ALU.subtract, ALU.max
    with ExitStack() as ctx:
        def sb(name, n, dt=F32):
            return ctx.enter_context(nc.sbuf_tensor(name, [128, n], dt))

        def sem(name):
            return ctx.enter_context(nc.semaphore(name))

        with nc.sbuf_tensor("ring", [128, NR * SLOT], F32) as ring:
            pass
        rlo = sb("rlo", NR * SLOT, F32R)
        xtok_ = sb("xtok", 2048)
        rhi = sb("rhi", NS * SLOT, F32R)
        xnh_ = sb("xnh", 2048, F32R)
        xnl_ = sb("xnl", 2048, F32R)
        cst = sb("cst", len(CN) * 128 + 16)
        prm = sb("prm", NPRM)
        row = sb("row", NROW)
        small = sb("small", 256)
        comb_ = sb("comb", 64)
        rope_ = sb("rope", 192)
        posi = sb("posi", 2, I32)
        with nc.sbuf_tensor("arena", [128, ARENA], F32) as arena:
            pass
        hhi_ = sb("hhi", 5632, F32R)
        hlo_ = sb("hlo", 5632, F32R)
        sg_ = sb("sg", 1024)
        hf_ = sb("hf", 1024)
        xnt_ = sb("xnt", 2048)
        ftmp = sb("ftmp", 2048)
        PS = [ctx.enter_context(nc.psum_tensor(f"ps{i}", [128, 512], F32)) for i in range(8)]
        xtok = xtok_[:, :].rearrange("p (t d) -> p t d", t=2)
        xnh, xnl = (x[:, :].rearrange("p (c t) -> p c t", c=8) for x in (xnh_, xnl_))
        f32 = lambda v: v.bitcast(F32)

        T, V, A, G, L = (Queue(sem(f"s_{n}")) for n in ("pe", "dve", "act", "pool", "sp"))
        d0 = Sem(sem("d_first"))
        dslot = [Sem(sem(f"d_slot{i}")) for i in range(NR)]
        dout = Sem(sem("d_out"))
        free = [[] for _ in range(8)]

        def C(name, n=128):
            return cst[:, CN[name] * 128:CN[name] * 128 + n]

        invf = cst[:, len(CN) * 128:len(CN) * 128 + 16]

        def pr(name, i=0, n=1):
            return prm[:, PRM[name] + i:PRM[name] + i + n]

        def ar(o, n):
            assert o + n <= ARENA, (o, n)
            return arena[:, o:o + n]

        def cols(w, a, b):
            return w.rearrange("(c p) n -> p c n", p=128)[:, :, a:b]

        def rows(w, a, b):
            return w.rearrange("(c p) n -> p c n", p=128)[:, a:b, :]

        loads = []

        def plan(*parts, split=True):
            n = len(loads)
            s = n % NR
            off, shapes, dmas = 0, [], []
            for src in parts:
                k, a, b = src.shape
                dmas.append((ring[0:k, s * SLOT + off:s * SLOT + off + a * b].rearrange("p (a b) -> p a b", a=a), src))
                shapes.append((off, a, b))
                off += a * b
            assert off <= SLOT
            dslot[s].n += 16 * len(parts)
            loads.append({"dmas": dmas, "sem": dslot[s], "tok": (dslot[s], dslot[s].n), 
                          "split": split, "shapes": shapes, "n": off, "at": n, "done": None, "ready": None})

        w_in = I["w_in"][0]
        for a in [3072] + list(range(1536, 3072, 256)) + list(range(0, 1536, 256)):
            plan(cols(w_in, a, a + 256))
        for a in range(0, 8, 2):
            plan(rows(I["w_out"][0], a, a + 2))
        plan(I["router"].rearrange("p (c n) -> p c n", c=8))
        for e in range(33):
            if e < 32:
                plan(cols(I["exp_w_gate"][0, e], 0, 256))
                plan(cols(I["exp_w_up"][0, e], 0, 256))
            if e:
                plan(rows(I["exp_w_down"][0, e - 1], 0, 2))

        def plan_ffn(wg_, wu_, wd_):
            for a in range(0, 2816, 256):
                plan(cols(wg_, a, a + 256))
                plan(cols(wu_, a, a + 256))
            for a in range(0, 22, 2):
                plan(rows(wd_, a, a + 2))

        for l in range(2):
            plan_ffn(I["ffn1_w_gate_2"][l], I["ffn1_w_up_2"][l], I["ffn1_w_down_2"][l])
            w = I["w_in_2"][l]
            for a in range(1024, 2560, 256):
                plan(cols(w, a, a + 256))
            plan(cols(w, 2592, 2848))
            wkv = I[f"wkv{l}"]
            plan(*(wkv[:, a:b].rearrange("p (c n) -> p c n", c=8) for a, b in ((0, 1024), (1024, 1536))))
            for a in range(3008, 3520, 256):
                plan(cols(w, a, a + 256))
            plan(rows(I["mla_w_uq_2"][l], 0, 2), split=False)
            plan(rows(I["mla_w_ukv_2"][l], 0, 1), split=False)
            for a in list(range(3520, 4544, 256)) + list(range(0, 1024, 256)):
                plan(cols(w, a, a + 256))
            for a in W_OUT_ORDER[::2]:
                plan(rows(I["w_out_2"][l], a, a + 2))
            plan_ffn(I["ffn2_w_gate_2"][l], I["ffn2_w_up_2"][l], I["ffn2_w_down_2"][l])

        split_loads = [x for x in loads if x["split"]]

        def prepare(n):
            if n >= len(loads) or not loads[n]["split"] or loads[n]["ready"]:
                return
            k = split_loads.index(loads[n])
            ld = split_loads[k]
            n, o, s = ld["n"], k % NS * SLOT, ld["at"] % NR * SLOT
            before = split_loads[k - NS]["done"] if k >= NS else None
            assert before or k < NS
            toks, mid = [], min(n, DVE_PART)
            for a, b in ((0, mid), (mid, n)):
                if a == b:
                    continue
                hi, lo, raw = rhi[:, o + a:o + b], rlo[:, s + a:s + b], ring[:, s + a:s + b]
                t = A.act(hi, raw, ACT.Copy, ld["tok"], before)
                q = G if a else V
                toks += [t, q.tt(lo, raw, f32(hi), ALU.subtract, t, ld["tok"], before)]
            ld["ready"] = toks
            ld["hi"] = [rhi[:, o + a:o + a + x * y].rearrange("p (a b) -> p a b", a=x) for a, x, y in ld["shapes"]]
            ld["lo"] = [rlo[:, s + a:s + a + x * y].rearrange("p (a b) -> p a b", a=x) for a, x, y in ld["shapes"]]

        turn = {"n": 0}

        def take():
            n = turn["n"]
            turn["n"] += 1
            prepare(n)
            for i in [i for i in range(n + 1, min(n + NR, len(loads))) if loads[i]["split"]][:NS - 1]:
                prepare(i)
            T.need(loads[n]["ready"] if loads[n]["split"] else loads[n]["tok"])
            return loads[n]

        def done(ld, p):
            ld["done"] = p

        def mm(out_, lhsT, rhs, start, stop, *toks, sig=False):
            fn = lambda e: e.matmul(out_, lhsT, rhs, start=start, stop=stop, skip_group_check=True)
            if sig:
                return T.op(fn, *toks)
            T.raw(fn, *toks)
            return None

        def tr(out_, in_, *toks, sig=False):
            idn = C("ident")[0:in_.shape[0], 0:in_.shape[0]]
            fn = lambda e: e.transpose(out_, in_, idn)
            if sig:
                return T.op(fn, *toks)
            T.raw(fn, *toks)
            return None

        x_in = L.dma(xtok, I["x"].rearrange("(t p) d -> p t d", p=128), Sem(sem("d_x")))
        L.dma(cst[:, 0:128], I["cst"][:, 0:128], d0)
        first = L.dma(prm[:, :], I["prm"], d0)
        for q in (T, V, A, G):
            q.need(first)
        wl2, wg2 = ar(18468, 512)[:, None, :], ar(18980, 512)[:, None, :]
        later = [(cst[:, 128:], I["cst"][:, 128:]), (row[:, :], I["rowp"]), (posi[:, :], I["positions"]),
                 (wl2[:, 0], I["w2a2"]), (wg2[:, 0], I["rw_g2"][0])]
        d_later = Sem(sem("d_later"))
        d_later.n = 16 * len(later)

        def rstd(out_, ssq, n, eps, *toks):
            t = V.ts(out_, ssq, 1.0 / n, eps, MUL, ADD, *toks)
            t = A.act(out_, out_, ACT.Sqrt, t)
            return V.rec(out_, out_, t)

        warm = [None]

        def sqrt_table():
            warm[0] = A.act(small[:, 240:241], C("ident", 1), ACT.Sqrt, warm[0])

        def norm_T(gname, xn_, toks=(None, None), ahead=None):
            xn = xn_.rearrange("p (t d) -> p t d", t=2)
            ss = small[:, 0:2]
            sqrt_table()
            sq = [A.act(xn[:, tt], xtok[:, tt], ACT.Square, toks[tt], accum=ss[:, tt:tt + 1]) for tt in range(2)]
            t = rstd(ss, ss, 1024, 1e-6, *sq)
            xs_t = [V.ts(xn[:, tt], xtok[:, tt], ss[:, tt:tt + 1], None, MUL, None, t) for tt in range(2)]
            if ahead is not None:
                prepare(ahead)
            res = [[], []]
            for hb in range(2):
                for tt in range(2):
                    b, s = hb * 2 + tt, slice(tt * 128, tt * 128 + 128)
                    T.need(xs_t[tt], *free[b])
                    for k in range(4):
                        c = hb * 4 + k
                        p = tr(PS[b][:, k * 128:k * 128 + 128], xn[:, tt, c * 128:c * 128 + 128], sig=(k == 3))
                    for k in range(4):
                        c = hb * 4 + k
                        eh = A.act(xnh[:, c, s], PS[b][:, k * 128:k * 128 + 128], ACT.Copy, p, scale=pr(gname, c))
                    for k in range(4):
                        c = hb * 4 + k
                        e = V.stt(xnl[:, c, s], PS[b][:, k * 128:k * 128 + 128], pr(gname, c), f32(xnh[:, c, s]), MUL, SUB, eh)
                    free[b] = [e]
                    res[hb] += [eh, e]
            return res

        def mm3(out_, lh, ll, rh, rl, start, stop, sig=False):
            mm(out_, lh, rh, start, False)
            mm(out_, lh, rl, False, False)
            return mm(out_, ll, rh, False, stop, sig=sig)

        def proj_T(ld, c0, bank, half, last, *toks, part=0):
            if half == 0:
                T.need(*free[bank])
            wh, wl = ld["hi"][part], ld["lo"][part]
            for c in range(8):
                T.need(*toks[c // 4:c // 4 + 1])
                p = mm3(PS[bank][:, half * 256:half * 256 + 256], wh[:, c, c0:c0 + 128], wl[:, c, c0:c0 + 128],
                        xnh[:, c, :], xnl[:, c, :], c == 0, c == 7, sig=(c == 7))
            if last:
                done(ld, p)
            return p

        def proj_tok(o, ld, part, tt, a, n, first, stop):
            s = slice(128 * tt, 128 * tt + 128)
            for c in range(8):
                p = mm3(o, xnh[:, c, s], xnl[:, c, s], ld["hi"][part][:, c, a:a + n], ld["lo"][part][:, c, a:a + n],
                        first and c == 0, stop and c == 7, sig=(c == 7))
            return p

        def down(ld, k0, nk, hh, hl, k_of=lambda k: k, needs=None):
            for i in range(2):
                k = k0 + i
                if needs:
                    T.need(*needs[k])
                for tt in range(2):
                    s = slice(128 * tt, 128 * tt + 128)
                    for dh in range(2):
                        d = slice(512 * dh, 512 * dh + 512)
                        p = mm3(PS[4 + 2 * tt + dh][:, :], hh[:, k_of(k), s], hl[:, k_of(k), s], ld["hi"][0][:, i, d], ld["lo"][0][:, i, d],
                                k == 0, k == nk - 1, sig=True)
            done(ld, p)
            return p

        def parts_of(hi, lo, v, *toks):
            t = A.act(hi, v, ACT.Copy, *toks)
            return [t, V.tt(lo, v, f32(hi), SUB, t)]

        def add_x(p, scale=1.0):
            res = []
            for b in range(4):
                o = xtok[:, b // 2, (b % 2) * 512:(b % 2) * 512 + 512]
                e = V.stt(o, PS[4 + b][:, :], scale, o, MUL, ADD, p)
                free[4 + b] = [e]
                res.append(e)
            return res[0:2], res[2:4]

        xn_t = norm_T("norm_mix_g", ar(8212, 2048), (x_in, x_in), ahead=0)

        urw = ar(0, 3598).rearrange("p (f t) -> p f t", f=14)
        um = ar(3600, 3584).rearrange("p (f t) -> p f t", f=14)
        Cc = ar(7184, 1028).rearrange("p (f t) -> p f t", f=4)
        EP = ar(8212, 1032).rearrange("p (f c t) -> p f c t", f=4, c=2)
        EN = ar(9244, 1032).rearrange("p (f c t) -> p f c t", f=4, c=2)
        v4 = lambda o: ar(o, 1024).rearrange("p (f t) -> p f t", f=4)
        aT, kkT, rT, zT, bT, kT, gT = (v4(o) for o in (10276, 11300, 12324, 13348, 14372, 15396, 16420))
        Vtok = ar(17444, 1024).rearrange("p (c n) -> p c n", c=2)
        BK = ar(18468, 1024).rearrange("p (c n) -> p c n", c=2)
        AT = ar(19492, 2048).rearrange("p (q t) -> p q t", q=16)
        X = ar(21540, 2048).rearrange("p (q t) -> p q t", q=16)
        XT = ar(23588, 2048).rearrange("p (q t) -> p q t", q=16)
        Y = ar(0, 2048).rearrange("p (q t) -> p q t", q=16)
        M = ar(2048, 1536).rearrange("p (b q t) -> p b q t", b=3, q=4)
        tmp = [v4(0), v4(1024), v4(2048)]
        qk = ar(19492, 2048).rearrange("p (f t) -> p f t", f=8)
        vtok = ar(21540, 1024).rearrange("p (c n) -> p c n", c=2)
        sbe = ar(22564, 1536).rearrange("p (b t) -> p b t", b=4)
        sbo = ar(24868, 1024).rearrange("p (f t) -> p f t", f=4)

        z0 = V.set(urw[:, :, 0:1], 0.0)
        um_t = [None] * 14
        nb = 0
        for f in [12, 0, 2, 4, 6, 8, 10]:
            ld = take()
            b = 4 + nb % 4
            nb += 1
            proj_T(ld, 0, b, 0, False, *xn_t)
            p = proj_T(ld, 128, b, 1, True)
            e = A.act(urw[:, f:f + 2, 1:257], PS[b][:, :].rearrange("p (f t) -> p f t", f=2), ACT.Copy, p)
            free[b] = [e]
            for ff in (f, f + 1):
                t = G.tt(um[:, ff], urw[:, ff, 0:256], urw[:, ff, 1:257], SUB, e, z0)
                um_t[ff] = V.stt(um[:, ff], um[:, ff], pr("shift_mu", ff), urw[:, ff, 1:257], MUL, ADD, t)
        for q in (T, V, A, G):
            q.need((d_later, d_later.n))
        qk_t, vt_t, prj = [None] * 8, [], {"i": 0, "nb": nb}

        def sb_proj():
            i = prj["i"]
            prj["i"] += 1
            ld = take()
            b = 4 + prj["nb"] % 4
            prj["nb"] += 1
            if i < 4:
                f = 2 * i
                proj_T(ld, 0, b, 0, False)
                p = proj_T(ld, 128, b, 1, True)
                e = A.act(qk[:, f:f + 2, :], PS[b][:, :].rearrange("p (f t) -> p f t", f=2), ACT.Copy, p,
                          scale=0.125 if f < 4 else 1.0)
                qk_t[f] = qk_t[f + 1] = e
            else:
                half = i - 4
                T.need(*free[b])
                for tt in range(2):
                    p = proj_tok(PS[b][:, 256 * tt:256 * tt + 256], ld, 0, tt, 0, 256, tt == 0, tt == 1)
                e = A.act(vtok[:, :, 256 * half:256 * half + 256], PS[b][:, :].rearrange("p (t n) -> p t n", t=2), ACT.Copy, p)
                vt_t.append(e)
                done(ld, p)
                prj["p"] = p
            free[b] = [e]

        def head_rstd(src, b0, bs, s1, s2, op0, op1, *toks):
            sel = C("bones")[:, 0:128:64]
            T.need(*toks, *free[b0])
            for tt in range(2):
                for f in range(4):
                    p = mm(PS[b0][:, 8 * tt + 2 * f:8 * tt + 2 * f + 2], src[:, f, 128 * tt:128 * tt + 128], sel, tt + f == 0, tt + f == 4, sig=(tt + f == 4))
            r = small[:, 200:216]
            t = V.ts(r, PS[b0][:, 0:16], s1, s2, op0, op1, p)
            free[b0] = [t]
            t = A.act(r, r, ACT.Sqrt, t)

            def spread():
                t2 = V.rec(r, r, t)
                res = []
                for half in range(2):
                    T.need(t2, *free[bs[half]])
                    for k in range(2):
                        for tt in range(2):
                            for hh in range(2):
                                h = 8 * tt + 2 * (2 * half + k) + hh
                                p = mm(PS[bs[half]][64 * hh:64 * hh + 64, 256 * k + 128 * tt:256 * k + 128 * tt + 128],
                                       r[:, h:h + 1].to_broadcast([128, 64]), C("ident"), True, True, sig=True)
                    res.append(p)
                return res
            return spread

        sq2 = ar(22564, 1024).rearrange("p (f t) -> p f t", f=4)
        so_t, ex_t, sp_t, w_t, pv_t = [], {}, {}, {}, {}
        zb = [4, 5, 0, 7]
        sb_at, sbx = {"h": 0}, {}

        def sb_scores(h):
            j, po, i = h // 2, 64 * (h % 2), h % 4
            b = zb[i]
            q, k, z = qk[po:po + 64, j], qk[po:po + 64, 4 + j], PS[b][:, 0:384]
            T.need(qk_t[j], qk_t[4 + j], *free[b])
            mm(PS[b][:, 0:256], k[:, 0:128], q, True, False)
            mm(PS[b][:, 256:384], k[:, 128:256], q[:, 128:256], False, False)
            mm(PS[b][:, 0:128], C("ident"), C("mnegs"), False, False)
            p = mm(PS[b][:, 256:384], C("ident"), C("mnegs"), False, True, sig=True)
            t = A.act(sbe[:, i], z, ACT.Abs, p, pv_t.get(h - 4))
            ex_t[h] = A.act(sbe[:, i], sbe[:, i], ACT.Exp, t, scale=-1.0)

        def sb_rest(h):
            i = h % 4
            t = A.act(sbe[:, i], sbe[:, i], ACT.Ln, ex_t[h], bias=1.0)
            sp_t[h] = V.stt(sbe[:, i], PS[zb[i]][:, 0:384], 0.0, sbe[:, i], MAX, ADD, t)

        def sb_weights(h):
            i = h % 4
            b = zb[i]
            T.need(sp_t[h])
            mm(PS[b][:, 0:256], C("ntri"), sbe[:, i, 0:256], False, False)
            mm(PS[b][:, 128:256], C("nones"), sbe[:, i, 256:384], False, False)
            p = mm(PS[b][:, 256:384], C("ntri"), sbe[:, i, 256:384], False, True, sig=True)
            w_t[h] = A.act(sbe[:, i], PS[b][:, 0:384], ACT.Exp, p, sp_t[h])
            free[b] = [w_t[h]]

        def sb_values(h):
            j, po, i, ob = h // 2, 64 * (h % 2), h % 4, 6
            T.need(w_t[h], *vt_t)
            if po == 0:
                T.need(*free[ob])
            hs = slice(h * 64, h * 64 + 64)
            mm(PS[ob][po:po + 64, 0:256], vtok[:, 0, hs], sbe[:, i, 0:256], True, False)
            pv_t[h] = mm(PS[ob][po:po + 64, 128:256], vtok[:, 1, hs], sbe[:, i, 256:384], False, True, sig=True)
            if po:
                t = A.act(sbo[:, j], PS[ob][:, 0:256], ACT.Copy, pv_t[h])
                free[ob] = [t]
                so_t.append(t)

        def sb_step():
            h = sb_at["h"]
            sb_at["h"] += 1
            if h < 5:
                now, last = (2 * h, 2 * h + 1) if h < 4 else (), (2 * h - 2, 2 * h - 1) if h else ()
                for x in now:
                    sb_scores(x)
                for x in last:
                    sb_weights(x)
                for x in now:
                    sb_rest(x)
                for x in last:
                    sb_values(x)
            if h == 5:
                sbx["s2"] = A.act(sq2, sbo, ACT.Square, *so_t, *pv_t.values())
            if h == 6:
                sbx["r"] = head_rstd(sq2, 4, (5, 6), 1.0 / 64, 1e-6, MUL, ADD, sbx["s2"])
            if h == 7:
                t = sbx["r"]()
                mt = [V.stt(sbo[:, f], sbo[:, f], pr("sb_out_g", f), PS[5 + f // 2][:, 256 * (f % 2):256 * (f % 2) + 256], MUL, MUL, t[f // 2], sbx["s2"])
                      for f in range(4)]
                free[5], free[6] = [mt[1]], [mt[3]]
                sbx["mt"] = parts_of(xnh[:, 0:4], xnl[:, 0:4], sbo, *mt, prj["p"])

        th = tmp[0][:, 0]
        t = A.act(th[0:64], um[0:64, 12], ACT.Tanh, *um_t)
        sgx = tmp[0][:, 1]
        e1 = A.act(sgx, um[:, 13], ACT.Sigmoid)
        sb_proj()
        lor = []
        for half in range(2):
            b = 1 + half
            T.need(t, *free[b])
            for k in range(2):
                f = half * 2 + k
                p = mm(PS[b][:, k * 256:k * 256 + 256], wl2[0:64, 0, f * 128:f * 128 + 128], th[0:64], True, True, sig=(k == 1))
            for k in range(2):
                f = half * 2 + k
                e = A.act(tmp[1][:, f], PS[b][:, k * 256:k * 256 + 256], ACT.Sigmoid, p, bias=pr("w0", f))
            free[b] = [e]
            lor.append(e)
        for half in range(2):
            b = (3, 1)[half]
            T.need(*free[b])
            for k in range(2):
                f = half * 2 + k
                p = mm(PS[b][:, k * 256:k * 256 + 256], wl2[64:128, 0, f * 128:f * 128 + 128], um[64:128, 12], True, True, sig=(k == 1))
            for k in range(2):
                f = half * 2 + k
                at = A.act(aT[:, f], PS[b][:, k * 256:k * 256 + 256], ACT.Sigmoid, p, bias=pr("a0", f))
            free[b] = [at]
        sb_proj()
        sb_proj()
        gt = []
        for half in range(2):
            b = 1 + half
            T.need(e1, *free[b])
            for k in range(2):
                f = half * 2 + k
                p = mm(PS[b][:, k * 256:k * 256 + 256], wg2[:, 0, f * 128:f * 128 + 128], sgx, True, True, sig=(k == 1))
            e = A.act(gT[:, 2 * half:2 * half + 2, :], PS[b][:, :].rearrange("p (f t) -> p f t", f=2), ACT.Copy, p)
            free[b] = [e]
            gt.append(e)
        lora_done = p
        sb_proj()
        lw = lor
        c0 = V.set(Cc[:, :, 0:1], 0.0)
        ct = []
        on256 = V.set(tmp[2][:, 0], 1.0, *um_t)
        for f in range(4):
            ct.append(V.op(lambda e, f=f: e.tensor_tensor_scan(Cc[:, f, 1:257], tmp[2][:, 0], tmp[1][:, f], 0.0, MUL, ADD), lw, on256))
        sb_proj()
        dt_ = []
        for c in range(2):
            cm = Cc[:, :, 64 + 128 * c:65 + 128 * c].to_broadcast([128, 4, 129])
            dt_.append(V.tt(EP[:, :, c, :], Cc[:, :, 128 * c:128 * c + 129], cm, SUB, *ct, c0))
        en = A.act(EN, EP, ACT.Exp, *dt_, scale=KAP)
        ep = A.act(EP, EP, ACT.Exp, en, scale=-KAP)
        sb_proj()
        sct = V.tt(small[:, 16:20], Cc[:, :, 192:193].rearrange("p f a -> p (f a)"), Cc[:, :, 64:65].rearrange("p f a -> p (f a)"), SUB, *ct)
        sct = A.act(small[:, 16:20], small[:, 16:20], ACT.Exp, sct, scale=-KAP)

        kkr = []
        for f in range(4):
            kkr.append(V.ts(kkT[:, f], um[:, 4 + f], pr("k_k", f), None, MUL, None))
        sq = A.act(tmp[2], kkT, ACT.Square, *kkr, *ct)
        sb_step()
        kn = head_rstd(tmp[2], 2, (3, 1), 1e-24, None, MAX, None, sq)
        sb_step()
        kn = kn()
        kkt = [V.tt(kkT[:, 2 * i:2 * i + 2], kkT[:, 2 * i:2 * i + 2], PS[b][:, :].rearrange("p (f t) -> p f t", f=2), MUL, kn[i], sq)
               for i, b in enumerate((3, 1))]
        free[3], free[1] = [kkt[0]], [kkt[1]]
        sb_step()
        km = []
        for f in range(4):
            t = V.ts(tmp[2][:, f], aT[:, f], 1.0, pr("k_a", f), SUB, MUL, at, kn)
            km.append(V.stt(um[:, 4 + f], tmp[2][:, f], 1.0, um[:, 4 + f], ADD, MUL, t, *kkr))
        sb_step()
        ch = lambda x: x.rearrange("p f (c t) -> p f c t", c=2)
        zt, rt, bt, kt = [], [], [], []
        ba = V.tt(aT, aT, kkT, MUL, kkt, *km)
        for c in range(2):
            s = slice(128 * c, 128 * c + 128)
            zt.append(V.stt(zT[:, :, s], kkT[:, :, s], -1.0, EP[:, :, c, 0:128], MUL, MUL, kkt, ep))
            rt.append(G.tt(rT[:, :, s], um[:, 0:4, s], EP[:, :, c, 1:129], MUL, ep))
            bt.append(V.tt(bT[:, :, s], aT[:, :, s], EN[:, :, c, 1:129], MUL, ba, en))
            kt.append(V.tt(kT[:, :, s], um[:, 4:8, s], EN[:, :, c, 1:129], MUL, en, *km))
        sb_step()
        bo = G.tt(tmp[0], um[:, 0:4], um[:, 4:8], MUL, *km, gt)
        bb = []
        for f in range(4):
            bb.append(V.ts(tmp[0][:, f], tmp[0][:, f], pr("r_k", f), None, MUL, None, bo))
        sb_step()
        bon = []
        for half in range(2):
            b = 1 + half
            T.need(*bb, *free[b])
            p = mm(PS[b][:, :], C("bones"), tmp[0][:, 2 * half:2 * half + 2], True, True, sig=True)
            e = V.tt(um[:, 4 + 2 * half:6 + 2 * half], PS[b][:, :].rearrange("p (f t) -> p f t", f=2),
                     um[:, 8 + 2 * half:10 + 2 * half], MUL, p, bo, *kt)
            free[b] = [e]
            bon.append(e)
        sb_step()
        tk = []
        for c in range(2):
            b = (3, 1)[c]
            T.need(*free[b])
            for f in range(4):
                p = tr(PS[b][:, f * 128:f * 128 + 128], um[:, 8 + f, c * 128:c * 128 + 128], sig=(f == 3))
            e = A.act(Vtok[:, c, :], PS[b][:, :], ACT.Copy, p)
            free[b] = [e]
            tk.append(e)
        for c, (src, st) in enumerate(((bT, bt), (kT, kt))):
            b = 2 + c
            T.need(*st, *free[b])
            for f in range(4):
                p = tr(PS[b][:, f * 128:f * 128 + 128], src[:, f, 0:128], sig=(f == 3))
            e = A.act(BK[:, c, :], PS[b][:, :], ACT.Copy, p, lora_done)
            free[b] = [e]
            tk.append(e)

        while sb_at["h"] < 5:
            sb_step()
        at_t = []
        for g in range(4):
            c, par = g // 2, g % 2
            b = g
            T.need(*zt, *bt, *free[b])
            for i in range(4):
                po, s = 64 * par, slice(128 * c, 128 * c + 128)
                p = mm(PS[b][:, i * 128:i * 128 + 128], bT[po:po + 64, i, s], zT[po:po + 64, i, s], True, True, sig=(i == 3))
            ms = C("ms")[:, None, :].to_broadcast([128, 4, 128])
            e = V.tt(AT[:, 4 * g:4 * g + 4], PS[b][:, :].rearrange("p (q t) -> p q t", q=4), ms, MUL, p, *pv_t.values())
            free[b] = [e]
            at_t.append(e)
        while sb_at["h"] < 8:
            sb_step()
        mt = sb_done = sbx["mt"]
        idb = C("ident")[:, None, :].to_broadcast([128, 4, 128])
        p3 = lambda b: PS[b][:, :].rearrange("p (q t) -> p q t", q=4)
        x_t = [[] for _ in range(4)]
        y_r = [[] for _ in range(4)]
        m_r = [[] for _ in range(3)]
        units = [(li, g) for li in range(len(LEVELS)) for g in range(4)]
        m_t, yt = {}, {}

        def mask_level(u):
            li, g = units[u]
            lv = C(f"lv{LEVELS[li]}")[:, None, :].to_broadcast([128, 4, 128])
            m_t[u] = G.tt(M[:, u % 3], AT[:, 4 * g:4 * g + 4], lv, MUL, at_t[g], *m_r[u % 3], *bon)

        def level_y(u):
            li, g = units[u]
            gs, b0, Mb = slice(4 * g, 4 * g + 4), (g % 2) * 3, M[:, u % 3]
            T.need(m_t[u], *x_t[g], *free[b0])
            for i in range(4):
                p = mm(PS[b0][:, i * 128:i * 128 + 128], Mb[:, i], C("ident") if li == 0 else X[:, 4 * g + i], True, True, sig=(i == 3))
            m_r[u % 3] = [p]
            if li == 0:
                e1 = V.tt(X[:, gs], p3(b0), idb, ADD, p, *sb_done)
                e2 = V.tt(XT[:, gs], Mb, idb, ADD, m_t[u], *sb_done)
                m_r[u % 3].append(e2)
                free[b0] = [e1]
                x_t[g] = [e1, e2]
                return
            yt[u] = A.act(Y[:, gs], p3(b0), ACT.Copy, p, *y_r[g])
            free[b0] = [yt[u]]

        def level_x(u):
            li, g = units[u]
            lastl = li == len(LEVELS) - 1
            gs, b1, b2 = slice(4 * g, 4 * g + 4), (g % 2) * 3 + 1, (g % 2) * 3 + 2
            T.need(yt[u], *free[b1], *free[b2])
            if not lastl:
                for i in range(4):
                    q = 4 * g + i
                    p1 = mm(PS[b1][:, i * 128:i * 128 + 128], XT[:, q], Y[:, q], True, True, sig=(i == 3))
            for i in range(4):
                q = 4 * g + i
                p2 = mm(PS[b2][:, i * 128:i * 128 + 128], Y[:, q], XT[:, q], True, True, sig=(i == 3))
            y_r[g] = [p2]
            x_t[g] = []
            if not lastl:
                e1 = V.tt(X[:, gs], p3(b1), X[:, gs], ADD, p1)
                free[b1] = [e1]
                x_t[g].append(e1)
            e2 = V.tt(XT[:, gs], p3(b2), XT[:, gs], ADD, p2)
            free[b2] = [e2]
            x_t[g].append(e2)

        mask_level(0)
        for u in range(len(units) + 1):
            if u + 1 < len(units):
                mask_level(u + 1)
            if u < len(units):
                level_y(u)
            if u and units[u - 1][0]:
                level_x(u - 1)

        GT = ar(8212, 2048).rearrange("p (k q t) -> p k q t", k=4, q=4)
        RHS = ar(10276, 1024).rearrange("p (c q n) -> p c q n", c=2, q=8)
        U = ar(0, 1024).rearrange("p (c q n) -> p c q n", c=2, q=8)
        S0 = ar(1024, 256).rearrange("p (f n) -> p f n", f=4)
        oT = kkT
        o_t = []
        s0_t = []
        msb = C("ms")[:, None, :].to_broadcast([128, 4, 128])
        mib = C("triu")[:, None, :].to_broadcast([128, 4, 128])
        GTs = [GT, ar(19492, 2048).rearrange("p (k q t) -> p k q t", k=4, q=4)]
        gr = [[], []]
        gt_of, ut = {}, {}
        fb = lambda x, h, s: x[64 * (h % 2):64 * (h % 2) + 64, h // 2, s]

        def unit(u):
            c, hg = u // 2, u % 2
            return c, hg, [2 * i + hg for i in range(4)], slice(128 * c, 128 * c + 128)

        def masked(u):
            c, hg, hh, s = unit(u)
            gt_of[u] = []
            for k, l_, r_, mk in ((0, kT, zT, msb), (1, kT, rT, mib), (2, bT, rT, mib)):
                T.need(*kt, *rt, *free[k], *x_t[u])
                for i, h in enumerate(hh):
                    p = mm(PS[k][:, i * 128:i * 128 + 128], fb(l_, h, s), fb(r_, h, s), True, True, sig=(i == 3))
                e = V.tt(GTs[u % 2][:, k], p3(k), mk, MUL, p, *gr[u % 2], *zt, *bt, *rt, *kt, *x_t[0], *x_t[1], *x_t[2], *x_t[3])
                free[k] = [e]
                gt_of[u].append(e)

        def solve(u):
            c, hg, hh, s = unit(u)
            po, gt_, Gu = 64 * hg, gt_of[u], GTs[u % 2]
            b = 3
            T.need(gt_[0], *tk, *s0_t, *free[b])
            for i, h in enumerate(hh):
                o = PS[b][:, i * 64:i * 64 + 64]
                p = mm(o, Gu[:, 0, i], Vtok[:, c, h * 64:h * 64 + 64], i == 0, c == 0 and i == 3, sig=(c == 0 and i == 3))
                if c == 1:
                    p = mm(o, fb(zT, h, s), S0[po:po + 64, h // 2], False, i == 3, sig=(i == 3))
            rhs_t = A.act(RHS[:, c, 4 * hg:4 * hg + 4], PS[b][:, 0:256].rearrange("p (q n) -> p q n", q=4), ACT.Copy, p, *bt)
            free[b] = [rhs_t]
            if u < 3:
                masked(u + 1)
            b = 4
            T.need(rhs_t, *free[b])
            for i, h in enumerate(hh):
                p = mm(PS[b][:, i * 64:i * 64 + 64], XT[:, 4 * u + i], RHS[:, c, 4 * hg + i], True, True, sig=(i == 3))
            ut[u] = A.act(U[:, c, 4 * hg:4 * hg + 4], PS[b][:, 0:256].rearrange("p (q n) -> p q n", q=4), ACT.Copy, p,
                          y_r[0], y_r[1], y_r[2], y_r[3])
            free[b] = [ut[u]]

        def outputs(u):
            c, hg, hh, s = unit(u)
            po, gt_, Gu, b = 64 * hg, gt_of[u], GTs[u % 2], 5 + hg
            T.need(ut[u], gt_[1], gt_[2], *free[b])
            for i, h in enumerate(hh):
                o = PS[b][po:po + 64, i * 128:i * 128 + 128]
                mm(o, Vtok[:, c, h * 64:h * 64 + 64], Gu[:, 1, i], i == 0, False)
                p = mm(o, U[:, c, 4 * hg + i], Gu[:, 2, i], False, c == 0 and i == 3, sig=True)
                if c == 1:
                    p = mm(o, S0[po:po + 64, h // 2], fb(rT, h, s), False, i == 3, sig=True)
            gr[u % 2] = [p]
            e = A.act(oT[po:po + 64, :, s], PS[b][po:po + 64, :].rearrange("p (j t) -> p j t", j=4), ACT.Copy, p, *zt, ba)
            free[b] = [e]
            o_t.append(e)

        def state():
            b = 7
            T.need(ut[0], ut[1], *tk, *free[b])
            for h in range(8):
                po = 64 * (h % 2)
                o = PS[b][po:po + 64, (h // 2) * 64:(h // 2) * 64 + 64]
                mm(o, BK[:, 0, h * 64:h * 64 + 64], U[:, 0, 4 * (h % 2) + h // 2], h < 2, False)
                p = mm(o, BK[:, 1, h * 64:h * 64 + 64], Vtok[:, 0, h * 64:h * 64 + 64], False, h >= 6, sig=(h == 7))
            for f in range(4):
                e = V.ts(S0[:, f], PS[b][:, f * 64:f * 64 + 64], small[:, 16 + f:17 + f], None, MUL, None, p, sct, *y_r)
                s0_t.append(e)
            free[b] = [e]

        masked(0)
        solve(0)
        outputs(0)
        solve(1)
        state()
        outputs(1)
        solve(2)
        outputs(2)
        solve(3)
        outputs(3)

        mu = v4(12324)
        sqd = v4(13348)
        us = []
        for half in range(2):
            b = half
            hs2 = slice(2 * half, 2 * half + 2)
            T.need(*o_t, *free[b])
            p = mm(PS[b][:, :], C("bones"), oT[:, hs2], True, True, sig=True)
            e = V.stt(mu[:, hs2], PS[b][:, :].rearrange("p (f t) -> p f t", f=2), -1.0 / 64, oT[:, hs2], MUL, ADD, p)
            free[b] = [e]
            us.append(e)
        s2 = A.act(sqd, mu, ACT.Square, *us)
        T.need(*mt, *free[4], *free[5], *free[6], *free[7])
        p = down(take(), 0, 8, xnh, xnl)
        gn = head_rstd(sqd, 2, (3, 0), 1.0 / 64, 64e-5, MUL, ADD, s2)
        p = down(take(), 2, 8, xnh, xnl)
        gn = gn()
        fin = []
        for f in range(4):
            t1 = V.stt(mu[:, f], mu[:, f], pr("ln_w", f), PS[(3, 0)[f // 2]][:, 256 * (f % 2):256 * (f % 2) + 256], MUL, MUL, gn[f // 2], s2)
            free[(3, 0)[f // 2]] = [t1]
            t1 = V.stt(mu[:, f], mu[:, f], pr("ln_b", f), um[:, 4 + f], ADD, ADD, t1, *bon)
            fin.append(V.tt(mu[:, f], mu[:, f], gT[:, f], MUL, t1, *gt))
        fin = parts_of(xnh[:, 4:8], xnl[:, 4:8], mu, *fin, prj["p"])
        T.need(*fin)
        for k in (4, 6):
            p = down(take(), k, 8, xnh, xnl)
        ot = add_x(p)

        xn_t = norm_T("norm_ffn_g", xnt_[:, :], ot)
        gB = ftmp[:, 1024:2048]
        gb_t = G.dma(gB, I["final_norm_g"].rearrange("(a n) -> a n", a=1).to_broadcast([128, 1024]), Sem(sem("d_gb")), p)
        lg = ftmp[:, 0:72].rearrange("p (t n) -> p t n", t=2)
        ld = take()
        lgT = ftmp[:, 528:784]
        T.need(*free[4], *free[5])
        for c in range(8):
            T.need(xn_t[c // 4])
            p = mm3(PS[4][0:36, 0:256], ld["hi"][0][:, c], ld["lo"][0][:, c], xnh[:, c, :], xnl[:, c, :], c == 0, c == 7, sig=(c == 7))
        done(ld, p)
        lg_e = A.act(lgT[0:36], PS[4][0:36, 0:256], ACT.Copy, p)
        free[4] = [lg_e]
        lg_t = []
        comb = comb_[:, :].rearrange("p (t n) -> p t n", t=2)
        sc = ftmp[:, 128:528]
        on8 = ftmp[:, 96:128]
        t_on = V.set(on8, 1.0)
        cmb_t = []

        def logits():
            T.need(lg_e)
            for tt in range(2):
                p = tr(PS[5][:, 64 * tt:64 * tt + 36], lgT[0:36, 128 * tt:128 * tt + 128], sig=True)
            for tt in range(2):
                lg_t.append(V.tt(lg[:, tt], PS[5][:, 64 * tt:64 * tt + 36], row[:, 0:36], ADD, p))
            free[5] = [lg_t[1]]

        def router(tt):
            o, e = 200 * tt, lg_t[tt]
            gl, el = lg[:, tt, 0:4], lg[:, tt, 4:36]
            gm, gs_, ngm = sc[:, o:o + 1], sc[:, o + 1:o + 2], sc[:, o + 2:o + 3]
            ge, eq, cs, oh, pen = (sc[:, o + 4 + 4 * i:o + 8 + 4 * i] for i in range(5))
            ml, e1h, c32, m2 = (sc[:, o + 28 + 32 * i:o + 60 + 32 * i] for i in range(4))
            m1, mx2, ex, den, w1, w2s = (sc[:, o + 160 + i:o + 161 + i] for i in range(6))

            def onehot(dst, src, mx, cum, n, tk_):
                t_ = V.ts(dst, src, mx, None, ALU.is_equal, None, tk_)
                t_ = V.op(lambda e: e.tensor_tensor_scan(cum, on8[:, 0:n], dst, 0.0, MUL, ADD), t_, t_on)
                return V.stt(dst, cum, 1.0, dst, ALU.is_equal, MUL, t_)

            t = V.red(gm, gl, MAX, e)
            tg = V.ts(ngm, gm, -1.0, None, MUL, None, t)
            tg = A.act(ge, gl, ACT.Exp, tg, bias=ngm, accum=gs_)
            t = onehot(oh, gl, gm, cs, 4, t)
            t = V.ts(pen, oh, -1.0, BIG, ADD, MUL, t)
            t = V.tt(ml.rearrange("p (g n) -> p g n", g=4), el.rearrange("p (g n) -> p g n", g=4),
                     pen[:, :, None].to_broadcast([128, 4, 8]), ADD, t)
            t = V.red(m1, ml, MAX, t)
            t = onehot(e1h, ml, m1, c32, 32, t)
            t = V.stt(ml, e1h, -4.0 * BIG, ml, MUL, ADD, t)
            t = V.red(mx2, ml, MAX, t)
            t2 = onehot(m2, ml, mx2, c32, 32, t)
            t = V.tt(ex, mx2, m1, SUB, t)
            t = A.act(ex, ex, ACT.Exp, t)
            t = V.stt(den, ex, 1.0, gs_, ADD, MUL, t, tg)
            t = V.rec(w1, den, t)
            t = V.tt(w2s, ex, w1, MUL, t)
            t3 = V.ts(m2, m2, w2s, None, MUL, None, t, t2)
            cmb_t.append(V.stt(comb[:, tt], e1h, w1, m2, MUL, ADD, t3))

        hhi, hlo = (x[:, :].rearrange("p (f t) -> p f t", f=22) for x in (hhi_, hlo_))
        sg, hf = (x[:, :].rearrange("p (b f t) -> p b f t", b=2, f=2) for x in (sg_, hf_))
        hf_r = [None, None]
        last_p = [None]

        def gate_up(i, f, *reads):
            bg, bu, i = i % 2, 2 + i % 2, i % 2
            v2 = lambda b: PS[b][:, :].rearrange("p (f t) -> p f t", f=2)
            ld = take()
            proj_T(ld, 0, bg, 0, False, *xn_t)
            pg = proj_T(ld, 128, bg, 1, True)
            ld = take()
            proj_T(ld, 0, bu, 0, False)
            pu = proj_T(ld, 128, bu, 1, True)
            a = A.act(sg[:, i], v2(bg), ACT.Silu, pg, hf_r[i])
            free[bg] = [a]
            v = V.tt(hf[:, i], v2(bu), sg[:, i], MUL, pu, a, hf_r[i])
            free[bu] = [v]
            t = A.act(hhi[:, f:f + 2], hf[:, i], ACT.Copy, v, *reads)
            hf_r[i] = G.tt(hlo[:, f:f + 2], hf[:, i], f32(hhi[:, f:f + 2]), SUB, t, v, *reads)
            return [t, hf_r[i]]

        hv, hE_r = {}, [None, None]
        for ei in range(33):
            if ei < 32:
                hv[ei] = gate_up(ei, 2 * (ei % 2), hE_r[ei % 2])
            if ei == 0:
                logits()
                router(0)
                continue
            if ei == 1:
                router(1)
                moe_prev = [[c] for c in cmb_t for _ in range(2)]
            c = ei - 1
            ld = take()
            T.need(*hv[c], *free[4], *free[5], *free[6], *free[7])
            p = down(ld, 0, 2, hhi, hlo, k_of=lambda k: 2 * (c % 2) + k)
            hE_r[c % 2] = p
            for b in range(4):
                o = xtok[:, b // 2, (b % 2) * 512:(b % 2) * 512 + 512]
                e = V.stt(o, PS[4 + b][:, :], comb[:, b // 2, c:c + 1], o, MUL, ADD, p, *moe_prev[b])
                free[4 + b] = [e]
                moe_prev[b] = [e]
        ss = small[:, 32:34]
        sqrt_table()
        sq = [A.act(xnt_[:, 1024 * tt:1024 * tt + 1024], xtok[:, tt], ACT.Square, moe_prev[2 * tt], moe_prev[2 * tt + 1], accum=ss[:, tt:tt + 1]) for tt in range(2)]
        tq = rstd(ss, ss, 1024, 1e-6, *sq)
        x_now = [V.stt(xtok[:, tt], xtok[:, tt], ss[:, tt:tt + 1], gB, MUL, MUL, tq, gb_t) for tt in range(2)]

        ang, rk, rq = (rope_[:, 64 * i:64 * i + 64].rearrange("p (f t n) -> p f t n", f=2, t=2) for i in range(3))
        posf = small[:, 36:38]
        t = V.cp(posf, posi[:, :])
        for tt in range(2):
            for f in range(2):
                last = V.ts(ang[:, f, tt], invf, posf[:, tt:tt + 1], None, MUL, None, t)
        fl = lambda x: x.rearrange("p f t n -> p (f t n)")
        MAGIC = 12582912.0
        P1, P2, P3 = 6.28125, 1.9350051879882812e-3, 3.01991598195675e-7
        t = last
        tk_ = []
        for f in range(2):
            t0 = V.ts(rk[:, f], ang[:, f], 1.0 / (2 * math.pi), 0.25 if f == 0 else 0.0, MUL, ADD, t)
            t0 = V.ts(rk[:, f], rk[:, f], MAGIC, MAGIC, ADD, SUB, t0)
            tk_.append(t0)
        t = V.stt(fl(rq), fl(rk), -P1, fl(ang), MUL, ADD, *tk_)
        t = V.stt(fl(rq), fl(rk), -P2, fl(rq), MUL, ADD, t)
        t = V.stt(fl(rq), fl(rk), -P3, fl(rq), MUL, ADD, t)
        t = V.ts(rq[:, 0], rq[:, 0], math.pi / 2, None, ADD, None, t)
        t = V.ts(fl(rq), fl(rq), 3.1415925, -3.1415925, ALU.min, MAX, t)
        rope_t = A.act(fl(ang), fl(rq), ACT.Sin, t)
        cosT, sinT = ang[:, 0], ang[:, 1]

        def ffn(gname):
            nonlocal xn_t, x_now
            hf_r[0] = hf_r[1] = None
            xn_t = norm_T(gname, xnt_[:, :], x_now)
            needs = {}
            for i in range(11):
                needs[2 * i] = needs[2 * i + 1] = gate_up(i, 2 * i)
            T.need(*free[4], *free[5], *free[6], *free[7])
            for i in range(11):
                p = down(take(), 2 * i, 22, hhi, hlo, needs=needs)
            x_now = add_x(p, 0.5)
            last_p[0] = p

        def mixer(l):
            nonlocal xn_t, x_now
            N = lambda s: f"{s}{l}"
            xn_t = norm_T(N("mix_norm"), ar(16000, 2048), x_now)
            zs = ar(0, 2048).rearrange("p (f t) -> p f t", f=8)
            yT = ar(2048, 4096).rearrange("p (f t) -> p f t", f=16)
            qkl = ar(6144, 768).rearrange("p (f t) -> p f t", f=3)
            cc = ar(6912, 1032).rearrange("p (f t) -> p f t", f=4)
            cbg = ar(7944, 1024).rearrange("p (f t) -> p f t", f=4)
            chh = ar(8968, 1024).rearrange("p (f t) -> p f t", f=4)
            dts = ar(9992, 512)
            B0 = 10504
            xb = ar(B0, 3120).rearrange("p (f t) -> p f t", f=12)
            xbc = ar(B0 + 3120, 3072).rearrange("p (f t) -> p f t", f=12)
            xd = [ar(o, 2048).rearrange("p (c n) -> p c n", c=2) for o in (B0 + 6192, 6912)]
            cb = ar(B0 + 8240, 1024).rearrange("p (g s t) -> p g s t", g=2, s=2)
            seg = ar(B0 + 9264, 1536).rearrange("p (b t) -> p b t", b=4)
            Md = ar(B0 + 10800, 1536).rearrange("p (b t) -> p b t", b=4)
            dtr = dts[:, 0:192].rearrange("p (t n) -> p t n", t=2)
            kpe = dts[:, 192:256].rearrange("p (t n) -> p t n", t=2)
            dt = dts[:, 256:320].rearrange("p (t n) -> p t n", t=2)
            dta = dts[:, 320:384].rearrange("p (t n) -> p t n", t=2)
            ncs = dts[:, 384:448].rearrange("p (t n) -> p t n", t=2)
            Ar = dts[:, 448:480]
            tsp = dts[:, 0:64].rearrange("p (t n) -> p t n", t=2)

            pad = [V.set(xb[:, :, 0:2], 0.0, last_p[0]), V.set(xb[:, :, 258:260], 0.0), V.set(cc[:, :, 0:1], 0.0), V.set(cc[:, :, 257:258], 0.0)]
            st = {"b": 0}

            def nxt():
                st["b"] += 1
                return 4 + st["b"] % 4

            def pair():
                b = nxt()
                ld = take()
                proj_T(ld, 0, b, 0, False, *xn_t)
                p = proj_T(ld, 128, b, 1, True)
                return b, p, PS[b][:, :].rearrange("p (f t) -> p f t", f=2)

            conv_t = []

            raw = lambda ld: ld["dmas"][0][0]

            def conv(f, e):
                for ff in (f, f + 1):
                    t = V.ts(xbc[:, ff], xb[:, ff, 0:256], pr(N("conv_w"), ff), None, MUL, None, e, *pad)
                    for k in range(1, 5):
                        t = V.stt(xbc[:, ff], xb[:, ff, k:k + 256], pr(N("conv_w"), 12 * k + ff), xbc[:, ff], MUL, ADD, t)
                    conv_t.append(t)

            late = []
            for f in range(0, 12, 2):
                b, p, v = pair()
                e = A.act(xb[:, f:f + 2, 2:258], v, ACT.Copy, p)
                free[b] = [e]
                if late:
                    conv(*late.pop())
                late.append((f, e))
            b, p, v = pair()
            conv(*late.pop())
            e = A.act(qkl[:, 0:2], v, ACT.Copy, p)
            free[b] = [e]
            ql_t = [e]
            ld = take()
            b = nxt()
            p = proj_T(ld, 0, b, 0, False)
            e = A.act(qkl[:, 2], PS[b][:, 0:256], ACT.Copy, p)
            free[b] = [e]
            ql_t.append(e)
            dtp = ar(B0 + 10032, 256)
            b = nxt()
            T.need(*free[b])
            for c in range(8):
                p = mm3(PS[b][0:64, 0:256], ld["hi"][1][:, c], ld["lo"][1][:, c], xnh[:, c, :], xnl[:, c, :], c == 0, c == 7, sig=(c == 7))
            done(ld, p)
            e = A.act(dtp[0:64], PS[b][0:64, 0:256], ACT.Copy, p)
            free[b] = [e]
            dt_t, pe_t = [], []

            def dt_tok():
                b = 1
                T.need(dt_e, *free[b])
                for tt in range(2):
                    p = tr(PS[b][:, 64 * tt:64 * tt + 64], dtp[0:64, 128 * tt:128 * tt + 128], sig=True)
                r = ROW[N("dt_bias")]
                for tt in range(2):
                    dt_t.append(V.tt(dt[:, tt], PS[b][:, 64 * tt:64 * tt + 32], row[:, r:r + 32], ADD, p))
                    pe_t.append(V.cp(kpe[:, tt], PS[b][:, 64 * tt + 32:64 * tt + 64], p))
                free[b] = [pe_t[1]]

            qks = ar(B0, 3072).rearrange("p (t h n) -> p t h n", t=2, h=16)
            kv = ar(B0 + 12336, 2048).rearrange("p (t h n) -> p t h n", t=2, h=8)
            ql = ar(B0 + 9264, 768).rearrange("p (f t) -> p f t", f=3)
            tq = ar(B0 + 9264, 3072).rearrange("p (t h n) -> p t h n", t=2, h=16)
            t4 = ar(B0 + 8240, 1024)
            ms_ = small[:, 40:240]
            qk_t, rope_done = [[], []], [None, None]

            def latents():
                t = A.act(ql, qkl, ACT.Square, *ql_t)
                gq = [V.ts(qkl[:, f], qkl[:, f], pr(N("q_norm"), f) if f < 2 else pr(N("kv_norm")), None, MUL, None, t) for f in range(3)]
                T.need(t, *free[0])
                for tt in range(2):
                    s = slice(128 * tt, 128 * tt + 128)
                    mm(PS[0][:, 2 * tt:2 * tt + 1], ql[:, 0, s], C("ones", 1), tt == 0, False)
                    mm(PS[0][:, 2 * tt:2 * tt + 1], ql[:, 1, s], C("ones", 1), False, False)
                    p = mm(PS[0][:, 2 * tt + 1:2 * tt + 2], ql[:, 2, s], C("ones", 1), False, tt == 1, sig=True)
                lr = ms_[:, 0:4].rearrange("p (t n) -> p t n", t=2)
                pv = PS[0][:, 0:4].rearrange("p (t n) -> p t n", t=2)
                a = V.ts(lr[:, :, 0], pv[:, :, 0], 1.0 / 256, 1e-6, MUL, ADD, p)
                a2 = V.ts(lr[:, :, 1], pv[:, :, 1], 1.0 / 128, 1e-6, MUL, ADD)
                free[0] = [a2]
                t = A.act(ms_[:, 0:4], ms_[:, 0:4], ACT.Sqrt, a, a2)
                return lr, V.rec(ms_[:, 0:4], ms_[:, 0:4], t), gq

            def heads(lr, lr_t, gq):
                ldq, ldk = take(), take()
                wuq, wukv = raw(ldq), raw(ldk)
                T.need(ldq["tok"], ldk["tok"], *gq)
                for tt in range(2):
                    s = slice(128 * tt, 128 * tt + 128)
                    for b, (a, n, h0, nh) in enumerate(((0, 480, 0, 5), (480, 288, 5, 3))):
                        T.need(*free[b])
                        mm(PS[b][:, 0:n], qkl[:, 0, s], wuq[:, 0, a:a + n], True, False)
                        p = mm(PS[b][:, 0:n], qkl[:, 1, s], wuq[:, 1, a:a + n], False, True, sig=True)
                        e = A.act(qks[:, tt, h0:h0 + nh], PS[b][:, 0:n].rearrange("p (h n) -> p h n", n=96), ACT.Copy, p, lr_t, *conv_t,
                                  scale=lr[:, tt, 0:1])
                        free[b] = [e]
                        qk_t[tt].append(e)
                    for part in range(2):
                        b = 2 + part
                        T.need(*free[b])
                        p = mm(PS[b][:, :], qkl[:, 2, s], wukv[:, 0, part * 512:part * 512 + 512], True, True, sig=True)
                        v = PS[b][:, :].rearrange("p (h n) -> p h n", h=4)
                        A.act(qks[:, tt, 8 + 4 * part:12 + 4 * part, 0:64], v[:, :, 0:64], ACT.Copy, p, lr_t, scale=lr[:, tt, 1:2])
                        e = A.act(kv[:, tt, 4 * part:4 * part + 4, 64:128], v[:, :, 64:128], ACT.Copy, scale=lr[:, tt, 1:2])
                        free[b] = [e]
                        qk_t[tt].append(e)
                done(ldq, p)
                done(ldk, p)

            hn = [None, None]

            def head_squares(tt):
                t = G.cp(qks[:, tt, 8:16, 64:96], kpe[:, tt, None, :].to_broadcast([128, 8, 32]), pe_t[tt], *conv_t)
                hn[tt] = A.act(tq[:, tt], qks[:, tt], ACT.Square, *qk_t[tt], t)

            def head_sums(tt):
                nr = ms_[:, 8 + 16 * tt:24 + 16 * tt]
                t = V.red(nr, tq[:, tt], ADD, hn[tt])
                t = V.ts(nr, nr, 1.0 / 96, 1e-6, MUL, ADD, t)
                hn[tt] = A.act(nr, nr, ACT.Sqrt, t)

            def head_rope(tt):
                nr = ms_[:, 8 + 16 * tt:24 + 16 * tt]
                t = V.rec(nr, nr, hn[tt])
                t = V.tt(qks[:, tt], qks[:, tt], nr[:, :, None].to_broadcast([128, 16, 96]), MUL, t)
                r = ROW[N("qk_g")]
                gb = row[:, r:r + 192].rearrange("p (g n) -> p g n", g=2)[:, :, None, :].to_broadcast([128, 2, 8, 96])
                qv = qks[:, tt].rearrange("p (g h) n -> p g h n", g=2)
                t = V.tt(qv, qv, gb, MUL, t)
                x1, x2 = qks[:, tt, :, 64:80], qks[:, tt, :, 80:96]
                cB = cosT[:, tt, None, :].to_broadcast([128, 16, 16])
                sB = sinT[:, tt, None, :].to_broadcast([128, 16, 16])
                m = [t4[:, 256 * i:256 * i + 256].rearrange("p (h n) -> p h n", h=16) for i in range(4)]
                V.tt(m[0], x1, cB, MUL, t, rope_t)
                V.tt(m[1], x2, sB, MUL)
                V.tt(m[2], x1, sB, MUL)
                t = V.tt(m[3], x2, cB, MUL)
                V.tt(x1, m[0], m[1], SUB, t)
                rope_done[tt] = V.tt(x2, m[2], m[3], ADD)

            dt_e = e
            lat = latents()
            ch_t, cb_t, cc_t, zs_t = [], [], [], []
            for i in range(2):
                b, p, v = pair()
                ch_t.append(A.act(chh[:, 2 * i:2 * i + 2], v, ACT.Copy, p))
                free[b] = [ch_t[i]]
            dt_tok()
            heads(*lat)
            for i in range(2):
                b, p, v = pair()
                cb_t.append(A.act(cbg[:, 2 * i:2 * i + 2], v, ACT.Copy, p))
                free[b] = [cb_t[i]]
                head_squares(i)
                if i:
                    head_sums(0)
            for i in range(2):
                b, p, v = pair()
                cc_t.append(V.tt(cc[:, 2 * i:2 * i + 2, 1:257], v, chh[:, 2 * i:2 * i + 2], MUL, p, ch_t[i]))
                free[b] = [cc_t[i]]
                if i == 0:
                    head_sums(1)
                head_rope(i)
            mla_pre = rope_done[1]

            def z_pair(i):
                b, p, v = pair()
                zs_t.append(A.act(zs[:, 2 * i:2 * i + 2], v, ACT.Silu, p))
                free[b] = [zs_t[i]]

            z_pair(0)
            xb_t = {}
            for f in [8, 10, 9, 11] + list(range(8)):
                xb_t[f] = A.act(xbc[:, f], xbc[:, f], ACT.Silu, conv_t[f], bias=pr(N("conv_b"), f))
            cv = []
            for f in range(4):
                t = V.ts(chh[:, f], cc[:, f, 0:256], pr(N("cw"), f), None, MUL, None, cc_t, pad)
                for k in (1, 2):
                    t = V.stt(chh[:, f], cc[:, f, k:k + 256], pr(N("cw"), 4 * k + f), chh[:, f], MUL, ADD, t)
                cv.append(t)
            gc = V.tt(chh, chh, cbg, MUL, *cv, *cb_t)
            z_pair(1)
            r = ROW[N("a_log")]
            t = A.act(Ar, row[:, r:r + 32], ACT.Exp)
            ta = V.ts(Ar, Ar, -1.0, None, MUL, None, t)
            t = A.act(tsp, dt, ACT.Abs, *dt_t)
            t = A.act(tsp, tsp, ACT.Exp, t, scale=-1.0)
            t = A.act(tsp, tsp, ACT.Ln, t, bias=1.0)
            td = V.stt(dt, dt, 0.0, tsp, MAX, ADD, t)
            dta_t = V.tt(dta, dt, Ar[:, None, :].to_broadcast([128, 2, 32]), MUL, td, ta)
            gc = A.act(cbg, chh, ACT.Square, gc)
            cbt = []
            for g in range(2):
                b = g
                T.need(xb_t[8 + g], xb_t[10 + g], *free[b])
                mm(PS[b][:, 0:256], xbc[:, 8 + g, 0:128], xbc[:, 10 + g], True, False)
                p = mm(PS[b][:, 256:512], xbc[:, 8 + g, 128:256], xbc[:, 10 + g], False, True, sig=True)
                e = A.act(cb[:, g], PS[b][:, :].rearrange("p (s t) -> p s t", s=2), ACT.Copy, p, mla_pre)
                free[b] = [e]
                cbt.append(e)
            z_pair(2)
            rc = yT[:, 12:16]
            gn = head_rstd(cbg, 2, (3, 1), 1.0 / 64, 1e-6, MUL, ADD, gc)
            b = 0
            T.need(dta_t, *free[b])
            o = lambda tt, d: PS[b][:, 32 * tt + 16 * d:32 * tt + 16 * d + 16]
            f_, k_ = slice(0, 16), slice(16, 32)
            mm(o(0, 0), C("triu"), dta[:, 0, f_], True, False)
            mm(o(1, 0), C("triu"), dta[:, 1, f_], False, False)
            mm(o(1, 0), C("ones"), dta[:, 0, f_], False, False)
            mm(o(0, 1), C("tril"), dta[:, 0, k_], False, False)
            mm(o(0, 1), C("ones"), dta[:, 1, k_], False, False)
            p = mm(o(1, 1), C("tril"), dta[:, 1, k_], False, True, sig=True)
            cs_t = V.ts(ncs, PS[b][:, 0:64].rearrange("p (t n) -> p t n", t=2), -1.0, None, MUL, None, p)
            free[b] = [cs_t]
            t = gn()
            yc = [V.stt(rc[:, f], chh[:, f], pr(N("conv_out"), f), PS[(3, 1)[f // 2]][:, 256 * (f % 2):256 * (f % 2) + 256], MUL, MUL, t[f // 2])
                  for f in range(4)]
            free[3], free[1] = [yc[1]], [yc[3]]
            xs_t = []

            def x_tok(tt):
                for hb in range(2):
                    b = 2 * tt + hb
                    T.need(*(xb_t[f] for f in range(8)), *free[b])
                    for k in range(4):
                        p = tr(PS[b][:, k * 128:k * 128 + 128], xbc[:, hb * 4 + k, tt * 128:tt * 128 + 128], sig=(k == 3))
                    for d in range(2):
                        dtb = dt[:, tt, 16 * d + 8 * hb:16 * d + 8 * hb + 8][:, :, None].to_broadcast([128, 8, 64])
                        e = V.tt(xd[d][:, tt, hb * 512:hb * 512 + 512].rearrange("p (h n) -> p h n", h=8),
                                 PS[b][:, :].rearrange("p (h n) -> p h n", h=8), dtb, MUL, p, td, *yc)
                    free[b] = [e]
                    xs_t.append(e)

            x_tok(0)
            z_pair(3)
            x_tok(1)
            seg_r, Md_r = {}, {}
            exp_t, m_t, y_t, ys = {}, {}, {}, []
            ends = lambda d: (0, 1) if d == 0 else (1, 0)
            near = lambda d: slice(128 * d, 128 * d + 128)
            far = lambda d: slice(128 - 128 * d, 256 - 128 * d)

            def ssd_decay(k):
                h, d, b, i = k // 2, k % 2, k % 4, k % 4
                hd = 16 * d + h
                T.need(*free[b])
                bc = lambda tt: dta[:, tt, hd:hd + 1].to_broadcast([128, 128])
                wide, tri = ("triu", "triu") if d == 0 else ("ones2", "tril")
                mm(PS[b][:, 0:256], bc(d), C(wide, 256), True, False)
                p = mm(PS[b][:, far(d)], bc(1 - d), C(tri), False, True, sig=True)
                (sfull, shalf), mk = ends(d), C("mnegf") if d == 0 else C("mnegb")
                V.stt(seg[:, i, near(d)], PS[b][:, near(d)], ncs[:, sfull, hd:hd + 1], mk, ADD, ADD, p, cs_t, seg_r.get(k - 4), mla_pre)
                e = V.stt(seg[:, i, 256:384], PS[b][:, far(d)], ncs[:, shalf, hd:hd + 1], mk, ADD, ADD)
                a = A.act(seg[:, i, far(d)], PS[b][:, far(d)], ACT.Exp, e, bias=ncs[:, sfull, hd:hd + 1])
                free[b] = [a]
                sv = seg[:, i].rearrange("p (x t) -> p x t", x=3)[:, d::2 - d]
                exp_t[k] = A.act(sv, sv, ACT.Exp, e)

            def ssd_weights(k):
                h, d, i = k // 2, k % 2, k % 4
                g, (sfull, shalf) = h // 8, ends(d)
                q = G if k % 2 else V
                q.tt(Md[:, i, 0:256], seg[:, i, 0:256], cb[:, g, sfull], MUL, exp_t[k], cbt[g], Md_r.get(k - 4), mla_pre)
                e = q.tt(Md[:, i, 256:384], seg[:, i, 256:384], cb[:, g, shalf, far(d)], MUL)
                seg_r[k] = m_t[k] = e

            def ssd_values(h):
                po, ob = 64 * (h % 2), 4 + (h // 2) % 4
                T.need(m_t[2 * h], m_t[2 * h + 1], *xs_t)
                if po == 0:
                    T.need(*free[ob])
                O = lambda a, n: PS[ob][po:po + 64, a:a + n]
                hx = slice(h * 64, h * 64 + 64)
                i0, i1 = 2 * h % 4, (2 * h + 1) % 4
                mm(O(0, 256), xd[0][:, 0, hx], Md[:, i0, 0:256], True, False)
                mm(O(128, 128), xd[0][:, 1, hx], Md[:, i0, 256:384], False, False)
                mm(O(0, 256), xd[1][:, 1, hx], Md[:, i1, 0:256], False, False)
                y_t[h] = mm(O(0, 128), xd[1][:, 0, hx], Md[:, i1, 256:384], False, True, sig=True)
                Md_r[2 * h] = Md_r[2 * h + 1] = y_t[h]

            def ssd_out(f):
                ob = 4 + f % 4
                t = V.stt(yT[:, f], xbc[:, f], pr(N("ssd_d"), f), PS[ob][:, 0:256], MUL, ADD, y_t[2 * f + 1])
                free[ob] = [t]
                ys.append(G.tt(yT[:, f], yT[:, f], zs[:, f], MUL, t, *zs_t))

            for k in range(40):
                if k < 32:
                    ssd_decay(k)
                if 2 <= k < 34:
                    ssd_weights(k - 2)
                if k >= 4 and k % 2 == 0 and k < 36:
                    ssd_values((k - 4) // 2)
                if k >= 8 and k % 4 == 0:
                    ssd_out((k - 8) // 4)
            yl = lambda k: hhi_[:, 2048 + 256 * k:2304 + 256 * k] if k < 14 else hlo_[:, 256 * (k - 14):256 * (k - 13)]
            yh0 = hhi_[:, 0:2048].rearrange("p (f t) -> p f t", f=8)
            yh1 = hlo_[:, 1280:3328].rearrange("p (f t) -> p f t", f=8)
            yh = lambda k: (yh0 if k < 8 else yh1)[:, k % 8]
            sqs = ar(B0 + 9264, 2048).rearrange("p (f t) -> p f t", f=8)
            rs = ar(B0 + 11312, 512).rearrange("p (g t) -> p g t", g=2)
            sq_t = A.act(sqs, yT[:, 0:8], ACT.Square, *ys)
            conv_y = [A.act(yh1[:, 4:8], yT[:, 12:16], ACT.Copy, *yc, y_t[15])]
            conv_y += [V.tt(yl(k), yT[:, k], f32(yh(k)), SUB, *conv_y) for k in range(12, 16)]
            y_of = dict.fromkeys(range(12, 16), conv_y)

            def ssd_norm():
                T.need(sq_t, *free[3])
                for g in range(2):
                    for k in range(4):
                        p = mm(PS[3][:, 256 * g:256 * g + 256], C("ones"), sqs[:, 4 * g + k], k == 0 and g == 0, k == 3 and g == 1, sig=(k == 3))
                e = V.ts(rs, PS[3][:, :].rearrange("p (g t) -> p g t", g=2), 1.0 / 512, 1e-6, MUL, ADD, p)
                free[3] = [e]
                return A.act(rs, rs, ACT.Sqrt, e)

            yl0 = hhi_[:, 2048:4096].rearrange("p (f t) -> p f t", f=8)

            def ssd_parts(i, t):
                fs = slice(2 * i, 2 * i + 2)
                yn = [V.stt(yT[:, f], yT[:, f], pr(N("ssd_norm"), f), rs[:, f // 4], MUL, MUL, t) for f in (2 * i, 2 * i + 1)]
                y_of.update(dict.fromkeys((2 * i, 2 * i + 1), parts_of(yh0[:, fs], yl0[:, fs], yT[:, fs], *yn, *ys)))

            wst = {"i": 0}

            def w_out_step():
                i = wst["i"]
                wst["i"] += 1
                k = W_OUT_ORDER[i]
                if i == 0:
                    T.need(*free[4], *free[5], *free[6], *free[7])
                if i % 2 == 0:
                    wst["ld"] = take()
                ld = wst["ld"]
                T.need(*y_of[k])
                for tt in range(2):
                    s = slice(128 * tt, 128 * tt + 128)
                    for dh in range(2):
                        d = slice(512 * dh, 512 * dh + 512)
                        p = mm3(PS[4 + 2 * tt + dh][:, :], yh(k)[:, s], yl(k)[:, s], ld["hi"][0][:, i % 2, d], ld["lo"][0][:, i % 2, d],
                                i == 0, i == 15, sig=True)
                if i % 2:
                    done(ld, p)
                return p


            qkT = ar(B0 + 3120, 4096).rearrange("p (h t) -> p h t", h=16)
            Pm = ar(B0 + 7216, 1024).rearrange("p (b k) -> p b k", b=4)
            PT = ar(B0 + 8240, 1024).rearrange("p (b k t) -> p b k t", b=2, k=4)
            om = ar(24888, 1024).rearrange("p (t h n) -> p t h n", t=2, h=8)
            kt_ = []
            for tt in range(2):
                for q4 in range(4):
                    b = 4 + q4
                    T.need(rope_done[tt], *free[b])
                    for k in range(4):
                        p = tr(PS[b][0:96, k * 128:k * 128 + 128], qks[:, tt, 4 * q4 + k], sig=(k == 3))
                    e = A.act(qkT[0:96, 4 * q4:4 * q4 + 4, 128 * tt:128 * tt + 128], PS[b][0:96, :].rearrange("p (h t) -> p h t", h=4),
                              ACT.Copy, p, y_t[15], *ys)
                    free[b] = [e]
                    kt_.append(e)
            mx, sm = ms_[:, 40:56], ms_[:, 56:72]
            scl = 96.0 ** -0.5
            mx_t, pt_t, pv_t = {}, {}, {}

            def scores(h):
                b = 0
                T.need(*kt_, *free[b])
                for tt in range(2):
                    p = mm(PS[b][:, 256 * tt:256 * tt + 256], qkT[0:96, h, 128 * tt:128 * tt + 128], qkT[0:96, 8 + h], tt == 0, tt == 1, sig=(tt == 1))
                t = V.red(mx[:, 2 * h:2 * h + 2], PS[b][:, :].rearrange("p (t k) -> p t k", t=2), MAX, p)
                t = V.ts(mx[:, 2 * h:2 * h + 2], mx[:, 2 * h:2 * h + 2], -scl, None, MUL, None, t)
                for tt in range(2):
                    i = (2 * h + tt) % 4
                    a = A.act(Pm[:, i], PS[b][:, 256 * tt:256 * tt + 256], ACT.Exp, t, P_r[i],
                              bias=mx[:, 2 * h + tt:2 * h + tt + 1], scale=scl, accum=sm[:, 2 * h + tt:2 * h + tt + 1])
                free[b] = [a]
                mx_t[h] = a

            def turned(h):
                b = 1
                T.need(mx_t[h], *free[b])
                for tt in range(2):
                    for ks in range(2):
                        p = tr(PS[b][:, (2 * tt + ks) * 128:(2 * tt + ks) * 128 + 128], Pm[:, (2 * h + tt) % 4, ks * 128:ks * 128 + 128], sig=True)
                P_r[(2 * h) % 4] = P_r[(2 * h + 1) % 4] = p
                pt_t[h] = V.cp(PT[:, h % 2], PS[b][:, :].rearrange("p (k t) -> p k t", k=4), p, PT_r[h % 2])
                free[b] = [pt_t[h]]

            def values(h):
                T.need(pt_t[h])
                for tt in range(2):
                    if h == 0:
                        T.need(*free[2 + tt])
                    for ks in range(2):
                        p = mm(PS[2 + tt][:, h * 64:h * 64 + 64], PT[:, h % 2, 2 * tt + ks], kv[:, ks, h, 64:128], h == 0 and ks == 0, h == 7 and ks == 1, sig=True)
                PT_r[h % 2] = p
                return p

            P_r, PT_r = [None] * 4, [None] * 2
            w_out_step()
            w_out_step()
            for h in range(10):
                if h < 8:
                    scores(h)
                if 1 <= h < 9:
                    turned(h - 1)
                if h == 0:
                    nrm = ssd_norm()
                if h == 1:
                    nrm = V.rec(rs, rs, nrm)
                if 1 <= h < 5:
                    ssd_parts(h - 1, nrm)
                if 2 <= h < 8:
                    w_out_step()
                if h >= 2:
                    p = values(h - 2)
            a = mx_t[7]
            t = V.rec(sm, sm, a)
            smv = sm.rearrange("p (h t) -> p h t", t=2)
            mla_t = []
            for tt in range(2):
                o = V.tt(om[:, tt], PS[2 + tt][:, :].rearrange("p (h n) -> p h n", h=8), smv[:, :, tt:tt + 1].to_broadcast([128, 8, 64]), MUL, p, t)
                free[2 + tt] = [o]
            q8 = ar(B0 + 9264, 1024).rearrange("p (t h n) -> p t h n", t=2, h=8)
            a = A.act(q8, om, ACT.Square, o)
            w_out_step()
            nr = ms_[:, 80:96]
            nrv = nr.rearrange("p (t h) -> p t h", t=2)
            a = V.red(nrv, q8, ADD, a)
            w_out_step()
            a = rstd(nr, nr, 64, 1e-6, a)
            w_out_step()
            for tt in range(2):
                o = V.tt(om[:, tt], om[:, tt], nrv[:, tt, :, None].to_broadcast([128, 8, 64]), MUL, a)
                if tt == 0:
                    w_out_step()
                a = o
                b = tt
                T.need(a, *free[b])
                fo = om[:, tt].rearrange("p h n -> p (h n)")
                for k in range(4):
                    p2 = tr(PS[b][:, k * 128:k * 128 + 128], fo[:, k * 128:k * 128 + 128], sig=(k == 3))
                for k in range(4):
                    s = slice(128 * tt, 128 * tt + 128)
                    e = A.act(yh1[:, k, s], PS[b][:, k * 128:k * 128 + 128], ACT.Copy, p2, conv_y, scale=pr(N("out_norm"), k))
                mla_t.append(e)
                for k in range(4):
                    e = V.stt(yl(8 + k)[:, s], PS[b][:, k * 128:k * 128 + 128], pr(N("out_norm"), k), f32(yh1[:, k, s]), MUL, SUB, e)
                free[b] = [e]
                mla_t.append(e)
            y_of.update({k: mla_t for k in range(8, 12)})
            for k in range(4):
                p = w_out_step()
            x_now = add_x(p)

        for l in range(2):
            ffn(f"ffn1_norm{l}")
            mixer(l)
            ffn(f"ffn2_norm{l}")
        assert turn["n"] == len(loads)

        for n, ld in enumerate(loads):
            if n == 3:
                for dst, src in later:
                    L.items.append((lambda e, dst=dst, src=src: e.dma_start(dst, src), d_later.sem, 16))
            if n >= NR:
                L.need(loads[n - NR]["done"])
            for dst, src in ld["dmas"]:
                L.items.append((lambda e, dst=dst, src=src: e.dma_start(dst, src), ld["sem"].sem, 16))
        for tt in range(2):
            done = L.dma(out[128 * tt:128 * tt + 128, :], xtok[:, tt], dout, *x_now[tt])
        L.need(done)

        block = ctx.enter_context(nc.Block())

        @block.sync
        def _(e):
            L.emit(e)

        @block.tensor
        def _(e):
            T.emit(e)

        @block.vector
        def _(e):
            V.emit(e)

        @block.scalar
        def _(e):
            A.emit(e)

        @block.gpsimd
        def _(e):
            G.emit(e)


_BIG = ["w_in", "rw_g2", "w_out", "exp_w_gate", "exp_w_up", "exp_w_down", "final_norm_g"]
_BIG2 = ["ffn1_w_gate_2", "ffn1_w_up_2", "ffn1_w_down_2", "w_in_2", "mla_w_uq_2", "mla_w_ukv_2", "w_out_2",
         "ffn2_w_gate_2", "ffn2_w_up_2", "ffn2_w_down_2"]


def layout(inputs):
    a = {n: np.ascontiguousarray(inputs[n]) for n in _BIG + _BIG2}
    f = {n: np.asarray(v) for n, v in inputs.items()}
    a["x"] = np.ascontiguousarray(f["x"][0])
    a["positions"] = np.ascontiguousarray(f["positions_2"].reshape(2, 128).T)
    a["w2a2"] = np.concatenate([f["rw_w2"][0], f["rw_a2"][0]], axis=0)
    a["router"] = np.ascontiguousarray(
        np.concatenate([f["router_grp_w"][0], f["router_exp_w"][0]], axis=1).reshape(8, 128, 36).transpose(1, 0, 2).reshape(128, 288))
    for l in range(2):
        w = f["w_in_2"][l]
        a[f"wkv{l}"] = np.concatenate([w[:, i:j].reshape(8, 128, j - i).transpose(1, 0, 2).reshape(128, 8 * (j - i))
                                       for w, i, j in ((w, 2848, 2976), (np.concatenate([w[:, 2560:2592], w[:, 2976:3008]], axis=1), 0, 64))], axis=1)
    c = lambda v: np.asarray(v).reshape(-1, 128).T
    parts = [c(f[n][0]) for n in ("norm_mix_g", "shift_mu", "sb_out_g", "rw_w0", "rw_a0", "rw_k_k", "rw_k_a", "rw_r_k",
                                  "rw_ln_w", "rw_ln_b", "norm_ffn_g")]
    for l in range(2):
        parts += [c(f["ffn1_norm_2"][l]), c(f["mix_norm_2"][l]), c(f["ssd_conv_w_2"][l]), c(f["ssd_conv_b_2"][l]),
                  c(f["ssd_norm_2"][l]), c(np.repeat(f["ssd_d_2"][l], 64)), c(f["mla_q_norm_2"][l]), c(f["mla_kv_norm_2"][l]),
                  c(f["mla_out_norm_2"][l]), c(f["conv_w_2"][l]), c(f["conv_out_norm_2"][l]), c(f["ffn2_norm_2"][l])]
    a["prm"] = np.ascontiguousarray(np.concatenate(parts, axis=1))
    rows_ = [f["router_grp_b"][0], f["router_exp_b"][0]]
    for l in range(2):
        rows_ += [f["ssd_dt_bias_2"][l].reshape(-1), f["ssd_a_log_2"][l].reshape(-1), f["mla_q_head_norm_2"][l], f["mla_k_head_norm_2"][l]]
    a["rowp"] = np.ascontiguousarray(np.broadcast_to(np.concatenate(rows_)[None], (128, NROW)))
    a["cst"] = constants()
    return a


def kernel(**inputs):
    import concourse.bacc as bacc
    from concourse.bass_utils import run_bass_kernel_spmd

    nc = bacc.Bacc("TRN2", target_bir_lowering=False, num_devices=1)
    arrays = {f"in_{n}": v for n, v in layout(inputs).items()}
    aps = {n[3:]: nc.dram_tensor(n, v.shape, mybir.dt.from_np(v.dtype), kind="ExternalInput").ap() for n, v in arrays.items()}
    out = nc.dram_tensor("out_0", (256, 1024), F32, kind="ExternalOutput").ap()
    program(nc, aps, out)
    r = run_bass_kernel_spmd(nc, [arrays], core_ids=[0])
    return r.results[0]["out_0"].reshape(1, 256, 1024)
```
